# Optimizing a Trainium2 kernel written in Bass

```python
import jax, jax.numpy as jnp
from jax import lax
import numpy as np
import math

D_MODEL = 1024
BATCH = 1
SEQ = 512
DEPTH = 2

DEEPNORM_ALPHA = (2 * DEPTH) ** 0.25
DEEPNORM_BETA = (8 * DEPTH) ** -0.25
LN_EPS = 1e-5

CONV_CH = D_MODEL
CONV_WIDTH = 31
SSM_INNER = D_MODEL
SSM_HEAD_DIM = 64
SSM_HEADS = SSM_INNER // SSM_HEAD_DIM
SSM_GROUPS = 2
SSM_HPG = SSM_HEADS // SSM_GROUPS
SSM_STATE = 128
SSM_CONV = 4
SSM_CHUNK = 128
SSM_XBC = SSM_INNER + 2 * SSM_GROUPS * SSM_STATE
EVEN_IN = 2 * CONV_CH + SSM_INNER + SSM_XBC + SSM_HEADS
EVEN_MIX = CONV_CH + SSM_INNER

GLA_HEADS = 4
GLA_DK_TOTAL = D_MODEL // 2
GLA_DV_TOTAL = D_MODEL
GLA_DK = GLA_DK_TOTAL // GLA_HEADS
GLA_DV = GLA_DV_TOTAL // GLA_HEADS
GLA_RANK = 16
GLA_TAU = 16.0
GLA_CHUNK = 64
ODD_IN = 2 * GLA_DK_TOTAL + 2 * GLA_DV_TOTAL + GLA_RANK

MEM_LEN = 256
XA_HEADS = 4
XA_HEAD_DIM = D_MODEL // XA_HEADS
D_FF = 4 * D_MODEL

N_EVEN = (DEPTH + 1) // 2
N_ODD = DEPTH // 2


def layer_norm(x, g, b):
    xf = x.astype(jnp.float32)
    mu = jnp.mean(xf, -1, keepdims=True)
    var = jnp.mean(jnp.square(xf - mu), -1, keepdims=True)
    return ((xf - mu) * lax.rsqrt(var + LN_EPS) * g + b).astype(x.dtype)

def rms_norm(x, g):
    xf = x.astype(jnp.float32)
    return (xf * lax.rsqrt(jnp.mean(xf * xf, -1, keepdims=True) + LN_EPS) * g).astype(x.dtype)

def causal_depthwise_conv(x, w, b):
    width = w.shape[0]
    y = lax.conv_general_dilated(x, w[:, None, :].astype(x.dtype), window_strides=(1,),
                                 padding=[(width - 1, 0)],
                                 dimension_numbers=('NWC', 'WIO', 'NWC'),
                                 feature_group_count=x.shape[-1])
    return y + b

def ssd_chunked(x, a, b_mat, c_mat):
    bsz, seqlen = x.shape[:2]
    nc, q = seqlen // SSM_CHUNK, SSM_CHUNK
    xc = x.reshape(bsz, nc, q, SSM_GROUPS, SSM_HPG, SSM_HEAD_DIM)
    ac = jnp.moveaxis(a.astype(jnp.float32).reshape(bsz, nc, q, SSM_GROUPS, SSM_HPG), 2, -1)
    bm = b_mat.reshape(bsz, nc, q, SSM_GROUPS, SSM_STATE)
    cm = c_mat.reshape(bsz, nc, q, SSM_GROUPS, SSM_STATE)
    a_cs = jnp.cumsum(ac, axis=-1)
    causal = jnp.tril(jnp.ones((q, q), dtype=bool))
    seg = a_cs[..., :, None] - a_cs[..., None, :]
    decay = jnp.exp(jnp.where(causal, seg, -jnp.inf)).astype(x.dtype)
    cb = jnp.einsum('bclgn,bcsgn->bcgls', cm, bm)
    y_diag = jnp.einsum('bcgkls,bcsgkp->bclgkp', cb[:, :, :, None] * decay, xc)
    decay_to_end = jnp.exp(a_cs[..., -1:] - a_cs).astype(x.dtype)
    states = jnp.einsum('bcsgn,bcgks,bcsgkp->bcgkpn', bm, decay_to_end, xc)
    chunk_decay = jnp.exp(a_cs[..., -1])

    def step(h, inp):
        st, dec = inp
        return h * dec[..., None, None] + st, h

    h0 = jnp.zeros((bsz, SSM_GROUPS, SSM_HPG, SSM_HEAD_DIM, SSM_STATE), jnp.float32)
    _, prev = lax.scan(step, h0, (jnp.moveaxis(states, 1, 0), jnp.moveaxis(chunk_decay, 1, 0)))
    prev = jnp.moveaxis(prev, 0, 1)
    y_off = jnp.einsum('bclgn,bcgkpn,bcgkl->bclgkp', cm, prev, jnp.exp(a_cs))
    return (y_diag + y_off).astype(x.dtype).reshape(bsz, seqlen, SSM_HEADS, SSM_HEAD_DIM)

def even_mixer(x, w_in, conv_w, conv_b, conv_ln_g, conv_ln_b, ssm_conv_w, ssm_conv_b,
               dt_bias, a_log, d_skip, ssm_norm_g, w_out):
    bsz, seqlen, _ = x.shape
    proj = x @ w_in
    c0 = CONV_CH
    c1 = 2 * CONV_CH
    c2 = c1 + SSM_INNER
    c3 = c2 + SSM_XBC
    conv_val, conv_gate, z, xbc, dt = jnp.split(proj, [c0, c1, c2, c3], axis=-1)
    u = conv_val * jax.nn.sigmoid(conv_gate)
    u = causal_depthwise_conv(u, conv_w, conv_b)
    u = jax.nn.silu(layer_norm(u, conv_ln_g, conv_ln_b))
    xbc = jax.nn.silu(causal_depthwise_conv(xbc, ssm_conv_w, ssm_conv_b))
    xs, bm, cm = jnp.split(xbc, [SSM_INNER, SSM_INNER + SSM_GROUPS * SSM_STATE], axis=-1)
    dt = jax.nn.softplus((dt + dt_bias).astype(jnp.float32))
    a = -jnp.exp(a_log.astype(jnp.float32))
    xs_h = xs.reshape(bsz, seqlen, SSM_HEADS, SSM_HEAD_DIM)
    y = ssd_chunked((xs_h * dt[..., None]).astype(x.dtype), dt * a,
                    bm.reshape(bsz, seqlen, SSM_GROUPS, SSM_STATE),
                    cm.reshape(bsz, seqlen, SSM_GROUPS, SSM_STATE))
    y = (y + xs_h * d_skip[:, None]).reshape(bsz, seqlen, SSM_INNER) * jax.nn.silu(z)
    y = rms_norm(y.reshape(bsz, seqlen, SSM_GROUPS, SSM_INNER // SSM_GROUPS),
                 ssm_norm_g.reshape(SSM_GROUPS, SSM_INNER // SSM_GROUPS)).reshape(bsz, seqlen, SSM_INNER)
    return jnp.concatenate([u, y.astype(u.dtype)], axis=-1) @ w_out

def gla_chunked(q, k, v, log_g):
    bsz, seqlen = q.shape[:2]
    n, c = seqlen // GLA_CHUNK, GLA_CHUNK
    q = q.reshape(bsz, n, c, GLA_HEADS, GLA_DK)
    k = k.reshape(bsz, n, c, GLA_HEADS, GLA_DK)
    v = v.reshape(bsz, n, c, GLA_HEADS, GLA_DV)
    b_cs = jnp.cumsum(log_g.astype(jnp.float32).reshape(bsz, n, c, GLA_HEADS, GLA_DK), axis=2)
    q_t = q * jnp.exp(b_cs) * (GLA_DK ** -0.5)
    k_t = k * jnp.exp(-b_cs)
    k_end = k * jnp.exp(b_cs[:, :, -1:] - b_cs)
    causal = jnp.tril(jnp.ones((c, c), dtype=bool))
    att = jnp.where(causal, jnp.einsum('bnlhd,bnshd->bnhls', q_t, k_t), 0.0)
    o = jnp.einsum('bnhls,bnshv->bnlhv', att, v)
    kv = jnp.einsum('bnshd,bnshv->bnhdv', k_end, v)
    chunk_decay = jnp.exp(b_cs[:, :, -1])

    def step(s, inp):
        kv_c, dec = inp
        return s * dec[..., None] + kv_c, s

    s0 = jnp.zeros((bsz, GLA_HEADS, GLA_DK, GLA_DV), jnp.float32)
    _, prev = lax.scan(step, s0, (jnp.moveaxis(kv, 1, 0), jnp.moveaxis(chunk_decay, 1, 0)))
    prev = jnp.moveaxis(prev, 0, 1)
    o = o + jnp.einsum('bnlhd,bnhdv->bnlhv', q_t, prev)
    return o.astype(v.dtype).reshape(bsz, seqlen, GLA_HEADS, GLA_DV)

def odd_mixer(x, w_in, w_gate2, b_gate, head_norm_g, w_out):
    bsz, seqlen, _ = x.shape
    proj = x @ w_in
    s0 = GLA_DK_TOTAL
    s1 = 2 * GLA_DK_TOTAL
    s2 = s1 + GLA_DV_TOTAL
    s3 = s2 + GLA_DV_TOTAL
    q, k, v, g_out, g_low = jnp.split(proj, [s0, s1, s2, s3], axis=-1)
    log_g = jax.nn.log_sigmoid((g_low @ w_gate2 + b_gate).astype(jnp.float32)) / GLA_TAU
    o = gla_chunked(q.reshape(bsz, seqlen, GLA_HEADS, GLA_DK),
                    k.reshape(bsz, seqlen, GLA_HEADS, GLA_DK),
                    v.reshape(bsz, seqlen, GLA_HEADS, GLA_DV),
                    log_g.reshape(bsz, seqlen, GLA_HEADS, GLA_DK))
    o = rms_norm(o, head_norm_g).reshape(bsz, seqlen, GLA_DV_TOTAL) * jax.nn.silu(g_out)
    return o @ w_out

def memory_cross_attention(x, mem, w_q, w_k, w_v, w_o):
    bsz, seqlen, _ = x.shape
    q = (x @ w_q).reshape(bsz, seqlen, XA_HEADS, XA_HEAD_DIM)
    k = (mem @ w_k).reshape(bsz, mem.shape[1], XA_HEADS, XA_HEAD_DIM)
    v = (mem @ w_v).reshape(bsz, mem.shape[1], XA_HEADS, XA_HEAD_DIM)
    s = jnp.einsum('blhd,bmhd->bhlm', q, k).astype(jnp.float32) * (XA_HEAD_DIM ** -0.5)
    p = jax.nn.softmax(s, axis=-1).astype(v.dtype)
    o = jnp.einsum('bhlm,bmhd->blhd', p, v).reshape(bsz, seqlen, D_MODEL)
    return o @ w_o

def sq_relu_mlp(x, w1, w2):
    return jnp.square(jax.nn.relu(x @ w1)) @ w2

def first_inputs(seed: int = 0) -> dict:
    key = jax.random.key(seed)
    ks = iter(jax.random.split(key, 40))
    f32 = jnp.float32

    def nrm(shape, scale):
        return jax.random.normal(next(ks), shape, f32) * scale

    dt0 = jnp.exp(jax.random.uniform(next(ks), (N_EVEN, SSM_HEADS), f32,
                                     np.log(1e-3).astype(np.float32), np.log(1e-1).astype(np.float32)))
    return {
        "x": nrm((BATCH, SEQ, D_MODEL), 1.0),
        "mem": nrm((BATCH, MEM_LEN, D_MODEL), 1.0),
        "even_w_in": nrm((N_EVEN, D_MODEL, EVEN_IN), D_MODEL ** -0.5),
        "even_conv_w": nrm((N_EVEN, CONV_WIDTH, CONV_CH), CONV_WIDTH ** -0.5),
        "even_conv_b": nrm((N_EVEN, CONV_CH), 0.01),
        "even_conv_ln_g": 1.0 + nrm((N_EVEN, CONV_CH), 0.02),
        "even_conv_ln_b": nrm((N_EVEN, CONV_CH), 0.02),
        "even_ssm_conv_w": nrm((N_EVEN, SSM_CONV, SSM_XBC), SSM_CONV ** -0.5),
        "even_ssm_conv_b": nrm((N_EVEN, SSM_XBC), 0.01),
        "even_dt_bias": dt0 + jnp.log(-jnp.expm1(-dt0)),
        "even_a_log": jnp.log(jax.random.uniform(next(ks), (N_EVEN, SSM_HEADS), f32, 1.0, 16.0)),
        "even_d_skip": 1.0 + nrm((N_EVEN, SSM_HEADS), 0.02),
        "even_ssm_norm_g": 1.0 + nrm((N_EVEN, SSM_INNER), 0.02),
        "even_w_out": nrm((N_EVEN, EVEN_MIX, D_MODEL), EVEN_MIX ** -0.5 * DEEPNORM_BETA),
        "odd_w_in": nrm((N_ODD, D_MODEL, ODD_IN), D_MODEL ** -0.5),
        "odd_w_gate2": nrm((N_ODD, GLA_RANK, GLA_DK_TOTAL), GLA_RANK ** -0.5),
        "odd_b_gate": nrm((N_ODD, GLA_DK_TOTAL), 0.1),
        "odd_head_norm_g": 1.0 + nrm((N_ODD, GLA_DV), 0.02),
        "odd_w_out": nrm((N_ODD, GLA_DV_TOTAL, D_MODEL), GLA_DV_TOTAL ** -0.5 * DEEPNORM_BETA),
        "xa_w_q": nrm((DEPTH, D_MODEL, D_MODEL), D_MODEL ** -0.5),
        "xa_w_k": nrm((DEPTH, D_MODEL, D_MODEL), D_MODEL ** -0.5),
        "xa_w_v": nrm((DEPTH, D_MODEL, D_MODEL), D_MODEL ** -0.5),
        "xa_w_o": nrm((DEPTH, D_MODEL, D_MODEL), D_MODEL ** -0.5 * DEEPNORM_BETA),
        "mlp_w1": nrm((DEPTH, D_MODEL, D_FF), D_MODEL ** -0.5),
        "mlp_w2": nrm((DEPTH, D_FF, D_MODEL), D_FF ** -0.5 * DEEPNORM_BETA),
        "ln_g": 1.0 + nrm((DEPTH, 3, D_MODEL), 0.02),
        "ln_b": nrm((DEPTH, 3, D_MODEL), 0.02),
    }

def first_block(x, mem, even_w_in, even_conv_w, even_conv_b, even_conv_ln_g, even_conv_ln_b,
              even_ssm_conv_w, even_ssm_conv_b, even_dt_bias, even_a_log, even_d_skip,
              even_ssm_norm_g, even_w_out, odd_w_in, odd_w_gate2, odd_b_gate, odd_head_norm_g,
              odd_w_out, xa_w_q, xa_w_k, xa_w_v, xa_w_o, mlp_w1, mlp_w2, ln_g, ln_b):
    h = x
    for i in range(DEPTH):
        j = i // 2
        if i % 2 == 0:
            m = even_mixer(h, even_w_in[j], even_conv_w[j], even_conv_b[j], even_conv_ln_g[j],
                           even_conv_ln_b[j], even_ssm_conv_w[j], even_ssm_conv_b[j],
                           even_dt_bias[j], even_a_log[j], even_d_skip[j], even_ssm_norm_g[j],
                           even_w_out[j])
        else:
            m = odd_mixer(h, odd_w_in[j], odd_w_gate2[j], odd_b_gate[j], odd_head_norm_g[j],
                          odd_w_out[j])
        h = layer_norm(DEEPNORM_ALPHA * h + m, ln_g[i, 0], ln_b[i, 0])
        h = layer_norm(DEEPNORM_ALPHA * h + memory_cross_attention(h, mem, xa_w_q[i], xa_w_k[i],
                                                                   xa_w_v[i], xa_w_o[i]),
                       ln_g[i, 1], ln_b[i, 1])
        h = layer_norm(DEEPNORM_ALPHA * h + sq_relu_mlp(h, mlp_w1[i], mlp_w2[i]),
                       ln_g[i, 2], ln_b[i, 2])
    return h


DEPTH_2 = 1

HEAD_DIM = 64
BLOCK = 128
RMS_EPS = 1e-6
SUBLN_EPS = 1e-5
A_HEADS = 4
A_QK = A_HEADS * 2 * HEAD_DIM
A_WIDTH = A_HEADS * 2 * HEAD_DIM
B_HEADS = 8
B_KV_HEADS = 2
B_GROUP = B_HEADS // B_KV_HEADS
B_WIDTH = B_HEADS * HEAD_DIM
B_KV = B_KV_HEADS * HEAD_DIM
WINDOW = 128
C_HEADS = 8
C_WIDTH = C_HEADS * HEAD_DIM
N_BRANCH = 3
SPLITS = (A_QK, A_QK, A_WIDTH, A_WIDTH,
          B_WIDTH, B_KV, B_KV, B_WIDTH,
          C_WIDTH, C_WIDTH, C_WIDTH, C_HEADS, C_WIDTH,
          N_BRANCH * D_MODEL)
D_IN = sum(SPLITS)


def rms_norm_2(x, gain, eps):
    xf = x.astype(jnp.float32)
    y = xf * lax.rsqrt(jnp.mean(xf * xf, axis=-1, keepdims=True) + eps)
    return (y * gain.astype(jnp.float32)).astype(x.dtype)

def alibi_slopes(n_heads):
    return 2.0 ** (-8.0 * jnp.arange(1, n_heads + 1, dtype=jnp.float32) / n_heads)

def diff_attention(q, k, v, lam, slopes):
    B, S, H, _, d = q.shape
    nb = S // BLOCK
    scale = d ** -0.5
    qb = jnp.moveaxis(q.reshape(B, nb, BLOCK, H, 2, d), 1, 0)
    k_pos = jnp.arange(S)

    def one_block(args):
        qblk, start = args
        s = jnp.einsum('bqhmd,bkhmd->bhmqk', qblk, k).astype(jnp.float32) * scale
        dist = (start + jnp.arange(BLOCK))[:, None] - k_pos[None, :]
        bias = jnp.where(dist >= 0, -slopes[:, None, None] * dist.astype(jnp.float32), -jnp.inf)
        p = jax.nn.softmax(s + bias[None, :, None], axis=-1)
        w = p[:, :, 0] - lam * p[:, :, 1]
        return jnp.einsum('bhqk,bkhe->bqhe', w.astype(v.dtype), v)

    out = lax.map(one_block, (qb, jnp.arange(nb) * BLOCK))
    return jnp.moveaxis(out, 0, 1).reshape(B, S, H, v.shape[-1])

def sliding_window_attention(q, k, v, sinks, slopes):
    B, S, HQ, d = q.shape
    KV = k.shape[2]
    G = HQ // KV
    nb = S // BLOCK
    scale = d ** -0.5
    qb = q.reshape(B, nb, BLOCK, KV, G, d)

    def banded(t):
        tb = t.reshape(B, nb, BLOCK, KV, d)
        prev = jnp.concatenate([jnp.zeros_like(tb[:, :1]), tb[:, :-1]], axis=1)
        return jnp.concatenate([prev, tb], axis=2)

    kb, vb = banded(k), banded(v)
    s = jnp.einsum('bnqhgd,bnkhd->bnhgqk', qb, kb).astype(jnp.float32) * scale
    i = jnp.arange(BLOCK)[:, None]
    j = jnp.arange(2 * BLOCK)[None, :]
    dist = i - j + BLOCK
    key_pos = jnp.arange(nb)[:, None, None] * BLOCK + j - BLOCK
    valid = (dist >= 0) & (dist < WINDOW) & (key_pos >= 0)
    bias = -slopes.reshape(KV, G)[:, :, None, None] * dist.astype(jnp.float32)
    s = jnp.where(valid[None, :, None, None], s + bias[None, None], -jnp.inf)
    sink = sinks.astype(jnp.float32).reshape(KV, G)[None, None, :, :, None, None]
    m = jnp.maximum(jnp.max(s, axis=-1, keepdims=True), sink)
    e = jnp.exp(s - m)
    p = e / (jnp.sum(e, axis=-1, keepdims=True) + jnp.exp(sink - m))
    out = jnp.einsum('bnhgqk,bnkhd->bnqhgd', p.astype(v.dtype), vb)
    return out.reshape(B, S, HQ * d)

def forgetting_attention(q, k, v, logf):
    B, S, H, d = q.shape
    nb = S // BLOCK
    scale = d ** -0.5
    c = jnp.cumsum(logf, axis=1)
    c_k = jnp.transpose(c, (0, 2, 1))
    qb = jnp.moveaxis(q.reshape(B, nb, BLOCK, H, d), 1, 0)
    cb = jnp.moveaxis(c.reshape(B, nb, BLOCK, H), 1, 0)
    k_pos = jnp.arange(S)

    def one_block(args):
        qblk, cblk, start = args
        s = jnp.einsum('bqhd,bkhd->bhqk', qblk, k).astype(jnp.float32) * scale
        decay = jnp.transpose(cblk, (0, 2, 1))[:, :, :, None] - c_k[:, :, None, :]
        dist = (start + jnp.arange(BLOCK))[:, None] - k_pos[None, :]
        s = jnp.where((dist >= 0)[None, None], s + decay, -jnp.inf)
        p = jax.nn.softmax(s, axis=-1)
        return jnp.einsum('bhqk,bkhd->bqhd', p.astype(v.dtype), v)

    out = lax.map(one_block, (qb, cb, jnp.arange(nb) * BLOCK))
    return jnp.moveaxis(out, 0, 1).reshape(B, S, H * d)

def second_inputs(seed: int = 0) -> dict:
    key = jax.random.key(seed)
    ks = jax.random.split(key, 16)
    f32 = jnp.float32
    nrm = lambda k, shape: jax.random.normal(k, shape, dtype=f32)
    return {
        "x": nrm(ks[0], (BATCH, SEQ, D_MODEL)),
        "norm_gain": 1.0 + 0.05 * nrm(ks[1], (DEPTH_2, D_MODEL)),
        "w_in": nrm(ks[2], (DEPTH_2, D_MODEL, D_IN)) * D_MODEL ** -0.5,
        "b_forget": 0.1 * nrm(ks[3], (DEPTH_2, C_HEADS)),
        "lambda_q1": 0.1 * nrm(ks[4], (DEPTH_2, HEAD_DIM)),
        "lambda_k1": 0.1 * nrm(ks[5], (DEPTH_2, HEAD_DIM)),
        "lambda_q2": 0.1 * nrm(ks[6], (DEPTH_2, HEAD_DIM)),
        "lambda_k2": 0.1 * nrm(ks[7], (DEPTH_2, HEAD_DIM)),
        "subln_gain": 1.0 + 0.05 * nrm(ks[8], (DEPTH_2, 2 * HEAD_DIM)),
        "sinks": 0.5 * nrm(ks[9], (DEPTH_2, B_HEADS)),
        "w_up_a": nrm(ks[10], (DEPTH_2, A_WIDTH, D_MODEL)) * A_WIDTH ** -0.5,
        "w_up_b": nrm(ks[11], (DEPTH_2, B_WIDTH, D_MODEL)) * B_WIDTH ** -0.5,
        "w_up_c": nrm(ks[12], (DEPTH_2, C_WIDTH, D_MODEL)) * C_WIDTH ** -0.5,
        "w_o": nrm(ks[13], (DEPTH_2, D_MODEL, D_MODEL)) * D_MODEL ** -0.5,
        "final_gain": 1.0 + 0.05 * nrm(ks[14], (D_MODEL,)),
    }

def second_block(x, norm_gain, w_in, b_forget, lambda_q1, lambda_k1, lambda_q2, lambda_k2,
              subln_gain, sinks, w_up_a, w_up_b, w_up_c, w_o, final_gain):
    B, S, D = x.shape
    offsets = np.cumsum(SPLITS)[:-1].tolist()
    slopes_a = alibi_slopes(A_HEADS)
    slopes_b = alibi_slopes(B_HEADS)
    for l in range(DEPTH_2):
        h = rms_norm_2(x, norm_gain[l], RMS_EPS)
        proj = jnp.einsum('bsd,de->bse', h, w_in[l])
        (qa, ka, va, ga, qb, kb, vb, gb,
         qc, kc, vc, fc, gc, gm) = jnp.split(proj, offsets, axis=-1)

        lam_init = 0.8 - 0.6 * math.exp(-0.3 * l)
        lam = (jnp.exp(jnp.sum(lambda_q1[l].astype(jnp.float32) * lambda_k1[l].astype(jnp.float32)))
               - jnp.exp(jnp.sum(lambda_q2[l].astype(jnp.float32) * lambda_k2[l].astype(jnp.float32)))
               + lam_init)
        ya = diff_attention(qa.reshape(B, S, A_HEADS, 2, HEAD_DIM),
                            ka.reshape(B, S, A_HEADS, 2, HEAD_DIM),
                            va.reshape(B, S, A_HEADS, 2 * HEAD_DIM), lam, slopes_a)
        ya = (rms_norm_2(ya, subln_gain[l], SUBLN_EPS) * (1.0 - lam_init)).reshape(B, S, A_WIDTH)

        yb = sliding_window_attention(qb.reshape(B, S, B_HEADS, HEAD_DIM),
                                      kb.reshape(B, S, B_KV_HEADS, HEAD_DIM),
                                      vb.reshape(B, S, B_KV_HEADS, HEAD_DIM),
                                      sinks[l], slopes_b)

        logf = jax.nn.log_sigmoid(fc.astype(jnp.float32) + b_forget[l].astype(jnp.float32))
        yc = forgetting_attention(qc.reshape(B, S, C_HEADS, HEAD_DIM),
                                  kc.reshape(B, S, C_HEADS, HEAD_DIM),
                                  vc.reshape(B, S, C_HEADS, HEAD_DIM), logf)

        ua = jnp.einsum('bse,ed->bsd', ya * jax.nn.silu(ga), w_up_a[l])
        ub = jnp.einsum('bse,ed->bsd', yb * jax.nn.silu(gb), w_up_b[l])
        uc = jnp.einsum('bse,ed->bsd', yc * jax.nn.silu(gc), w_up_c[l])
        gates = jax.nn.sigmoid(gm.reshape(B, S, N_BRANCH, D))
        merged = gates[:, :, 0] * ua + gates[:, :, 1] * ub + gates[:, :, 2] * uc
        x = x + jnp.einsum('bsd,de->bse', merged, w_o[l])
    return rms_norm_2(x, final_gain, RMS_EPS)


def setup_inputs(seed=0):
    out = dict(first_inputs(seed))
    for name, value in second_inputs(seed + 1).items():
        if name != "x":
            out[name + "_2"] = value
    return out


def reference(
    x, mem, even_w_in, even_conv_w, even_conv_b, even_conv_ln_g, even_conv_ln_b,
    even_ssm_conv_w, even_ssm_conv_b, even_dt_bias, even_a_log, even_d_skip, even_ssm_norm_g,
    even_w_out, odd_w_in, odd_w_gate2, odd_b_gate, odd_head_norm_g, odd_w_out, xa_w_q, xa_w_k,
    xa_w_v, xa_w_o, mlp_w1, mlp_w2, ln_g, ln_b, norm_gain_2, w_in_2, b_forget_2, lambda_q1_2,
    lambda_k1_2, lambda_q2_2, lambda_k2_2, subln_gain_2, sinks_2, w_up_a_2, w_up_b_2, w_up_c_2,
    w_o_2, final_gain_2,
):
    x = first_block(
        x, mem, even_w_in, even_conv_w, even_conv_b, even_conv_ln_g, even_conv_ln_b,
        even_ssm_conv_w, even_ssm_conv_b, even_dt_bias, even_a_log, even_d_skip,
        even_ssm_norm_g, even_w_out, odd_w_in, odd_w_gate2, odd_b_gate, odd_head_norm_g,
        odd_w_out, xa_w_q, xa_w_k, xa_w_v, xa_w_o, mlp_w1, mlp_w2, ln_g, ln_b,
    )
    return second_block(
        x, norm_gain_2, w_in_2, b_forget_2, lambda_q1_2, lambda_k1_2, lambda_q2_2, lambda_k2_2,
        subln_gain_2, sinks_2, w_up_a_2, w_up_b_2, w_up_c_2, w_o_2, final_gain_2,
    )


_drawn_inputs = setup_inputs


def setup_inputs(seed=0):
    import zlib

    import numpy as np

    out = dict(_drawn_inputs(seed))
    spreads = {}
    factors = {'even_conv_b': 8.0,
     'even_conv_ln_g': 8.0,
     'even_conv_ln_b': 8.0,
     'even_ssm_conv_b': 8.0,
     'even_d_skip': 8.0,
     'even_ssm_norm_g': 8.0,
     'odd_b_gate': 5.228,
     'odd_head_norm_g': 8.0,
     'b_forget_2': 8.0,
     'lambda_q1_2': 8.0,
     'lambda_k1_2': 6.87,
     'lambda_q2_2': 5.862,
     'lambda_k2_2': 4.373,
     'subln_gain_2': 4.721,
     'sinks_2': 6.835}
    for name, (base, spread) in spreads.items():
        noise = np.random.default_rng([zlib.crc32(name.encode()), seed]).standard_normal(out[name].shape)
        drawn = base * np.exp(spread * noise) if base else spread * noise
        out[name] = __import__('jax').numpy.asarray(drawn.astype(out[name].dtype))
    for name, factor in factors.items():
        out[name] = (out[name] * factor).astype(out[name].dtype)
    return out
```

```python
from contextlib import ExitStack

import concourse.bass as bass
from concourse import mybir

F32 = mybir.dt.float32
F32R = mybir.dt.float32r
ALU = mybir.AluOpType
ACT = mybir.ActivationFunctionType
AX = mybir.AxisListType

P = 128
T = 512
TT = T // P
D = 1024
KC = D // P
PANEL = 256
LN_EPS = 1e-5
RMS_EPS = 1e-6
ALPHA = 4.0 ** 0.25
NEG = -1.0e30

CONV_W = 31
SSM_W = 4
SH = 16
SP_ = 64
XBC = 1536
XC = XBC // P

MEM = 256
XH = 4
GH = 4
GV = 256

RAW_SLOTS = 2
W_SLOTS = 4
LEAD = 3

FM, TM, TM_MEM, FM_MEM, UP = "fm", "tm", "tm_mem", "fm_mem", "up"


def weight_plan():
    plan = []

    def add(stage, weight, row, cols, kind):
        for c in cols:
            plan.append((stage, weight, row, c, kind))

    for j in range(4):
        add("conv_in", "even_w_in", 0, [2 * j * PANEL // 2, D + 2 * j * PANEL // 2], FM)
    add("xbc", "even_w_in", 0, range(3 * D, 3 * D + XBC, PANEL), FM)
    add("z", "even_w_in", 0, range(2 * D, 3 * D, PANEL), TM)
    add("even_out_conv", "even_w_out", 0, range(0, D, PANEL), FM)
    add("even_out_ssm", "even_w_out", D, range(0, D, PANEL), FM)

    def attention(i):
        add(f"xk{i}", f"xa_w_k{i}", 0, range(0, D, PANEL), FM_MEM)
        add(f"xv{i}", f"xa_w_v{i}", 0, range(0, D, PANEL), TM_MEM)
        add(f"xq{i}", f"xa_w_q{i}", 0, range(0, D, PANEL), FM)
        add(f"xo{i}", f"xa_w_o{i}", 0, range(0, D, PANEL), FM)

    def mlp(i):
        for q in range(4):
            add(f"mlp{i}", f"mlp_w1{i}", 0, range(q * D, (q + 1) * D, PANEL), FM)
            add(f"mlp{i}", f"mlp_w2{i}", q * D, range(0, D, PANEL), FM)

    attention(0)
    mlp(0)
    add("gla_qk", "odd_w_in", 0, range(0, D, PANEL), FM)
    add("gla_v", "odd_w_in", 0, range(D, 2 * D, PANEL), TM)
    add("gla_g", "odd_w_in", 0, range(2 * D, 3 * D, PANEL), TM)
    add("odd_out", "odd_w_out", 0, range(0, D, PANEL), FM)
    attention(1)
    mlp(1)
    base = dict(a=0, b=2048, c=3328, gm=5384)
    for n, b in enumerate("abc"):
        if b == "b":
            add("qk_b", "w_in_2q", 0, [base["b"], base["b"] + PANEL], FM)
            add("kv_b", "w_in_2", 0, [base["b"] + 512], "kv")
            add("g_b", "w_in_2", 0, [base["b"] + 768, base["b"] + 1024], TM)
        else:
            add(f"qk_{b}", "w_in_2", 0, range(base[b], base[b] + D, PANEL), FM)
            add(f"v_{b}", "w_in_2", 0, range(base[b] + D, base[b] + D + 512, PANEL), TM)
            g = base[b] + D + 512 + (8 if b == "c" else 0)
            add(f"g_{b}", "w_in_2", 0, range(g, g + 512, PANEL), TM)
        for half in range(2):
            c = base["gm"] + n * D + 512 * half
            add(f"merge_{b}", "w_in_2", 0, [c, c + PANEL], FM)
            add(f"merge_{b}", f"w_up_{b}_2", 0, [512 * half], UP)
    add("w_o", "w_o_2", 0, range(0, D, PANEL), FM)
    return plan


PLAN = weight_plan()
NPANEL = len(PLAN)
FIRST_PANEL = {}
for _n, _p in enumerate(PLAN):
    FIRST_PANEL.setdefault(_p[0], _n)
CHUNKS = {FM: 2, TM: 2, FM_MEM: 2, TM_MEM: 1, UP: 4, "kv": 2}
CHUNK0 = [0]
for _p in PLAN:
    CHUNK0.append(CHUNK0[-1] + CHUNKS[_p[4]])


def stage_chunk(name):
    return CHUNK0[FIRST_PANEL[name]]


def aux_plan():
    e = [("par", i) for i in range(4)] + [("x", k) for k in range(KC)] + [("dt",)]
    for c in range(TT):
        e += [("acs", c)] + [("bc", c, q) for q in range(4)] + [("cb", c), ("xs", c, 0), ("xs", c, 1), ("bt", c)]
        for g in range(2):
            e += [("yd", c, g)] + ([("yo", c, g)] if c else [])
        e += [("st", c, g) for g in range(2)] + [("yt", c, g) for g in range(2)]
    e += [("ln", "conv", i) for i in range(2)]

    def ln(name):
        return [("ln", name, i) for i in range(2)]

    def attention(i):
        out = [("mem", i, j) for j in range(4)]
        out += units("x" + str(i), range(TT), 2, 2)
        return out + [("xpv", i, j) for j in range(KC)]

    def units(name, us, ns, nt, pv=False):
        us = list(us)
        out = [(name, "S", us[0], j) for j in range(ns)]
        for n, u in enumerate(us):
            if n + 1 < len(us):
                out += [(name, "S", us[n + 1], j) for j in range(ns)]
            out += [(name, "T", u, j) for j in range(nt)]
            if pv:
                out += [(name, "PV", u)]
        return out

    e += ln("m0") + attention(0) + ln("a0") + ln("f0")
    e += [("glow",)]
    for hd in range(GH):
        e += [("gate", hd), ("kend", hd)]
        for t in range(TT):
            e += [("gatt", hd, t), ("gkv", hd, t, 0), ("gkv", hd, t, 1), ("go", hd, t)]
        e += [("gt", hd, j) for j in range(2)]
    e += ln("m1") + attention(1) + ln("a1") + ln("f1")
    e += [("rms", 0)]
    e += units("A", [(hd, t) for hd in range(4) for t in range(TT)], 2, 1, True) + [("At", j) for j in range(4)]
    e += units("B", [(hd, t) for hd in range(4) for t in range(TT)], 2, 1, True) + [("Bt", j) for j in range(4)]
    e += [("fc",), ("cc",)]
    for hd in range(8):
        e += [("cb_c", hd)] + units("C", [(hd, t) for t in range(TT)], 1, 1, True)
    e += [("Ct", j) for j in range(4)]
    e += [("rms", 1)] + [("out", t, j) for t in range(TT) for j in range(2)]
    return e


AUX_PLAN = aux_plan()
AUX = {key: n for n, key in enumerate(AUX_PLAN)}
assert len(AUX) == len(AUX_PLAN)

UNITS = ([("x0", t) for t in range(TT)] + [("x1", t) for t in range(TT)]
         + [("A", (hd, t)) for hd in range(4) for t in range(TT)]
         + [("B", (hd, t)) for hd in range(4) for t in range(TT)]
         + [("C", (hd, t)) for hd in range(8) for t in range(TT)])
UNIT = {key: n for n, key in enumerate(UNITS)}

X_FILLS = ["x", "m0", "a0", "f0", "m1", "a1", "rms", "merged"]
PARAMS = [(0, "ln_g", 48), (0, "ln_b", 48),
          (1, "even_conv_ln_g", 8), (1, "even_conv_ln_b", 8), (1, "even_conv_b", 8), (1, "even_ssm_conv_b", 12),
          (1, "even_ssm_norm_g", 8), (1, "odd_b_gate", 4), (1, "odd_head_norm_g", 2), (1, "norm_gain_2", 8),
          (1, "final_gain_2", 8), (1, "subln_gain_2", 1), (1, "even_ssm_conv_w", 48),
          (2, "even_conv_w", 124), (3, "even_conv_w", 124)]
PAR_AT, _rows = {}, [0, 0, 0, 0]
for _g, _name, _n in PARAMS:
    PAR_AT.setdefault(_name, (_g, _rows[_g]))
    _rows[_g] += _n
PAR_ROWS = _rows


def stage_end_chunk(name):
    last = max(n for n, p in enumerate(PLAN) if p[0] == name)
    return CHUNK0[last + 1]

Y_FILLS = [("conv", 8)] + [(f"hid{i}{q}", 8) for i in range(2) for q in range(4)]
Y0, _y = {}, 0
for _name, _n in Y_FILLS:
    Y0[_name] = _y
    _y += _n

GEMM_BANKS = 4
AUX_BANKS = 4


def build(nc, w, out):
    with ExitStack() as ctx:
        sems = {}

        def sb(name, shape, dt=F32):
            return ctx.enter_context(nc.sbuf_tensor(name, shape, dt))

        def sem(name):
            sems[name] = ctx.enter_context(nc.semaphore(name))
            return sems[name]

        raw = sb("raw", [P, RAW_SLOTS, KC, PANEL])
        w_hi = sb("w_hi", [P, W_SLOTS, KC, P], F32R)
        w_lo = sb("w_lo", [P, W_SLOTS, KC, P], F32R)
        x_hi = sb("x_hi", [P, KC, T], F32R)
        x_lo = sb("x_lo", [P, KC, T], F32R)
        y_hi = sb("y_hi", [P, KC, T], F32R)
        y_lo = sb("y_lo", [P, KC, T], F32R)
        h = sb("h", [P, KC, T])
        WN = 18432
        work = sb("work", [P, WN])
        par = sb("par", [P, sum(PAR_ROWS)])
        ident = sb("ident", [P, P])
        triu = sb("triu", [P, P])
        ones = sb("ones", [P, P])
        w_small = sb("w_small", [P, KC, 16])
        row16 = sb("row16", [P, 3, SH])
        cst = sb("cst", [P, 4])
        mxs = sb("mxs", [P, 2, 4])
        rs = sb("rs", [P, 2, 4])
        sm = sb("sm", [P, 16, SH])
        gate2 = sb("gate2", [16, 512])
        lam = sb("lam", [P, 8])

        psum = [ctx.enter_context(nc.psum_tensor(f"gemm{i}", [P, 512], F32)) for i in range(GEMM_BANKS)]
        paux = [ctx.enter_context(nc.psum_tensor(f"aux{i}", [P, 512], F32)) for i in range(AUX_BANKS)]
        h_spill = nc.dram_tensor("h_spill", [P, KC * T], F32, kind="Internal").ap()

        raw_loaded = [sem(f"raw_loaded{i}") for i in range(RAW_SLOTS)]
        w_hi_ready, w_lo_ready = sem("w_hi_ready"), sem("w_lo_ready")
        chunk_done = sem("chunk_done")
        chunk_free = [sem(f"chunk_free{i}") for i in range(GEMM_BANKS)]
        aux_done = sem("aux_done")
        aux_free = [sem(f"aux_free{i}") for i in range(AUX_BANKS)]
        x_ready, y_ready = sem("x_ready"), sem("y_ready")
        x_hi_done, y_hi_done = sem("x_hi_done"), sem("y_hi_done")
        act_step, dve_step, pool_step = sem("act_step"), sem("dve_step"), sem("pool_step")
        stage_end = sem("stage_end")
        consts_ready = sem("consts_ready")
        names = ("par_loaded x_loaded small_loaded rows_loaded spilled reloaded mem_loaded lam_loaded out_sent "
                 "dt_abs dt_soft dta_ready bcr_ready seg_ready dte_ready decay_ready m_ready xdt_ready state_ready "
                 "conv_sum xbc_conv xbc_ready gated ssm_rstd y_gated sq_ready sum_in ln_var ln_rstd ln_xn "
                 "h_ready hid_relu unit_max unit_exp p_ready log_ready b_ready eb_ready qkt_ready s_ready s_read "
                 "gla_rstd o_ready lam_sum lam_ready ya_rstd y_tm_ready c_abs c_soft c_rhs merged_ready").split()
        S = {n: sem(n) for n in names}

        block = ctx.enter_context(nc.Block())

        def area(at, *shape):
            n = 1
            for s in shape:
                n *= s
            v = work[:, at:at + n]
            if len(shape) == 2:
                v = v.rearrange("p (a b) -> p a b", b=shape[1])
            elif len(shape) == 3:
                v = v.rearrange("p (a b c) -> p a b c", b=shape[1], c=shape[2])
            return v

        x_in = area(4336, TT, D)
        par_in = area(0, 4, P)
        U = area(0, KC, T + CONV_W - 1)
        XB = area(4336, XC, T + SSM_W - 1)
        TMP = area(10516, 2, T)
        XS = area(11540, D)
        BT = area(12564, 2, P)
        M = area(12820, SH, P)
        XDT = area(14868, SH, SP_)
        XW = area(15892, SH, SP_)
        ST = area(16916, 2, T)
        LN = area(11540, 5, T)
        Z = h[:, :, :].rearrange("p a b -> p (a b)").rearrange("p (t n) -> p t n", n=D)
        XQ = area(0, KC, T)
        KT = area(4096, KC, MEM)
        VM = area(6144, 2, D)
        PR = area(8192, 2, XH * MEM)
        PTX = area(10240, 2, XH, T)
        mem_in = area(10240, 2, D)
        GQ = area(0, 4, T)
        GK = area(2048, 4, T)
        GVV = area(4096, TT, D)
        GG = area(8192, TT, D)
        GB, GEB, GENB = area(12288, T), area(12800, T), area(13312, T)
        GQE, GQO, GKT = area(13824, T), area(14336, T), area(14848, TT, P)
        GY = area(15360, TT, GV)
        GS = area(16384, GV)
        GA = area(16640, 2, P)
        GL = area(16896, T)
        GMASK = area(17408, T)
        QK = area(0, KC, T)
        BV = area(4096, TT, T)
        BG = area(6144, TT, T)
        MG = area(8192, KC, T)
        YT = area(12288, TT, T)
        EX = area(14336, 2, 2, T)
        PT = area(16384, 2, T)
        GATE = area(14336, 4, T)
        NC = area(17408, T)
        RB = area(17408, 2 * P)
        R = area(17920, T)

        def par_col(name, i=0):
            g, r = PAR_AT[name]
            at = sum(PAR_ROWS[:g]) + r + i
            return par[:, at:at + 1]

        def raw_value(n):
            return 16 * sum(2 if PLAN[m][4] == UP else 4 if PLAN[m][1] == "w_in_2q" else 1
                            for m in range(n % RAW_SLOTS, n + 1, RAW_SLOTS))

        def chunk_end(n):
            return CHUNK0[n + 1]

        def wait_chunk(eng, c):
            eng.wait_ge(chunk_done, c + 1)
            return psum[c % GEMM_BANKS]

        def wait_aux(eng, key):
            eng.wait_ge(aux_done, AUX[key] + 1)
            return paux[AUX[key] % AUX_BANKS]

        def chunk_read(eng, c):
            eng.wait_ge(chunk_free[c % GEMM_BANKS], c // GEMM_BANKS + 1)

        def aux_read(eng, *key):
            eng.wait_ge(aux_free[AUX[key] % AUX_BANKS], AUX[key] // AUX_BANKS + 1)

        def free_chunk(ins, c):
            ins.then_inc(chunk_free[c % GEMM_BANKS], 1)

        def free_aux(ins, key):
            ins.then_inc(aux_free[AUX[key] % AUX_BANKS], 1)

        @block.sync
        def _(sp):
            def load(n):
                stage, name, row, col, kind = PLAN[n]
                s = n % RAW_SLOTS
                if n >= RAW_SLOTS:
                    sp.wait_ge(w_lo_ready, 2 * (n - RAW_SLOTS + 1))
                if kind == UP:
                    src = w[name][0:512, col:col + 512].rearrange("(k p) n -> p k n", p=P)
                    for half in range(2):
                        sp.dma_start(raw[:, s, 4 * half:4 * half + 4, :],
                                     src[:, :, half * PANEL:(half + 1) * PANEL]).then_inc(raw_loaded[s], 16)
                    return
                if name == "w_in_2q":
                    a = (col - 2048) // PANEL
                    src = w["w_in_2"][0:D, 2048:2560].rearrange("(k p) (g j d) -> p k j g d", p=P, g=2, d=64)
                    dst = raw[:, s, :, :].rearrange("p k (j g d) -> p k j g d", g=2, d=64)
                    for j in range(2):
                        for g in range(2):
                            ins = sp.dma_start(dst[:, :, j, g, :], src[:, :, 2 * a + j, g, :])
                            ins.then_inc(raw_loaded[s], 16)
                    return
                src = w[name][row:row + D, col:col + PANEL].rearrange("(k p) n -> p k n", p=P)
                sp.dma_start(raw[:, s, :, :], src).then_inc(raw_loaded[s], 16)

            for n in range(NPANEL):
                load(n)

        @block.gpsimd
        def _(pool):
            steps = [0]

            def step(ins):
                steps[0] += 1
                ins.then_inc(pool_step, 1)
                pool.wait_ge(pool_step, steps[0])

            pool.memset(ones[:, :], 1.0)
            pool.memset(cst[:, 0:1], LN_EPS)
            pool.memset(cst[:, 1:2], RMS_EPS)
            pool.memset(ident[:, :], 0.0)
            step(pool.memset(triu[:, :], 1.0))
            step(pool.affine_select(out=ident[:, :], in_=ident[:, :], compare_op=ALU.not_equal, fill=1.0, base=0,
                                    pattern=[[-1, P]], channel_multiplier=1))
            step(pool.affine_select(out=triu[:, :], in_=triu[:, :], compare_op=ALU.is_ge, fill=0.0, base=0,
                                    pattern=[[1, P]], channel_multiplier=-1))
            pool.drain().then_inc(consts_ready, 1)
            pool.wait_ge(stage_end, 3 * 5)
            step(pool.iota(R, [[1, T]], base=-384, channel_multiplier=-1, allow_small_or_imprecise_dtypes=True))
            step(pool.affine_select(out=R, in_=R, compare_op=ALU.is_ge, fill=NEG, base=384,
                                    pattern=[[-1, T]], channel_multiplier=1))
            step(pool.tensor_copy(RB, R[:, 256:512]))
            step(pool.affine_select(out=RB[:, 0:P], in_=RB[:, 0:P], compare_op=ALU.is_ge, fill=NEG, base=-1,
                                    pattern=[[1, P]], channel_multiplier=-1))
            pool.drain().then_inc(consts_ready, 1)

        @block.tensor
        def _(pe):
            at = dict(panel=0, chunk=0, aux=0, end=0)

            def stage_barrier():
                at["end"] += 1
                pe.drain().then_inc(stage_end, 1)
                pe.wait_ge(stage_end, 3 * at["end"])

            def next_chunk():
                c = at["chunk"]
                if c >= GEMM_BANKS:
                    pe.wait_ge(chunk_free[c % GEMM_BANKS], c // GEMM_BANKS)
                at["chunk"] += 1
                return psum[c % GEMM_BANKS]

            def next_aux(*key):
                a = at["aux"]
                assert AUX_PLAN[a] == key, (AUX_PLAN[a], key)
                if a >= AUX_BANKS:
                    pe.wait_ge(aux_free[a % AUX_BANKS], a // AUX_BANKS)
                at["aux"] += 1
                return paux[a % AUX_BANKS]

            def w_ready(upto):
                pe.wait_ge(w_lo_ready, upto)

            def product3(dst, a_hi, a_lo, b_hi, b_lo, first, last):
                pe.matmul(dst, a_hi, b_hi, start=first, stop=False)
                pe.matmul(dst, a_hi, b_lo, start=False, stop=False)
                return pe.matmul(dst, a_lo, b_hi, start=False, stop=last)

            def gemm(stage, hi, lo, ready=None, panels=None):
                n0 = at["panel"]
                n1 = n0 + panels if panels else n0 + sum(1 for p in PLAN if p[0] == stage)
                seen = [0]

                def operand(k):
                    if ready is not None and k >= seen[0]:
                        ready(k)
                        seen[0] = k + 1

                for n in range(n0, n1):
                    kind = PLAN[n][4]
                    assert PLAN[n][0] == stage
                    if kind in (FM, FM_MEM):
                        cols = T if kind == FM else MEM
                        for s in (2 * n, 2 * n + 1):
                            w_ready(s + 1)
                            dst = next_chunk()
                            for k in range(KC):
                                operand(k)
                                ins = product3(dst[:, 0:cols], w_hi[:, s % W_SLOTS, k, :], w_lo[:, s % W_SLOTS, k, :],
                                               hi[:, k, 0:cols], lo[:, k, 0:cols], k == 0, k == KC - 1)
                            ins.then_inc(chunk_done, 1)
                    elif kind in (TM, TM_MEM):
                        w_ready(2 * n + 2)
                        a = 2 * n % W_SLOTS
                        for t2 in range(2 if kind == TM else 1):
                            dst = next_chunk()
                            for t in range(2):
                                tok = slice((2 * t2 + t) * P, (2 * t2 + t + 1) * P)
                                for k in range(KC):
                                    operand(k)
                                    ins = product3(dst[:, t * PANEL:(t + 1) * PANEL], hi[:, k, tok], lo[:, k, tok],
                                                   w_hi[:, a:a + 2, k, :], w_lo[:, a:a + 2, k, :],
                                                   k == 0, k == KC - 1)
                            ins.then_inc(chunk_done, 1)
                    elif kind == UP:
                        for s in (2 * n, 2 * n + 1):
                            w_ready(s + 1)
                            for half in range(2):
                                dst = next_chunk()
                                for k in range(4):
                                    operand(k)
                                    kk = 4 * half + k
                                    ins = product3(dst[:, :], w_hi[:, s % W_SLOTS, kk, :], w_lo[:, s % W_SLOTS, kk, :],
                                                   hi[:, k, :], lo[:, k, :], k == 0, k == 3)
                                ins.then_inc(chunk_done, 1)
                    else:
                        w_ready(2 * n + 2)
                        a = 2 * n % W_SLOTS
                        dst = next_chunk()
                        for k in range(KC):
                            ins = product3(dst[:, :], w_hi[:, a, k, :], w_lo[:, a, k, :], hi[:, k, :], lo[:, k, :],
                                           k == 0, k == KC - 1)
                        ins.then_inc(chunk_done, 1)
                        dst = next_chunk()
                        for t in range(TT):
                            tok = slice(t * P, (t + 1) * P)
                            for k in range(KC):
                                ins = product3(dst[:, tok], hi[:, k, tok], lo[:, k, tok], w_hi[:, a + 1, k, :],
                                               w_lo[:, a + 1, k, :], k == 0, k == KC - 1)
                        ins.then_inc(chunk_done, 1)
                at["panel"] = n1

            def turn(dst, src):
                return pe.transpose(dst, src, ident[0:src.shape[0], 0:src.shape[0]])

            def layer_sums(name, n):
                pe.wait_ge(S["sum_in"], KC * (n + 1))
                for i in range(2):
                    pe.matmul(next_aux("ln", name, i)[:, :], ones[:, :], LN[:, 3 + i, :], start=True, stop=True)\
                      .then_inc(aux_done, 1)

            def x_fill(name):
                return dict(ready=lambda k: pe.wait_ge(x_ready, KC * X_FILLS.index(name) + k + 1))

            def y_fill(name):
                return dict(ready=lambda k: pe.wait_ge(y_ready, Y0[name] + k + 1))

            pe.wait_ge(consts_ready, 1)
            pe.wait_ge(S["par_loaded"], 16 * len(PARAMS))
            for g in range(4):
                turn(next_aux("par", g)[:, 0:PAR_ROWS[g]], par_in[0:PAR_ROWS[g], g, :]).then_inc(aux_done, 1)
            pe.wait_ge(S["x_loaded"], 16)
            for k in range(KC):
                dst = next_aux("x", k)
                for t in range(TT):
                    ins = turn(dst[:, t * P:(t + 1) * P], x_in[:, t, k * P:(k + 1) * P])
                ins.then_inc(aux_done, 1)
            stage_barrier()

            pe.wait_ge(S["small_loaded"], 16)
            dst = next_aux("dt")
            for t in range(TT):
                for k in range(KC):
                    ins = pe.matmul(dst[:, SH * t:SH * (t + 1)], h[:, k, t * P:(t + 1) * P], w_small[:, k, :],
                                    start=(k == 0), stop=(k == KC - 1))
            ins.then_inc(aux_done, 1)
            gemm("conv_in", x_hi, x_lo, **x_fill("x"))
            gemm("xbc", x_hi, x_lo)
            gemm("z", x_hi, x_lo)
            for c in range(TT):
                tok = slice(SSM_W - 1 + c * P, SSM_W - 1 + (c + 1) * P)
                pe.wait_ge(S["dta_ready"], 1)
                pe.matmul(next_aux("acs", c)[:, 0:SH], triu[:, :], sm[:, c, :], start=True, stop=True)\
                  .then_inc(aux_done, 1)
                pe.wait_ge(S["bcr_ready"], c + 1)
                for q in range(4):
                    pe.matmul(next_aux("bc", c, q)[:, :], ones[:, :], M[:, 4 * q:4 * q + 4, :], start=True, stop=True)\
                      .then_inc(aux_done, 1)
                if c == 0:
                    pe.wait_ge(S["xbc_ready"], XC)
                dst = next_aux("cb", c)
                for g in range(2):
                    ins = pe.matmul(dst[:, g * P:(g + 1) * P], XB[:, 8 + g, tok], XB[:, 10 + g, tok],
                                    start=True, stop=True)
                ins.then_inc(aux_done, 1)
                for half in range(2):
                    dst = next_aux("xs", c, half)
                    for j in range(4):
                        ins = turn(dst[:, j * P:(j + 1) * P], XB[:, 4 * half + j, tok])
                    ins.then_inc(aux_done, 1)
                dst = next_aux("bt", c)
                for g in range(2):
                    ins = turn(dst[:, g * P:(g + 1) * P], XB[:, 8 + g, tok])
                ins.then_inc(aux_done, 1)
                pe.wait_ge(S["m_ready"], c + 1)
                pe.wait_ge(S["xdt_ready"], c + 1)
                aux_read(pe, "bt", c)
                if c:
                    pe.wait_ge(S["state_ready"], c)
                for g in range(2):
                    dst = next_aux("yd", c, g)
                    for j in range(8):
                        ins = pe.matmul(dst[:, 64 * j:64 * j + 64], M[:, 8 * g + j, :], XDT[:, 8 * g + j, :],
                                        start=True, stop=True)
                    ins.then_inc(aux_done, 1)
                    if c:
                        pe.matmul(next_aux("yo", c, g)[:, :], XB[:, 10 + g, tok], ST[:, g, :], start=True, stop=True)\
                          .then_inc(aux_done, 1)
                for g in range(2):
                    pe.matmul(next_aux("st", c, g)[:, :], BT[:, g, :], XW[:, 8 * g:8 * g + 8, :],
                              start=True, stop=True).then_inc(aux_done, 1)
                pe.wait_ge(S["y_gated"], c + 1)
                yv = XDT.rearrange("p a b -> p (a b)")
                for g in range(2):
                    dst = next_aux("yt", c, g)
                    for j in range(4):
                        ins = turn(dst[:, j * P:(j + 1) * P], yv[:, (4 * g + j) * P:(4 * g + j + 1) * P])
                    ins.then_inc(aux_done, 1)
            layer_sums("conv", 0)
            gemm("even_out_conv", y_hi, y_lo, **y_fill("conv"))
            gemm("even_out_ssm", x_hi, x_lo, ready=lambda k: aux_read(pe, "yt", TT - 1, k // 4))
            layer_sums("m0", 1)
            stage_barrier()

            def cross_attention(i):
                pe.wait_ge(S["mem_loaded"], 16 * (i + 1))
                for e in range(4):
                    dst = next_aux("mem", i, e)
                    for kk in range(2):
                        for t in range(2):
                            k = 2 * e + kk
                            ins = turn(dst[:, kk * MEM + t * P:kk * MEM + (t + 1) * P], mem_in[:, t, k * P:(k + 1) * P])
                    ins.then_inc(aux_done, 1)
                gemm(f"xk{i}", y_hi, y_lo, ready=lambda k: aux_read(pe, "mem", i, k // 2))
                gemm(f"xv{i}", y_hi, y_lo)
                gemm(f"xq{i}", x_hi, x_lo, **x_fill(f"m{i}"))
                chunk_read(pe, stage_end_chunk(f"xq{i}") - 1)
                name = f"x{i}"

                def scores(t):
                    for e in range(2):
                        dst = next_aux(name, "S", t, e)
                        for hh in range(2):
                            for d in range(2):
                                k = 2 * (2 * e + hh) + d
                                ins = pe.matmul(dst[:, hh * MEM:(hh + 1) * MEM], XQ[:, k, t * P:(t + 1) * P],
                                                KT[:, k, :], start=(d == 0), stop=(d == 1))
                        ins.then_inc(aux_done, 1)

                scores(0)
                for t in range(TT):
                    if t + 1 < TT:
                        scores(t + 1)
                    pe.wait_ge(S["p_ready"], UNIT[(name, t)] + 1)
                    for m in range(2):
                        dst = next_aux(name, "T", t, m)
                        for hd in range(XH):
                            ins = turn(dst[:, hd * P:(hd + 1) * P],
                                       PR[:, t % 2, hd * MEM + m * P:hd * MEM + (m + 1) * P])
                        ins.then_inc(aux_done, 1)
                aux_read(pe, name, "T", TT - 1, 1)
                for j in range(KC):
                    dst = next_aux("xpv", i, j)
                    for m in range(2):
                        ins = pe.matmul(dst[:, :], VM[:, m, j * P:(j + 1) * P], PTX[:, m, j // 2, :],
                                        start=(m == 0), stop=(m == 1))
                    ins.then_inc(aux_done, 1)
                gemm(f"xo{i}", x_hi, x_lo, ready=lambda k: aux_read(pe, "xpv", i, k))
                layer_sums(f"a{i}", 2 + 3 * i)
                stage_barrier()

            def mlp(i):
                for q in range(4):
                    gemm(f"mlp{i}", x_hi, x_lo, panels=4, **x_fill(f"a{i}"))
                    gemm(f"mlp{i}", y_hi, y_lo, panels=4, **y_fill(f"hid{i}{q}"))
                layer_sums(f"f{i}", 3 + 3 * i)
                stage_barrier()

            cross_attention(0)
            mlp(0)

            pe.wait_ge(S["small_loaded"], 32)
            pe.wait_ge(x_ready, KC * (X_FILLS.index("f0") + 1))
            dst = next_aux("glow")
            for k in range(KC):
                ins = pe.matmul(dst[0:16, :], w_small[:, k, :], h[:, k, :], start=(k == 0), stop=(k == KC - 1))
            ins.then_inc(aux_done, 1)
            gemm("gla_qk", x_hi, x_lo)
            gemm("gla_v", x_hi, x_lo)
            gemm("gla_g", x_hi, x_lo)
            aux_read(pe, "glow")
            chunk_read(pe, stage_end_chunk("gla_g") - 1)
            for hd in range(GH):
                pe.matmul(next_aux("gate", hd)[:, :], gate2[:, hd * P:(hd + 1) * P], GL[0:16, :],
                          start=True, stop=True).then_inc(aux_done, 1)
                pe.wait_ge(S["qkt_ready"], hd + 1)
                dst = next_aux("kend", hd)
                for t in range(TT):
                    ins = turn(dst[:, t * P:(t + 1) * P], GK[:, hd, t * P:(t + 1) * P])
                ins.then_inc(aux_done, 1)
                for t in range(TT):
                    tok = slice(t * P, (t + 1) * P)
                    vt = GVV[:, t, hd * GV:(hd + 1) * GV]
                    u = TT * hd + t
                    pe.matmul(next_aux("gatt", hd, t)[:, 0:P], GENB[:, tok], GQ[:, hd, tok], start=True, stop=True)\
                      .then_inc(aux_done, 1)
                    if t == 0:
                        aux_read(pe, "kend", hd)
                    for half in range(2):
                        a, b = 64 * half, 64 * half + 64
                        pe.matmul(next_aux("gkv", hd, t, half)[:, 0:GV], GKT[a:b, t, :], vt[a:b, :],
                                  start=True, stop=True).then_inc(aux_done, 1)
                    aux_read(pe, "gatt", hd, t)
                    dst = next_aux("go", hd, t)
                    pe.matmul(dst[:, 0:GV], GA[:, u % 2, :], vt, start=True, stop=False)
                    if t == 0:
                        pe.wait_ge(S["s_ready"], hd + 1)
                    else:
                        aux_read(pe, "gkv", hd, t - 1, 1)
                    pe.matmul(dst[:, 0:GV], GQE[:, tok], GS, start=False, stop=False).then_inc(S["s_read"], 1)
                    aux_read(pe, "gkv", hd, t, 0)
                    pe.matmul(dst[:, 0:GV], GQO[:, tok], GS, start=False, stop=True).then_inc(aux_done, 1)
                pe.wait_ge(S["o_ready"], hd + 1)
                for j in range(2):
                    dst = next_aux("gt", hd, j)
                    for t in range(TT):
                        ins = turn(dst[:, t * P:(t + 1) * P], GY[:, t, j * P:(j + 1) * P])
                    ins.then_inc(aux_done, 1)
            gemm("odd_out", x_hi, x_lo, ready=lambda k: aux_read(pe, "gt", k // 2, k % 2))
            layer_sums("m1", 4)
            stage_barrier()
            cross_attention(1)
            mlp(1)

            def square_sum(i):
                pe.wait_ge(S["sum_in"], KC * (7 + i + 1))
                pe.matmul(next_aux("rms", i)[:, :], ones[:, :], LN[:, 4, :], start=True, stop=True)\
                  .then_inc(aux_done, 1)

            def units(name, us, scores, nt, turns, values):
                scores(us[0])
                for n, u in enumerate(us):
                    if n + 1 < len(us):
                        scores(us[n + 1])
                    pe.wait_ge(S["p_ready"], UNIT[(name, u)] + 1)
                    turns(u, next_aux(name, "T", u, 0)).then_inc(aux_done, 1)
                    aux_read(pe, name, "T", u, 0)
                    values(u, next_aux(name, "PV", u)).then_inc(aux_done, 1)

            def turned_output(name, b, n):
                pe.wait_ge(S["y_tm_ready"], n + 1)
                for j in range(4):
                    dst = next_aux(name, j)
                    for t in range(TT):
                        ins = turn(dst[:, t * P:(t + 1) * P], YT[:, t, j * P:(j + 1) * P])
                    ins.then_inc(aux_done, 1)
                for half in range(2):
                    gemm(f"merge_{b}", x_hi, x_lo, panels=2)
                    gemm(f"merge_{b}", y_hi, y_lo, panels=1, ready=lambda k: aux_read(pe, name, k))

            square_sum(0)
            gemm("qk_a", x_hi, x_lo, **x_fill("rms"))
            gemm("v_a", x_hi, x_lo)
            gemm("g_a", x_hi, x_lo)
            chunk_read(pe, stage_end_chunk("g_a") - 1)

            def scores_a(u):
                hd, t = u
                for m in range(2):
                    a = 64 * m
                    pe.matmul(next_aux("A", "S", u, m)[:, 0:(t + 1) * P], QK[a:a + 64, hd, t * P:(t + 1) * P],
                              QK[a:a + 64, 4 + hd, 0:(t + 1) * P], start=True, stop=True).then_inc(aux_done, 1)

            def turns_a(u, dst):
                e = UNIT[("A", u)] % 2
                for kt in range(u[1] + 1):
                    ins = turn(dst[:, kt * P:(kt + 1) * P], EX[:, e, 0, kt * P:(kt + 1) * P])
                return ins

            def values_a(u, dst):
                hd, t = u
                e = UNIT[("A", u)] % 2
                for kt in range(t + 1):
                    ins = pe.matmul(dst[:, 0:P], PT[:, e, kt * P:(kt + 1) * P], BV[:, kt, hd * P:(hd + 1) * P],
                                    start=(kt == 0), stop=(kt == t))
                return ins

            units("A", [(hd, t) for hd in range(4) for t in range(TT)], scores_a, 1, turns_a, values_a)
            turned_output("At", "a", 0)

            gemm("qk_b", x_hi, x_lo)
            gemm("kv_b", x_hi, x_lo)
            gemm("g_b", x_hi, x_lo)
            chunk_read(pe, stage_end_chunk("g_b") - 1)

            def scores_b(u):
                j, t = u
                for g in range(2):
                    a = 64 * g
                    lo_key = max(t - 1, 0) * P
                    off = P if t == 0 else 0
                    pe.matmul(next_aux("B", "S", u, g)[:, off:256], QK[a:a + 64, j, t * P:(t + 1) * P],
                              QK[a:a + 64, 4, lo_key:(t + 1) * P], start=True, stop=True).then_inc(aux_done, 1)

            def turns_b(u, dst):
                e = UNIT[("B", u)] % 2
                for g in range(2):
                    for kk in range(1 if u[1] == 0 else 0, 2):
                        s = slice(g * 256 + kk * P, g * 256 + (kk + 1) * P)
                        ins = turn(dst[:, s], EX[:, e, 0, s])
                return ins

            def values_b(u, dst):
                j, t = u
                e = UNIT[("B", u)] % 2
                for g in range(2):
                    for kk in range(1 if t == 0 else 0, 2):
                        s = slice(g * 256 + kk * P, g * 256 + (kk + 1) * P)
                        ins = pe.matmul(dst[:, g * 64:(g + 1) * 64], PT[:, e, s],
                                        BV[:, t - 1 + kk, g * 64:(g + 1) * 64],
                                        start=(kk == 1 or False) if t == 0 else (kk == 0), stop=(kk == 1))
                return ins

            units("B", [(hd, t) for hd in range(4) for t in range(TT)], scores_b, 1, turns_b, values_b)
            turned_output("Bt", "b", 1)

            gemm("qk_c", x_hi, x_lo)
            gemm("v_c", x_hi, x_lo)
            pe.wait_ge(S["small_loaded"], 48)
            dst = next_aux("fc")
            for t in range(TT):
                for k in range(KC):
                    for part in range(2):
                        xx = (x_hi, x_lo)[part][:, k, t * P:(t + 1) * P].bitcast(F32)
                        ins = pe.matmul(dst[:, 8 * t:8 * t + 8], xx, w_small[:, k, 0:8],
                                        start=(k == 0 and part == 0), stop=(k == KC - 1 and part == 1))
            ins.then_inc(aux_done, 1)
            gemm("g_c", x_hi, x_lo)
            chunk_read(pe, stage_end_chunk("g_c") - 1)
            pe.wait_ge(S["log_ready"], GH + 1)
            dst = next_aux("cc")
            for t in range(TT):
                for s in range(t + 1):
                    ins = pe.matmul(dst[:, 8 * t:8 * t + 8], (triu if s == t else ones)[:, :], sm[:, s, 0:8],
                                    start=(s == 0), stop=(s == t))
            ins.then_inc(aux_done, 1)

            def scores_c(u):
                hd, t = u
                a = 64 * (hd % 2)
                pe.matmul(next_aux("C", "S", u, 0)[:, 0:(t + 1) * P], QK[a:a + 64, hd // 2, t * P:(t + 1) * P],
                          QK[a:a + 64, 4 + hd // 2, 0:(t + 1) * P], start=True, stop=True).then_inc(aux_done, 1)

            def turns_c(u, dst):
                e = UNIT[("C", u)] % 2
                for kt in range(u[1] + 1):
                    ins = turn(dst[:, kt * P:(kt + 1) * P], EX[:, e, 0, kt * P:(kt + 1) * P])
                return ins

            def values_c(u, dst):
                hd, t = u
                e = UNIT[("C", u)] % 2
                for kt in range(t + 1):
                    ins = pe.matmul(dst[:, 0:64], PT[:, e, kt * P:(kt + 1) * P], BV[:, kt, hd * 64:(hd + 1) * 64],
                                    start=(kt == 0), stop=(kt == t))
                return ins

            for hd in range(8):
                pe.wait_ge(S["c_rhs"], hd + 1)
                pe.matmul(next_aux("cb_c", hd)[:, :], ones[:, :], NC, start=True, stop=True).then_inc(aux_done, 1)
                units("C", [(hd, t) for t in range(TT)], scores_c, 1, turns_c, values_c)
            turned_output("Ct", "c", 2)
            gemm("w_o", x_hi, x_lo, **x_fill("merged"))
            square_sum(1)
            pe.wait_ge(S["h_ready"], KC * 9)
            for t in range(TT):
                for j in range(2):
                    dst = next_aux("out", t, j)
                    for k in range(4):
                        ins = turn(dst[:, k * P:(k + 1) * P], MG[:, 4 * j + k, t * P:(t + 1) * P])
                    ins.then_inc(aux_done, 1)
            assert at["panel"] == NPANEL and at["aux"] == len(AUX_PLAN)

        @block.scalar
        def _(act):
            at = dict(step=0, split=0, end=0, ln=0, sq=0, hr=0, xh=0, yh=0)

            def step(ins):
                at["step"] += 1
                ins.then_inc(act_step, 1)
                act.wait_ge(act_step, at["step"])

            def stage_barrier():
                at["end"] += 1
                act.drain().then_inc(stage_end, 1)
                act.wait_ge(stage_end, 3 * at["end"])

            def split_to(panel):
                while at["split"] < min(2 * panel + 2, 2 * NPANEL):
                    s = at["split"]
                    n = s // 2
                    act.wait_ge(raw_loaded[n % RAW_SLOTS], raw_value(n))
                    if s >= W_SLOTS:
                        done = (s - W_SLOTS) // 2
                        if PLAN[done][4] in (FM, FM_MEM):
                            act.wait_ge(chunk_done, CHUNK0[done] + (s % 2) + 1)
                        else:
                            act.wait_ge(chunk_done, chunk_end(done))
                    act.activation(w_hi[:, s % W_SLOTS, :, :], raw[:, n % RAW_SLOTS, :, (s % 2) * P:(s % 2 + 1) * P],
                                   ACT.Copy).then_inc(w_hi_ready, 1)
                    at["split"] += 1

            def operand_hi(dst, src, done, scale=1.0):
                act.activation(dst, src, ACT.Identity, scale=scale).then_inc(done, 1)

            def squares(src, waits):
                for k in range(KC):
                    waits(k)
                    if at["sq"] % KC >= 2:
                        act.wait_ge(S["sum_in"], at["sq"] - 1)
                    act.activation(LN[:, k % 2, :], src(k), ACT.Square).then_inc(S["sq_ready"], 1)
                    at["sq"] += 1

            def normalised(dst, gain, bias, func=ACT.Identity, eps=0, rms=False):
                n = at["ln"]
                act.wait_ge(S["ln_var"], n + 1)
                step(act.activation(LN[:, 2, :], LN[:, 1, :], ACT.Ln, bias=cst[:, eps:eps + 1]))
                act.activation(LN[:, 2, :], LN[:, 2, :], ACT.Exp, scale=-0.5).then_inc(S["ln_rstd"], 1)
                at["ln"] += 1
                for k in range(KC):
                    act.wait_ge(S["ln_xn"], KC * n + k + 1)
                    if rms:
                        act.activation(dst(k), LN[:, 3 + k % 2, :], func, scale=gain(k)).then_inc(S["h_ready"], 1)
                    else:
                        act.activation(dst(k), LN[:, 3 + k % 2, :], func, bias=bias(k), scale=gain(k))\
                           .then_inc(S["h_ready"], 1)

            def residual_squares(stage, half=0, panels=4):
                def waits(k):
                    n = FIRST_PANEL[stage] + half + k // 2
                    if k % 2 == 0:
                        split_to(n + 1)
                    chunk_read(act, CHUNK0[n] + k % 2)
                squares(lambda k: h[:, k, :], waits)

            def ln_cols(i, j):
                r = (3 * i + j) * KC
                return (lambda k: par_col("ln_g", r + k)), (lambda k: par_col("ln_b", r + k))

            def layer_norm(i, j):
                g, b = ln_cols(i, j)
                normalised(lambda k: h[:, k, :], g, b)

            count = [0, 0, 0, 0]
            for g, name, n in PARAMS:
                src = w[name]
                if name == "even_conv_w":
                    src = src.rearrange("w (c p) -> (w c) p", p=P)
                    src = src[0:124, :] if g == 2 else src[124:248, :]
                elif name == "even_ssm_conv_w":
                    src = src.rearrange("w (c p) -> (w c) p", p=P)
                elif name in ("ln_g", "ln_b"):
                    src = src.rearrange("i j (c p) -> (i j c) p", p=P)
                else:
                    src = src.rearrange("(c p) -> c p", p=P)
                act.dma_start(par_in[count[g]:count[g] + n, g, :], src).then_inc(S["par_loaded"], 16)
                count[g] += n
            act.dma_start(x_in, w["x"].rearrange("(t p) n -> p t n", p=P)).then_inc(S["x_loaded"], 16)
            act.dma_start(w_small[:, :, :], w["even_w_in"][:, 4608:4624].rearrange("(k p) n -> p k n", p=P))\
               .then_inc(S["small_loaded"], 16)
            for i, name in enumerate(("even_dt_bias", "even_a_log", "even_d_skip")):
                act.dma_start(row16[:, i, :], w[name].unsqueeze(0).broadcast_to([P, SH])).then_inc(S["rows_loaded"], 16)
            act.dma_start(gate2[:, :], w["odd_w_gate2"]).then_inc(S["rows_loaded"], 16)
            split_to(1)
            for g in range(4):
                bank = wait_aux(act, ("par", g))
                r = sum(PAR_ROWS[:g])
                free_aux(act.activation(par[:, r:r + PAR_ROWS[g]], bank[:, 0:PAR_ROWS[g]], ACT.Copy), ("par", g))
            for k in range(KC):
                bank = wait_aux(act, ("x", k))
                free_aux(act.activation(h[:, k, :], bank[:, :], ACT.Copy), ("x", k))
            act.wait_ge(S["rows_loaded"], 64)
            step(act.activation(row16[:, 1, :], row16[:, 1, :], ACT.Exp))
            stage_barrier()

            act.dma_start(h_spill, h[:, :, :].rearrange("p a b -> p (a b)")).then_inc(S["spilled"], 16)
            act.wait_ge(S["dt_abs"], 1)
            step(act.activation(work[:, 17940:18004], work[:, 17940:18004], ACT.Exp, scale=-1.0))
            act.activation(work[:, 17940:18004], work[:, 17940:18004], ACT.Ln, bias=1.0).then_inc(S["dt_soft"], 1)
            for f in range(KC):
                split_to(f + 2)
                c = 4 * (f // 2) + 2 + f % 2
                bank = wait_chunk(act, c)
                if f >= 2:
                    chunk_read(act, 4 * ((f - 2) // 2) + f % 2)
                free_chunk(act.activation(TMP[:, f % 2, :], bank[:, :], ACT.Sigmoid), c)
            for j in range(XC):
                if j % 2 == 0:
                    split_to(FIRST_PANEL["xbc"] + j // 2 + 1)
                c = stage_chunk("xbc") + j
                bank = wait_chunk(act, c)
                free_chunk(act.activation(XB[:, j, SSM_W - 1:], bank[:, :], ACT.Copy), c)
            act.wait_ge(S["spilled"], 16)
            for n in range(4):
                split_to(FIRST_PANEL["z"] + n + 1)
                for t2 in range(2):
                    c = stage_chunk("z") + 2 * n + t2
                    bank = wait_chunk(act, c)
                    free_chunk(act.activation(Z[:, 2 * t2:2 * t2 + 2, n * PANEL:(n + 1) * PANEL],
                                              bank[:, :].rearrange("p (t n) -> p t n", t=2), ACT.Silu), c)
            for j in range(XC):
                act.wait_ge(S["xbc_conv"], j + 1)
                act.activation(XB[:, j, SSM_W - 1:], TMP[:, j % 2, :], ACT.Silu).then_inc(S["xbc_ready"], 1)
            for c in range(TT):
                tok = slice(c * P, (c + 1) * P)
                act.wait_ge(S["seg_ready"], c + 1)
                act.activation(sm[:, 9, :], sm[:, 9, :], ACT.Exp)
                act.activation(sm[:, 10, :], sm[:, 10, :], ACT.Exp)
                act.activation(sm[:, 11, :], sm[:, 8, :], ACT.Exp).then_inc(S["dte_ready"], 1)
                act.activation(M, M, ACT.Exp).then_inc(S["decay_ready"], 1)
                for half in range(2):
                    bank = wait_aux(act, ("xs", c, half))
                    free_aux(act.activation(XS[:, half * 512:(half + 1) * 512], bank[:, :], ACT.Copy), ("xs", c, half))
                bank = wait_aux(act, ("bt", c))
                free_aux(act.activation(BT.rearrange("p a b -> p (a b)"), bank[:, 0:256], ACT.Copy), ("bt", c))
                act.wait_ge(S["gated"], c + 1)
                for g in range(2):
                    ins = act.activation(M[:, 4 * g:4 * g + 4, :], XDT[:, 8 * g:8 * g + 8, :].rearrange("p a b -> p (a b)").rearrange("p (a b) -> p a b", b=P),
                                         ACT.Square, accum_out=rs[:, 0, g:g + 1])
                step(ins)
                step(act.activation(rs[:, 1, 0:2], rs[:, 0, 0:2], ACT.Ln, bias=cst[:, 0:1], scale=1.0 / 512))
                act.activation(rs[:, 1, 0:2], rs[:, 1, 0:2], ACT.Exp, scale=-0.5).then_inc(S["ssm_rstd"], 1)
                for g in range(2):
                    bank = wait_aux(act, ("yt", c, g))
                    for j in range(4):
                        ins = act.activation(x_hi[:, 4 * g + j, tok], bank[:, j * P:(j + 1) * P], ACT.Identity,
                                             scale=par_col("even_ssm_norm_g", 4 * g + j))
                    ins.then_inc(x_hi_done, 1)
            act.wait_ge(S["y_gated"], TT)
            act.dma_start(h[:, :, :].rearrange("p a b -> p (a b)"), h_spill).then_inc(S["reloaded"], 16)
            squares(lambda k: U[:, k, CONV_W - 1:], lambda k: act.wait_ge(S["conv_sum"], k + 1))
            normalised(lambda k: U[:, k, CONV_W - 1:], lambda k: par_col("even_conv_ln_g", k),
                       lambda k: par_col("even_conv_ln_b", k), ACT.Silu)
            for n in range(4):
                split_to(FIRST_PANEL["even_out_conv"] + n + 1)
            residual_squares("even_out_ssm")
            layer_norm(0, 0)
            stage_barrier()

            def cross_attention(i):
                name = f"x{i}"
                act.dma_start(mem_in, w["mem"].rearrange("(t p) n -> p t n", p=P)).then_inc(S["mem_loaded"], 16)
                for e in range(4):
                    bank = wait_aux(act, ("mem", i, e))
                    operand_hi(y_hi[:, 2 * e:2 * e + 2, 0:MEM], bank[:, :].rearrange("p (a b) -> p a b", a=2), y_hi_done)
                for n in range(4):
                    split_to(FIRST_PANEL[f"xk{i}"] + n + 1)
                    for s in range(2):
                        c = stage_chunk(f"xk{i}") + 2 * n + s
                        bank = wait_chunk(act, c)
                        free_chunk(act.activation(KT[:, 2 * n + s, :], bank[:, 0:MEM], ACT.Copy), c)
                for n in range(4):
                    split_to(FIRST_PANEL[f"xv{i}"] + n + 1)
                    c = stage_chunk(f"xv{i}") + n
                    bank = wait_chunk(act, c)
                    free_chunk(act.activation(VM[:, :, n * PANEL:(n + 1) * PANEL],
                                              bank[:, :].rearrange("p (t n) -> p t n", t=2), ACT.Copy), c)
                for n in range(4):
                    split_to(FIRST_PANEL[f"xq{i}"] + n + 1)
                    for s in range(2):
                        c = stage_chunk(f"xq{i}") + 2 * n + s
                        bank = wait_chunk(act, c)
                        free_chunk(act.activation(XQ[:, 2 * n + s, :], bank[:, :], ACT.Copy, scale=1.0 / 16), c)

                def exps(t):
                    un = UNIT[(name, t)]
                    act.wait_ge(S["unit_max"], un + 1)
                    for hd in range(XH):
                        key = (name, "S", t, hd // 2)
                        ins = act.activation(PR[:, t % 2, hd * MEM:(hd + 1) * MEM],
                                             wait_aux(act, key)[:, (hd % 2) * MEM:(hd % 2 + 1) * MEM], ACT.Exp,
                                             bias=mxs[:, un % 2, hd:hd + 1], accum_out=rs[:, un % 2, hd:hd + 1])
                        if hd % 2:
                            free_aux(ins, key)

                exps(0)
                for t in range(TT):
                    if t + 1 < TT:
                        exps(t + 1)
                    for m in range(2):
                        bank = wait_aux(act, (name, "T", t, m))
                        free_aux(act.activation(PTX[:, m, :, t * P:(t + 1) * P],
                                                bank[:, :].rearrange("p (a b) -> p a b", b=P), ACT.Copy),
                                 (name, "T", t, m))
                for j in range(KC):
                    bank = wait_aux(act, ("xpv", i, j))
                    operand_hi(x_hi[:, j, :], bank[:, :], x_hi_done)
                residual_squares(f"xo{i}")
                layer_norm(i, 1)
                stage_barrier()

            def mlp(i):
                st = f"mlp{i}"
                for q in range(4):
                    for k in range(KC):
                        n = FIRST_PANEL[st] + 8 * q + k // 2
                        split_to(n + 1)
                        c = CHUNK0[n] + k % 2
                        bank = wait_chunk(act, c)
                        m = 32 * i + KC * q + k
                        if m % 32 >= 2:
                            act.wait_ge(y_ready, Y0[f"hid{i}0"] + (m % 32) - 1)
                        free_chunk(act.activation(area(0, 2, T)[:, k % 2, :], bank[:, :], ACT.Relu), c)
                        chunk_read(act, c)
                        act.activation(area(0, 2, T)[:, k % 2, :], area(0, 2, T)[:, k % 2, :], ACT.Square)\
                           .then_inc(S["hid_relu"], 1)
                    if q < 3:
                        for k in range(4):
                            split_to(FIRST_PANEL[st] + 8 * q + 4 + k + 1)
                    else:
                        residual_squares(st, half=28)
                layer_norm(i, 2)
                stage_barrier()

            cross_attention(0)
            act.dma_start(w_small[:, :, :], w["odd_w_in"][:, 3072:3088].rearrange("(k p) n -> p k n", p=P))\
               .then_inc(S["small_loaded"], 16)
            mlp(0)

            bank = wait_aux(act, ("glow",))
            free_aux(act.activation(GL[0:16, :], bank[0:16, :], ACT.Copy), ("glow",))
            for j in range(KC):
                if j % 2 == 0:
                    split_to(FIRST_PANEL["gla_qk"] + j // 2 + 1)
                c = stage_chunk("gla_qk") + j
                bank = wait_chunk(act, c)
                free_chunk(act.activation((GQ if j < 4 else GK)[:, j % 4, :], bank[:, :], ACT.Copy,
                                          scale=128.0 ** -0.5 if j < 4 else 1.0), c)
            for stage, dst, func in (("gla_v", GVV, ACT.Copy), ("gla_g", GG, ACT.Silu)):
                for n in range(4):
                    split_to(FIRST_PANEL[stage] + n + 1)
                    for t2 in range(2):
                        c = stage_chunk(stage) + 2 * n + t2
                        bank = wait_chunk(act, c)
                        free_chunk(act.activation(dst[:, 2 * t2:2 * t2 + 2, n * PANEL:(n + 1) * PANEL],
                                                  bank[:, :].rearrange("p (t n) -> p t n", t=2), func), c)
            for hd in range(GH):
                act.wait_ge(S["log_ready"], hd + 1)
                step(act.activation(GEB, GEB, ACT.Exp, scale=-1.0))
                act.activation(GEB, GEB, ACT.Ln, bias=1.0).then_inc(S["eb_ready"], 1)
                act.wait_ge(S["b_ready"], hd + 1)
                act.activation(GEB, GB, ACT.Exp)
                act.activation(GENB, GB, ACT.Exp, scale=-1.0)
                for n in range(8):
                    ins = act.activation(GKT.rearrange("p a b -> p (a b)")[:, 64 * n:64 * n + 64],
                                         GB[:, 64 * n:64 * n + 64], ACT.Exp, scale=-1.0,
                                         bias=GB[:, 64 * n + 63:64 * n + 64])
                ins.then_inc(S["eb_ready"], 1)
                bank = wait_aux(act, ("kend", hd))
                free_aux(act.activation(GKT.rearrange("p a b -> p (a b)"), bank[:, :], ACT.Copy), ("kend", hd))
                for t in range(TT):
                    aux_read(act, "go", hd, t)
                    step(act.activation(area(17920, GV), GY[:, t, :], ACT.Square, accum_out=rs[:, 0, 0:1]))
                    step(act.activation(rs[:, 1, 0:1], rs[:, 0, 0:1], ACT.Ln, bias=cst[:, 0:1], scale=1.0 / GV))
                    act.activation(rs[:, 1, 0:1], rs[:, 1, 0:1], ACT.Exp, scale=-0.5).then_inc(S["gla_rstd"], 1)
                for j in range(2):
                    bank = wait_aux(act, ("gt", hd, j))
                    operand_hi(x_hi[:, 2 * hd + j, :], bank[:, :], x_hi_done, par_col("odd_head_norm_g", j))
            residual_squares("odd_out")
            layer_norm(1, 0)
            stage_barrier()
            cross_attention(1)
            act.dma_start(w_small[:, :, 0:8], w["w_in_2"][:, 4864:4872].rearrange("(k p) n -> p k n", p=P))\
               .then_inc(S["small_loaded"], 16)
            act.dma_start(row16[:, 0, 0:8], w["b_forget_2"].unsqueeze(0).broadcast_to([P, 8]))\
               .then_inc(S["lam_loaded"], 16)
            act.dma_start(row16[:, 1, 0:8], w["sinks_2"].unsqueeze(0).broadcast_to([P, 8]))\
               .then_inc(S["lam_loaded"], 16)
            mlp(1)

            for i, n_ in enumerate(("lambda_q1_2", "lambda_k1_2", "lambda_q2_2", "lambda_k2_2")):
                act.dma_start(PT[:, 0, 64 * i:64 * i + 64], w[n_].unsqueeze(0).broadcast_to([P, 64]))\
                   .then_inc(S["lam_loaded"], 16)
            act.wait_ge(S["lam_sum"], 1)
            act.activation(lam[:, 0:2], lam[:, 0:2], ACT.Exp).then_inc(S["lam_ready"], 1)

            squares(lambda k: h[:, k, :], lambda k: None)
            normalised(lambda k: x_hi[:, k, :], lambda k: par_col("norm_gain_2", k), None, eps=1, rms=True)
            for n_, b in enumerate("abc"):
                scale = 1.0 / 8
                nq = 4
                for j in range(4 if b == "b" else KC):
                    if j % 2 == 0:
                        split_to(FIRST_PANEL[f"qk_{b}"] + j // 2 + 1)
                    c = stage_chunk(f"qk_{b}") + j
                    bank = wait_chunk(act, c)
                    free_chunk(act.activation(QK[:, j, :], bank[:, :], ACT.Copy, scale=scale if j < nq else 1.0), c)
                if b == "b":
                    split_to(FIRST_PANEL["kv_b"] + 1)
                    c = stage_chunk("kv_b")
                    bank = wait_chunk(act, c)
                    free_chunk(act.activation(QK[:, 4, :], bank[:, :], ACT.Copy), c)
                    bank = wait_chunk(act, c + 1)
                    free_chunk(act.activation(BV[:, :, 0:P], bank[:, :].rearrange("p (t n) -> p t n", n=P),
                                              ACT.Copy), c + 1)
                for stage, dst, func in ((f"v_{b}", BV, ACT.Copy), (f"g_{b}", BG, ACT.Silu)):
                    if stage not in FIRST_PANEL:
                        continue
                    for n in range(2):
                        split_to(FIRST_PANEL[stage] + n + 1)
                        for t2 in range(2):
                            c = stage_chunk(stage) + 2 * n + t2
                            bank = wait_chunk(act, c)
                            free_chunk(act.activation(dst[:, 2 * t2:2 * t2 + 2, n * PANEL:(n + 1) * PANEL],
                                                      bank[:, :].rearrange("p (t n) -> p t n", t=2), func), c)
                if b == "c":
                    act.wait_ge(S["c_abs"], 1)
                    step(act.activation(sm[:, 12:14, :], sm[:, 12:14, :], ACT.Exp, scale=-1.0))
                    act.activation(sm[:, 12:14, :], sm[:, 12:14, :], ACT.Ln, bias=1.0).then_inc(S["c_soft"], 1)
                us = [(hd, t) for hd in range(8 if b == "c" else 4) for t in range(TT)]
                B = b.upper()

                def exps(u):
                    un = UNIT[(B, u)]
                    e = un % 2
                    act.wait_ge(S["unit_max"], un + 1)
                    if b == "a":
                        for m in range(2):
                            v = EX[:, e, m, 0:(u[1] + 1) * P]
                            ins = act.activation(v, v, ACT.Exp, bias=mxs[:, e, m:m + 1], accum_out=rs[:, e, m:m + 1])
                    elif b == "b":
                        for g in range(2):
                            v = EX[:, e, 0, g * 256 + (P if u[1] == 0 else 0):(g + 1) * 256]
                            act.activation(v, v, ACT.Exp, bias=mxs[:, e, g:g + 1], accum_out=rs[:, e, g:g + 1])
                            hd = u[0] + 4 * g
                            ins = act.activation(rs[:, e, 2 + g:3 + g], row16[:, 1, hd:hd + 1], ACT.Exp,
                                                 bias=mxs[:, e, g:g + 1])
                    else:
                        v = EX[:, e, 0, 0:(u[1] + 1) * P]
                        ins = act.activation(v, v, ACT.Exp, bias=mxs[:, e, 0:1], accum_out=rs[:, e, 0:1])
                    ins.then_inc(S["unit_exp"], 1)

                def groups():
                    return [us] if b != "c" else [us[TT * i:TT * i + TT] for i in range(8)]

                for run in groups():
                    exps(run[0])
                    for n, u in enumerate(run):
                        if n + 1 < len(run):
                            exps(run[n + 1])
                        e = UNIT[(B, u)] % 2
                        bank = wait_aux(act, (B, "T", u, 0))
                        if b == "b":
                            lo = P if u[1] == 0 else 0
                            src = bank[:, :].rearrange("p (g n) -> p g n", g=2)[:, :, lo:]
                            dst = PT[:, e, :].rearrange("p (g n) -> p g n", g=2)[:, :, lo:]
                        else:
                            src, dst = bank[:, 0:(u[1] + 1) * P], PT[:, e, 0:(u[1] + 1) * P]
                        free_aux(act.activation(dst, src, ACT.Copy), (B, "T", u, 0))
                        if b == "a":
                            aux_read(act, "A", "PV", u)
                            hd, t = u
                            step(act.activation(PT[:, e, 0:P],
                                                YT[:, t, hd * P:(hd + 1) * P], ACT.Square, accum_out=rs[:, e, 2:3]))
                            step(act.activation(rs[:, e, 3:4], rs[:, e, 2:3], ACT.Ln, bias=cst[:, 0:1],
                                                scale=1.0 / P))
                            act.activation(rs[:, e, 3:4], rs[:, e, 3:4], ACT.Exp, scale=-0.5).then_inc(S["ya_rstd"], 1)
                for j in range(4):
                    bank = wait_aux(act, (B + "t", j))
                    operand_hi(y_hi[:, j, :], bank[:, :], y_hi_done, lam[:, 3:4] if b == "a" else 1.0)
                for half in range(2):
                    n0 = FIRST_PANEL[f"merge_{b}"] + 3 * half
                    for j in range(4):
                        split_to(n0 + j // 2 + 1)
                        c = CHUNK0[n0] + j
                        bank = wait_chunk(act, c)
                        if j == 0 and half and n_ == 0:
                            chunk_read(act, CHUNK0[n0 - 1] + 3)
                        elif j == 0 and half:
                            act.wait_ge(S["merged_ready"], KC * (n_ - 1) + 4)
                        free_chunk(act.activation(GATE[:, j, :], bank[:, :], ACT.Sigmoid), c)
                    split_to(n0 + 3)
            for k in range(KC):
                act.wait_ge(S["merged_ready"], KC + 4 * (k // 4 + 1))
                if k == 0:
                    act.wait_ge(chunk_done, stage_end_chunk("merge_c"))
                operand_hi(x_hi[:, k, :], MG[:, k, :], x_hi_done)
            residual_squares("w_o")
            normalised(lambda k: MG[:, k, :], lambda k: par_col("final_gain_2", k), None, eps=1, rms=True)
            for t in range(TT):
                for j in range(2):
                    bank = wait_aux(act, ("out", t, j))
                    free_aux(act.activation(area(0, TT, D)[:, t, 512 * j:512 * j + 512], bank[:, :], ACT.Copy),
                             ("out", t, j))
                aux_read(act, "out", t, 1)
                act.dma_start(out[t * P:(t + 1) * P, :], area(0, TT, D)[:, t, :]).then_inc(S["out_sent"], 16)
            act.wait_ge(S["out_sent"], 16 * TT)

        @block.vector
        def _(dve):
            at = dict(step=0, split=0, end=0, ln=0, sq=0, hr=0, xh=0, yh=0)

            def step(ins):
                at["step"] += 1
                ins.then_inc(dve_step, 1)
                dve.wait_ge(dve_step, at["step"])

            def stage_barrier():
                at["end"] += 1
                dve.drain().then_inc(stage_end, 1)
                dve.wait_ge(stage_end, 3 * at["end"])

            def split_chunk():
                s = at["split"]
                if s < 2 * NPANEL:
                    dve.wait_ge(w_hi_ready, s + 1)
                    half = slice((s % 2) * P, (s % 2 + 1) * P)
                    dve.tensor_tensor(w_lo[:, s % W_SLOTS, :, :], raw[:, s // 2 % RAW_SLOTS, :, half],
                                      w_hi[:, s % W_SLOTS, :, :].bitcast(F32), ALU.subtract).then_inc(w_lo_ready, 1)
                    at["split"] += 1

            def split_to(panel):
                while at["split"] < min(2 * panel + 2, 2 * NPANEL):
                    split_chunk()

            def operand(hi, lo, src, ready):
                step(dve.tensor_copy(hi, src))
                dve.tensor_tensor(lo, src, hi.bitcast(F32), ALU.subtract).then_inc(ready, 1)

            def operand_lo(hi, lo, src, hi_sem, which, scale=None):
                at[which] += 1
                dve.wait_ge(hi_sem, at[which])
                if scale is None:
                    return dve.tensor_tensor(lo, src, hi.bitcast(F32), ALU.subtract)
                return dve.scalar_tensor_tensor(lo, src, scale, hi.bitcast(F32), ALU.mult, ALU.subtract)

            def accumulate(k, src, mean=True):
                at["sq"] += 1
                dve.wait_ge(S["sq_ready"], at["sq"])
                sq = LN[:, k % 2, :]
                if k == 0:
                    if mean:
                        dve.tensor_copy(LN[:, 3, :], src)
                    ins = dve.tensor_copy(LN[:, 4, :], sq)
                else:
                    if mean:
                        dve.tensor_tensor(LN[:, 3, :], LN[:, 3, :], src, ALU.add)
                    ins = dve.tensor_tensor(LN[:, 4, :], LN[:, 4, :], sq, ALU.add)
                ins.then_inc(S["sum_in"], 1)
                dve.wait_ge(S["sum_in"], at["sq"])

            def normalise(name, src, finish, center=True):
                n = at["ln"]
                at["ln"] += 1
                if center:
                    bank = wait_aux(dve, ("ln", name, 0))
                    free_aux(dve.tensor_scalar(LN[:, 0, :], bank[:, :], 1.0 / D, None, ALU.mult), ("ln", name, 0))
                    aux_read(dve, "ln", name, 0)
                    step(dve.tensor_tensor(LN[:, 1, :], LN[:, 0, :], LN[:, 0, :], ALU.mult))
                    bank = wait_aux(dve, ("ln", name, 1))
                    free_aux(dve.scalar_tensor_tensor(LN[:, 1, :], bank[:, :], 1.0 / D, LN[:, 1, :], ALU.mult,
                                                      ALU.subtract), ("ln", name, 1))
                    aux_read(dve, "ln", name, 1)
                    dve.tensor_scalar(LN[:, 1, :], LN[:, 1, :], 0.0, None, ALU.max).then_inc(S["ln_var"], 1)
                else:
                    bank = wait_aux(dve, ("rms", name))
                    free_aux(dve.tensor_scalar(LN[:, 1, :], bank[:, :], 1.0 / D, None, ALU.mult), ("rms", name))
                    aux_read(dve, "rms", name)
                    dve.engine_nop().then_inc(S["ln_var"], 1)
                dve.wait_ge(S["ln_rstd"], n + 1)
                for k in range(KC + 1):
                    if k < KC:
                        xn = LN[:, 3 + k % 2, :]
                        if center:
                            step(dve.tensor_tensor(xn, src(k), LN[:, 0, :], ALU.subtract))
                            dve.tensor_tensor(xn, xn, LN[:, 2, :], ALU.mult).then_inc(S["ln_xn"], 1)
                        else:
                            dve.tensor_tensor(xn, src(k), LN[:, 2, :], ALU.mult).then_inc(S["ln_xn"], 1)
                    if k:
                        at["hr"] += 1
                        dve.wait_ge(S["h_ready"], at["hr"])
                        finish(k - 1)

            def to_x(k):
                operand(x_hi[:, k, :], x_lo[:, k, :], h[:, k, :], x_ready)

            def residual(stage, half=0, scale=None, sums=None):
                for k in range(KC):
                    n = FIRST_PANEL[stage] + half + k // 2
                    if k % 2 == 0:
                        split_to(n + 1)
                    c = CHUNK0[n] + k % 2
                    bank = wait_chunk(dve, c)
                    if scale is None:
                        free_chunk(dve.tensor_tensor(h[:, k, :], h[:, k, :], bank[:, :], ALU.add), c)
                    else:
                        free_chunk(dve.scalar_tensor_tensor(h[:, k, :], h[:, k, :], scale, bank[:, :], ALU.mult,
                                                            ALU.add), c)
                    if sums is not None:
                        if k:
                            accumulate(k - 1, h[:, k - 1, :], sums)
                        if k == KC - 1:
                            chunk_read(dve, c)
                            accumulate(k, h[:, k, :], sums)

            def spread(v, n):
                return v.unsqueeze(2).broadcast_to([P, v.shape[1], n])

            def over(v, n):
                return v.unsqueeze(1).broadcast_to([P, n, v.shape[1]])

            split_to(1)
            for k in range(KC):
                aux_read(dve, "x", k)
                to_x(k)
            stage_barrier()

            step(dve.memset(U[:, :, 0:CONV_W - 1], 0.0))
            step(dve.memset(XB[:, :, 0:SSM_W - 1], 0.0))
            bank = wait_aux(dve, ("dt",))
            soft = area(17940, TT, SH)
            dt = sm[:, 4:8, :]
            free_aux(dve.tensor_tensor(dt, bank[:, 0:TT * SH].rearrange("p (t n) -> p t n", n=SH),
                                       over(row16[:, 0, :], TT), ALU.add), ("dt",))
            aux_read(dve, "dt")
            dve.scalar_tensor_tensor(soft, dt, -1.0, dt, ALU.mult, ALU.max).then_inc(S["dt_abs"], 1)
            dve.wait_ge(S["dt_soft"], 1)
            step(dve.scalar_tensor_tensor(dt, dt, 0.0, soft, ALU.max, ALU.add))
            dve.scalar_tensor_tensor(sm[:, 0:4, :], dt, -1.0, over(row16[:, 1, :], TT), ALU.mult, ALU.mult)\
               .then_inc(S["dta_ready"], 1)
            for f in range(KC):
                split_to(f + 2)
                gate_chunk = 4 * (f // 2) + 2 + f % 2
                chunk_read(dve, gate_chunk)
                bank = wait_chunk(dve, gate_chunk - 2)
                free_chunk(dve.tensor_tensor(U[:, f, CONV_W - 1:], bank[:, :], TMP[:, f % 2, :], ALU.mult),
                           gate_chunk - 2)
            last_split = 2 * (FIRST_PANEL["z"] + 4)

            def taps(dst, src, width, weight, bias, last, every=0):
                step(dve.tensor_scalar(dst, src(0), weight(0), bias, ALU.mult, ALU.add))
                for i in range(1, width):
                    if every and i % every == 0 and at["split"] < last_split:
                        split_chunk()
                    out_ = dst if i < width - 1 else last[0]
                    ins = dve.scalar_tensor_tensor(out_, src(i), weight(i), dst, ALU.mult, ALU.add)
                    if i < width - 1:
                        step(ins)
                    else:
                        ins.then_inc(last[1], 1)

            for f in range(KC):
                if f == 0:
                    chunk_read(dve, stage_chunk("xbc") - 1 - 2)
                taps(TMP[:, 0, :], lambda i: U[:, f, i:i + T], CONV_W,
                     lambda i: par_col("even_conv_w", i * KC + f), par_col("even_conv_b", f),
                     (U[:, f, CONV_W - 1:], S["conv_sum"]), every=5)
                dve.wait_ge(S["conv_sum"], f + 1)
            split_to(FIRST_PANEL["z"] + 3)
            for j in range(XC):
                chunk_read(dve, stage_chunk("xbc") + j)
                if j >= 2:
                    dve.wait_ge(S["xbc_ready"], j - 1)
                taps(TMP[:, j % 2, :], lambda i: XB[:, j, i:i + T], SSM_W,
                     lambda i: par_col("even_ssm_conv_w", i * XC + j), par_col("even_ssm_conv_b", j),
                     (TMP[:, j % 2, :], S["xbc_conv"]))
            split_to(FIRST_PANEL["even_out_conv"])
            tri2 = over(triu[:, :], 2)
            cb = TMP[:, 0, 0:2 * P].rearrange("p (a b) -> p a b", b=P)
            for c in range(TT):
                tok = slice(c * P, (c + 1) * P)
                bank = wait_aux(dve, ("acs", c))
                free_aux(dve.tensor_copy(sm[:, 8, :], bank[:, 0:SH]), ("acs", c))
                aux_read(dve, "acs", c)
                dve.tensor_tensor(M, over(ident[:, :], SH), spread(sm[:, 8, :], P), ALU.mult)\
                   .then_inc(S["bcr_ready"], 1)
                for q in range(4):
                    bank = wait_aux(dve, ("bc", c, q))
                    rows = bank[:, :].rearrange("p (a b) -> p a b", b=P)
                    hs = slice(4 * q, 4 * q + 4)
                    dve.tensor_tensor(sm[:, 9, hs], rows[:, :, P - 1], sm[:, 8, hs], ALU.subtract)
                    dve.tensor_copy(sm[:, 10, hs], rows[:, :, P - 1])
                    for j in range(4):
                        hd = 4 * q + j
                        ins = dve.tensor_scalar(M[:, hd, :], rows[:, j, :], sm[:, 8, hd:hd + 1], 0.0, ALU.subtract,
                                                ALU.min)
                    free_aux(ins, ("bc", c, q))
                aux_read(dve, "bc", c, 3)
                dve.engine_nop().then_inc(S["seg_ready"], 1)
                if c == 0:
                    dve.wait_ge(S["xbc_ready"], XC)
                bank = wait_aux(dve, ("cb", c))
                free_aux(dve.tensor_tensor(cb, bank[:, 0:2 * P].rearrange("p (a b) -> p a b", b=P), tri2, ALU.mult),
                         ("cb", c))
                aux_read(dve, "cb", c)
                aux_read(dve, "bt", c)
                xs = XS.rearrange("p (a b) -> p a b", b=SP_)
                step(dve.tensor_tensor(XDT, xs, spread(sm[:, 4 + c, :], SP_), ALU.mult))
                dve.wait_ge(S["dte_ready"], c + 1)
                dve.tensor_tensor(XW, XDT, spread(sm[:, 9, :], SP_), ALU.mult).then_inc(S["xdt_ready"], 1)
                dve.wait_ge(S["decay_ready"], c + 1)
                for g in range(2):
                    m8 = M[:, 8 * g:8 * g + 8, :]
                    ins = dve.tensor_tensor(m8, m8, over(cb[:, g, :], 8), ALU.mult)
                ins.then_inc(S["m_ready"], 1)
                wait_aux(dve, ("yd", c, 1))
                skip = TMP.rearrange("p a b -> p (a b)").rearrange("p (a b) -> p a b", b=SP_)
                step(dve.tensor_tensor(skip, xs, spread(row16[:, 2, :], SP_), ALU.mult))
                for g in range(2):
                    y8 = XDT[:, 8 * g:8 * g + 8, :]
                    bank = wait_aux(dve, ("yd", c, g))
                    free_aux(dve.tensor_tensor(y8, bank[:, :].rearrange("p (a b) -> p a b", b=SP_),
                                               skip[:, 8 * g:8 * g + 8, :], ALU.add), ("yd", c, g))
                    if c:
                        bank = wait_aux(dve, ("yo", c, g))
                        aux_read(dve, "yd", c, g)
                        free_aux(dve.tensor_tensor(skip[:, 8 * g:8 * g + 8, :],
                                                   bank[:, :].rearrange("p (a b) -> p a b", b=SP_),
                                                   spread(sm[:, 11, 8 * g:8 * g + 8], SP_), ALU.mult), ("yo", c, g))
                if c:
                    aux_read(dve, "yo", c, 1)
                    step(dve.tensor_tensor(XDT, XDT, skip, ALU.add))
                else:
                    aux_read(dve, "yd", c, 1)
                if c == 0:
                    chunk_read(dve, stage_end_chunk("z") - 1)
                dve.tensor_tensor(XDT.rearrange("p a b -> p (a b)"), XDT.rearrange("p a b -> p (a b)"), Z[:, c, :],
                                  ALU.mult).then_inc(S["gated"], 1)
                st8 = ST.rearrange("p a b -> p (a b)").rearrange("p (a b) -> p a b", b=SP_)
                if c:
                    step(dve.tensor_tensor(st8, st8, spread(sm[:, 10, :], SP_), ALU.mult))
                for g in range(2):
                    bank = wait_aux(dve, ("st", c, g))
                    if c:
                        free_aux(dve.tensor_tensor(ST[:, g, :], ST[:, g, :], bank[:, :], ALU.add), ("st", c, g))
                    else:
                        free_aux(dve.tensor_copy(ST[:, g, :], bank[:, :]), ("st", c, g))
                aux_read(dve, "st", c, 1)
                dve.engine_nop().then_inc(S["state_ready"], 1)
                dve.wait_ge(S["ssm_rstd"], c + 1)
                dve.wait_ge(S["gated"], c + 1)
                for g in range(2):
                    y8 = XDT[:, 8 * g:8 * g + 8, :]
                    ins = dve.tensor_scalar(y8, y8, rs[:, 1, g:g + 1], None, ALU.mult)
                ins.then_inc(S["y_gated"], 1)
                for g in range(2):
                    bank = wait_aux(dve, ("yt", c, g))
                    at["xh"] += 1
                    dve.wait_ge(x_hi_done, at["xh"])
                    for j in range(4):
                        k = 4 * g + j
                        ins = dve.scalar_tensor_tensor(x_lo[:, k, tok], bank[:, j * P:(j + 1) * P],
                                                       par_col("even_ssm_norm_g", k), x_hi[:, k, tok].bitcast(F32),
                                                       ALU.mult, ALU.subtract)
                    free_aux(ins, ("yt", c, g))
            for k in range(KC):
                accumulate(k, U[:, k, CONV_W - 1:])
            normalise("conv", lambda k: U[:, k, CONV_W - 1:],
                      lambda k: operand(y_hi[:, k, :], y_lo[:, k, :], U[:, k, CONV_W - 1:], y_ready))
            dve.wait_ge(S["reloaded"], 16)
            residual("even_out_conv", scale=ALPHA)
            residual("even_out_ssm", sums=True)
            normalise("m0", lambda k: h[:, k, :], to_x)
            stage_barrier()

            def cross_attention(i):
                name = f"x{i}"
                for e in range(4):
                    bank = wait_aux(dve, ("mem", i, e))
                    s = slice(2 * e, 2 * e + 2)
                    free_aux(operand_lo(y_hi[:, s, 0:MEM], y_lo[:, s, 0:MEM],
                                        bank[:, :].rearrange("p (a b) -> p a b", a=2), y_hi_done, "yh"), ("mem", i, e))
                for stage in ("xk", "xv", "xq"):
                    for n in range(4):
                        split_to(FIRST_PANEL[f"{stage}{i}"] + n + 1)

                def maxima(t):
                    e2 = UNIT[(name, t)] % 2
                    for e in range(2):
                        bank = wait_aux(dve, (name, "S", t, e))
                        ins = dve.tensor_reduce(mxs[:, e2, 2 * e:2 * e + 2],
                                                bank[:, :].rearrange("p (a b) -> p a b", b=MEM), AX.X, ALU.max,
                                                negate=True)
                    ins.then_inc(S["unit_max"], 1)

                maxima(0)
                for t in range(TT):
                    if t + 1 < TT:
                        maxima(t + 1)
                    e2 = UNIT[(name, t)] % 2
                    aux_read(dve, name, "S", t, 1)
                    step(dve.reciprocal(rs[:, e2, :], rs[:, e2, :]))
                    pr = PR[:, t % 2, :].rearrange("p (a b) -> p a b", b=MEM)
                    dve.tensor_tensor(pr, pr, spread(rs[:, e2, :], MEM), ALU.mult).then_inc(S["p_ready"], 1)
                for j in range(KC):
                    bank = wait_aux(dve, ("xpv", i, j))
                    free_aux(operand_lo(x_hi[:, j, :], x_lo[:, j, :], bank[:, :], x_hi_done, "xh"), ("xpv", i, j))
                residual(f"xo{i}", scale=ALPHA, sums=True)
                normalise(f"a{i}", lambda k: h[:, k, :], to_x)
                stage_barrier()

            def mlp(i):
                st = f"mlp{i}"
                for q in range(4):
                    for k in range(KC):
                        split_to(FIRST_PANEL[st] + 8 * q + k // 2 + 1)
                        dve.wait_ge(S["hid_relu"], 32 * i + KC * q + k + 1)
                        operand(y_hi[:, k, :], y_lo[:, k, :], area(0, 2, T)[:, k % 2, :], y_ready)
                    residual(st, half=8 * q + 4, scale=ALPHA if q == 0 else None, sums=True if q == 3 else None)
                normalise(f"f{i}", lambda k: h[:, k, :], to_x if i == 0 else lambda k: None)
                stage_barrier()

            cross_attention(0)
            mlp(0)

            block_mask = area(18176, P)
            step(dve.memset(GA, 0.0))
            step(dve.tensor_copy(block_mask, triu[:, :]))
            step(dve.memset(block_mask[0:64, 64:128], 0.0))
            step(dve.memset(GMASK, 1.0))
            step(dve.memset(GMASK.rearrange("p (a b) -> p a b", b=64)[:, :, 0:1], 0.0))
            step(dve.memset(GQE, 0.0))
            step(dve.memset(GQO, 0.0))
            for stage in ("gla_qk", "gla_v", "gla_g"):
                for n in range(4):
                    split_to(FIRST_PANEL[stage] + n + 1)
            for hd in range(GH):
                bank = wait_aux(dve, ("gate", hd))
                free_aux(dve.tensor_scalar(GENB, bank[:, :], par_col("odd_b_gate", hd), None, ALU.add), ("gate", hd))
                aux_read(dve, "gate", hd)
                dve.scalar_tensor_tensor(GEB, GENB, -1.0, GENB, ALU.mult, ALU.max).then_inc(S["log_ready"], 1)
                dve.wait_ge(S["eb_ready"], 2 * hd + 1)
                step(dve.scalar_tensor_tensor(GENB, GENB, 0.0, GEB, ALU.min, ALU.subtract))
                step(dve.tensor_scalar(GENB, GENB, 1.0 / 16, None, ALU.mult))
                dve.tensor_tensor_scan(GB, GMASK, GENB, 0.0, ALU.mult, ALU.add).then_inc(S["b_ready"], 1)
                dve.wait_ge(S["eb_ready"], 2 * hd + 2)
                q = GQ[:, hd, :]
                step(dve.tensor_tensor(q, q, GEB, ALU.mult))
                for n, dst in enumerate((GQE, GQO)):
                    part = (lambda v: v.rearrange("p (t a b) -> p t a b", a=2, b=64)[:, :, n, :])
                    dve.tensor_copy(part(dst), part(q))
                dve.tensor_tensor(GENB, GK[:, hd, :], GENB, ALU.mult)
                step(dve.memset(GS, 0.0))
                dve.engine_nop().then_inc(S["s_ready"], 1)
                dve.tensor_tensor(GK[:, hd, :], GK[:, hd, :], GKT.rearrange("p a b -> p (a b)"), ALU.mult)\
                   .then_inc(S["qkt_ready"], 1)
                for t in range(TT):
                    u = TT * hd + t
                    bank = wait_aux(dve, ("gatt", hd, t))
                    free_aux(dve.copy_predicated(GA[:, u % 2, :], block_mask.bitcast(mybir.dt.uint32), bank[:, 0:P]),
                             ("gatt", hd, t))
                    kv = wait_aux(dve, ("gkv", hd, t, 0))
                    dve.wait_ge(S["s_read"], u + 1)
                    free_aux(dve.scalar_tensor_tensor(GS, GS, GEB[:, P * t + 63:P * t + 64], kv[:, 0:GV], ALU.mult,
                                                      ALU.add), ("gkv", hd, t, 0))
                    bank = wait_aux(dve, ("go", hd, t))
                    kv = wait_aux(dve, ("gkv", hd, t, 1))
                    aux_read(dve, "gkv", hd, t, 0)
                    free_aux(dve.scalar_tensor_tensor(GS, GS, GEB[:, P * t + 127:P * t + 128], kv[:, 0:GV],
                                                      ALU.mult, ALU.add), ("gkv", hd, t, 1))
                    free_aux(dve.tensor_copy(GY[:, t, :], bank[:, 0:GV]), ("go", hd, t))
                    dve.wait_ge(S["gla_rstd"], u + 1)
                    aux_read(dve, "go", hd, t)
                    ins = dve.scalar_tensor_tensor(GY[:, t, :], GY[:, t, :], rs[:, 1, 0:1],
                                                   GG[:, t, hd * GV:(hd + 1) * GV], ALU.mult, ALU.mult)
                ins.then_inc(S["o_ready"], 1)
                for j in range(2):
                    bank = wait_aux(dve, ("gt", hd, j))
                    k = 2 * hd + j
                    free_aux(operand_lo(x_hi[:, k, :], x_lo[:, k, :], bank[:, :], x_hi_done, "xh",
                                        par_col("odd_head_norm_g", j)), ("gt", hd, j))
            residual("odd_out", scale=ALPHA, sums=True)
            normalise("m1", lambda k: h[:, k, :], to_x)
            stage_barrier()
            cross_attention(1)
            mlp(1)

            dve.wait_ge(S["lam_loaded"], 16 * 6)
            lq = PT[:, 0, 0:256].rearrange("p (a b c) -> p a b c", a=2, b=2)
            prod = PT[:, 1, 0:128].rearrange("p (a b) -> p a b", a=2)
            step(dve.tensor_tensor(prod, lq[:, :, 0, :], lq[:, :, 1, :], ALU.mult))
            dve.tensor_reduce(lam[:, 0:2], prod, AX.X, ALU.add).then_inc(S["lam_sum"], 1)
            dve.wait_ge(S["lam_ready"], 1)
            step(dve.tensor_tensor(lam[:, 2:3], lam[:, 1:2], lam[:, 0:1], ALU.subtract))
            step(dve.tensor_scalar(lam[:, 2:3], lam[:, 2:3], -0.2, None, ALU.add))
            step(dve.tensor_scalar(lam[:, 3:4], par_col("subln_gain_2"), 0.8, None, ALU.mult))
            for k in range(KC):
                accumulate(k, None, False)

            def rms_lo(k):
                dve.scalar_tensor_tensor(x_lo[:, k, :], LN[:, 3 + k % 2, :], par_col("norm_gain_2", k),
                                         x_hi[:, k, :].bitcast(F32), ALU.mult, ALU.subtract).then_inc(x_ready, 1)
                dve.wait_ge(x_ready, KC * X_FILLS.index("rms") + k + 1)

            normalise(0, lambda k: h[:, k, :], rms_lo, center=False)
            dve.wait_ge(consts_ready, 2)
            for n_, b in enumerate("abc"):
                B = b.upper()
                for stage in (f"qk_{b}", f"kv_{b}", f"v_{b}", f"g_{b}"):
                    if stage in FIRST_PANEL:
                        for n in range(FIRST_PANEL[stage], len(PLAN)):
                            if PLAN[n][0] == stage:
                                split_to(n + 1)
                if b == "c":
                    bank = wait_aux(dve, ("fc",))
                    z = sm[:, 0:4, 0:8]
                    zabs = sm[:, 12:14, :].rearrange("p a b -> p (a b)").rearrange("p (a b) -> p a b", b=8)
                    free_aux(dve.tensor_tensor(z, bank[:, 0:32].rearrange("p (a b) -> p a b", b=8),
                                               over(row16[:, 0, 0:8], 4), ALU.add), ("fc",))
                    aux_read(dve, "fc")
                    dve.scalar_tensor_tensor(zabs, z, -1.0, z, ALU.mult, ALU.max).then_inc(S["c_abs"], 1)
                    dve.wait_ge(S["c_soft"], 1)
                    dve.scalar_tensor_tensor(z, z, 0.0, zabs, ALU.min, ALU.subtract).then_inc(S["log_ready"], 1)
                    bank = wait_aux(dve, ("cc",))
                    free_aux(dve.tensor_copy(sm[:, 4:8, 0:8], bank[:, 0:32].rearrange("p (a b) -> p a b", b=8)),
                             ("cc",))
                    aux_read(dve, "cc")
                    step(dve.tensor_scalar(R[:, 0:P], R[:, 384:512], NEG / 10, NEG, ALU.is_le, ALU.mult))

                def maxima(u):
                    e = UNIT[(B, u)] % 2
                    hd, t = u
                    n = (t + 1) * P
                    if b == "a":
                        for m in range(2):
                            bank = wait_aux(dve, ("A", "S", u, m))
                            free_aux(dve.scalar_tensor_tensor(EX[:, e, m, 0:n], R[:, 512 - n:512], 0.25 ** (hd + 1),
                                                              bank[:, 0:n], ALU.mult, ALU.add), ("A", "S", u, m))
                        aux_read(dve, "A", "S", u, 1)
                        ins = dve.tensor_reduce(mxs[:, e, 0:2], EX[:, e, :, 0:n], AX.X, ALU.max, negate=True)
                    elif b == "b":
                        off = P if t == 0 else 0
                        for g in range(2):
                            bank = wait_aux(dve, ("B", "S", u, g))
                            s = slice(g * 256 + off, (g + 1) * 256)
                            free_aux(dve.scalar_tensor_tensor(EX[:, e, 0, s], RB[:, off:256],
                                                              0.5 ** (hd + 4 * g + 1), bank[:, off:256],
                                                              ALU.mult, ALU.add), ("B", "S", u, g))
                        aux_read(dve, "B", "S", u, 1)
                        m = mxs[:, e, 0:2]
                        step(dve.tensor_reduce(m, EX[:, e, 0, :].rearrange("p (a b) -> p a b", a=2)[:, :, off:],
                                               AX.X, ALU.max))
                        step(dve.tensor_tensor(m, m, row16[:, 1, hd:hd + 5:4], ALU.max))
                        ins = dve.tensor_scalar(m, m, -1.0, None, ALU.mult)
                    else:
                        bank = wait_aux(dve, ("C", "S", u, 0))
                        free_aux(dve.scalar_tensor_tensor(EX[:, e, 0, 0:n], EX[:, 0, 1, 0:n], sm[:, 4 + t, hd:hd + 1],
                                                          bank[:, 0:n], ALU.add, ALU.add), ("C", "S", u, 0))
                        aux_read(dve, "C", "S", u, 0)
                        diag = EX[:, e, 0, n - P:n]
                        step(dve.tensor_tensor(diag, diag, R[:, 0:P], ALU.add))
                        ins = dve.tensor_reduce(mxs[:, e, 0:1], EX[:, e, 0, 0:n], AX.X, ALU.max, negate=True)
                    ins.then_inc(S["unit_max"], 1)

                def weights(u):
                    un = UNIT[(B, u)]
                    e = un % 2
                    hd, t = u
                    n = (t + 1) * P
                    dve.wait_ge(S["unit_exp"], un - 2 * TT + 1)
                    if b == "a":
                        step(dve.reciprocal(rs[:, e, 0:2], rs[:, e, 0:2]))
                        step(dve.tensor_tensor(rs[:, e, 1:2], rs[:, e, 1:2], lam[:, 2:3], ALU.mult))
                        step(dve.tensor_scalar(EX[:, e, 0, 0:n], EX[:, e, 0, 0:n], rs[:, e, 0:1], None, ALU.mult))
                        ins = dve.scalar_tensor_tensor(EX[:, e, 0, 0:n], EX[:, e, 1, 0:n], rs[:, e, 1:2],
                                                       EX[:, e, 0, 0:n], ALU.mult, ALU.add)
                    elif b == "b":
                        off = P if t == 0 else 0
                        step(dve.tensor_tensor(rs[:, e, 0:2], rs[:, e, 0:2], rs[:, e, 2:4], ALU.add))
                        step(dve.reciprocal(rs[:, e, 0:2], rs[:, e, 0:2]))
                        for g in range(2):
                            v = EX[:, e, 0, g * 256 + off:(g + 1) * 256]
                            ins = dve.tensor_scalar(v, v, rs[:, e, g:g + 1], None, ALU.mult)
                    else:
                        step(dve.reciprocal(rs[:, e, 0:1], rs[:, e, 0:1]))
                        ins = dve.tensor_scalar(EX[:, e, 0, 0:n], EX[:, e, 0, 0:n], rs[:, e, 0:1], None, ALU.mult)
                    ins.then_inc(S["p_ready"], 1)

                def values(u, last):
                    hd, t = u
                    e = UNIT[(B, u)] % 2
                    bank = wait_aux(dve, (B, "PV", u))
                    if b == "a":
                        y = YT[:, t, hd * P:(hd + 1) * P]
                        free_aux(dve.tensor_copy(y, bank[:, 0:P]), ("A", "PV", u))
                        aux_read(dve, "A", "PV", u)
                        dve.wait_ge(S["ya_rstd"], UNIT[("A", u)] - UNIT[("A", (0, 0))] + 1)
                        ins = dve.scalar_tensor_tensor(y, y, rs[:, e, 3:4], BG[:, t, hd * P:(hd + 1) * P],
                                                       ALU.mult, ALU.mult)
                        if last:
                            ins.then_inc(S["y_tm_ready"], 1)
                        return
                    if b == "b":
                        heads = (lambda v: v[:, t, :].rearrange("p (g j d) -> p g j d", g=2, d=64)[:, :, hd, :])
                        ins = dve.tensor_tensor(heads(YT), bank[:, 0:P].rearrange("p (g d) -> p g d", g=2), heads(BG),
                                                ALU.mult)
                    else:
                        s = slice(64 * hd, 64 * hd + 64)
                        ins = dve.tensor_tensor(YT[:, t, s], bank[:, 0:64], BG[:, t, s], ALU.mult)
                    free_aux(ins, (B, "PV", u))
                    if last:
                        aux_read(dve, B, "PV", u)
                        dve.engine_nop().then_inc(S["y_tm_ready"], 1)

                us = [(hd, t) for hd in range(8 if b == "c" else 4) for t in range(TT)]
                for run in ([us] if b != "c" else [us[TT * i:TT * i + TT] for i in range(8)]):
                    if b == "c":
                        hd = run[0][0]
                        dve.tensor_tensor(NC.rearrange("p (a b) -> p a b", b=P), over(ident[:, :], TT),
                                          spread(sm[:, 4:8, hd], P), ALU.mult).then_inc(S["c_rhs"], 1)
                        bank = wait_aux(dve, ("cb_c", hd))
                        free_aux(dve.tensor_scalar(EX[:, 0, 1, :], bank[:, :], -1.0, None, ALU.mult), ("cb_c", hd))
                        aux_read(dve, "cb_c", hd)
                    maxima(run[0])
                    for n, u in enumerate(run):
                        if n + 1 < len(run):
                            maxima(run[n + 1])
                        weights(u)
                        values(u, u == us[-1])
                for j in range(4):
                    bank = wait_aux(dve, (B + "t", j))
                    free_aux(operand_lo(y_hi[:, j, :], y_lo[:, j, :], bank[:, :], y_hi_done, "yh",
                                        lam[:, 3:4] if b == "a" else None), (B + "t", j))
                for half in range(2):
                    n0 = FIRST_PANEL[f"merge_{b}"] + 3 * half
                    split_to(n0 + 3)
                    chunk_read(dve, CHUNK0[n0] + 3)
                    for i, f in enumerate((0, 2, 1, 3)):
                        c = CHUNK0[n0 + 2] + i
                        bank = wait_chunk(dve, c)
                        m = MG[:, 4 * half + f, :]
                        if n_ == 0:
                            free_chunk(dve.tensor_tensor(m, bank[:, :], GATE[:, f, :], ALU.mult), c)
                        else:
                            free_chunk(dve.tensor_tensor(GATE[:, f, :], bank[:, :], GATE[:, f, :], ALU.mult), c)
                            chunk_read(dve, c)
                            dve.tensor_tensor(m, m, GATE[:, f, :], ALU.add).then_inc(S["merged_ready"], 1)
            for k in range(KC):
                operand_lo(x_hi[:, k, :], x_lo[:, k, :], MG[:, k, :], x_hi_done, "xh").then_inc(x_ready, 1)
            residual("w_o", sums=False)
            normalise(1, lambda k: h[:, k, :], lambda k: None, center=False)


def build_program(nc, shapes):
    t = {n: nc.dram_tensor(f"in_{n}_dram", s, F32, kind="ExternalInput").ap() for n, s in shapes}
    out = nc.dram_tensor("out_0_dram", (1, T, D), F32, kind="ExternalOutput").ap()
    w = {}
    for n, a in t.items():
        if n.startswith(("xa_w", "mlp_w")):
            for i in range(2):
                w[f"{n}{i}"] = a[i]
        elif n in ("ln_g", "ln_b", "final_gain_2"):
            w[n] = a
        else:
            w[n] = a[0]
    build(nc, w, out[0])


def kernel(**inputs):
    import numpy as _np
    import concourse.bacc as _bacc
    from concourse.bass_utils import run_bass_kernel_spmd as _run

    nc = _bacc.Bacc("TRN2", target_bir_lowering=False, num_devices=1)
    arrays = {f"in_{n}_dram": _np.ascontiguousarray(a) for n, a in inputs.items()}
    build_program(nc, [(n, a.shape) for n, a in inputs.items()])
    r = _run(nc, [arrays], core_ids=[0])
    return r.results[0]["out_0_dram"]
```

```python
from contextlib import ExitStack

import concourse.bass as bass
from concourse import mybir

F32 = mybir.dt.float32
F32R = mybir.dt.float32r
ALU = mybir.AluOpType
ACT = mybir.ActivationFunctionType
AX = mybir.AxisListType

P = 128
T = 512
TT = T // P
D = 1024
KC = D // P
PANEL = 256
LN_EPS = 1e-5
RMS_EPS = 1e-6
ALPHA = 4.0 ** 0.25
NEG = -1.0e30

CONV_W = 31
SSM_W = 4
SH = 16
SP_ = 64
XBC = 1536
XC = XBC // P

MEM = 256
XH = 4
GH = 4
GV = 256

RAW_SLOTS = 2
W_SLOTS = 4
LEAD = 3

FM, TM, TM_MEM, FM_MEM, UP = "fm", "tm", "tm_mem", "fm_mem", "up"


def weight_plan():
    plan = []

    def add(stage, weight, row, cols, kind):
        for c in cols:
            plan.append((stage, weight, row, c, kind))

    add("xbc", "even_w_in", 0, range(3 * D, 3 * D + XBC, PANEL), FM)
    for j in range(4):
        add("conv_in", "even_w_in", 0, [j * PANEL, D + j * PANEL], FM)
    add("z", "even_w_in", 0, range(2 * D, 3 * D, PANEL), TM)
    add("even_out_ssm", "even_w_out", D, range(0, D, PANEL), FM)
    add("even_out_conv", "even_w_out", 0, range(0, D, PANEL), FM)

    def attention(i):
        add(f"xk{i}", f"xa_w_k{i}", 0, range(0, D, PANEL), FM_MEM)
        add(f"xv{i}", f"xa_w_v{i}", 0, range(0, D, PANEL), TM_MEM)
        add(f"xq{i}", f"xa_w_q{i}", 0, range(0, D, PANEL), FM)
        add(f"xo{i}", f"xa_w_o{i}", 0, range(0, D, PANEL), FM)

    def mlp(i):
        for q in range(4):
            add(f"mlp{i}", f"mlp_w1{i}", 0, range(q * D, (q + 1) * D, PANEL), FM)
            add(f"mlp{i}", f"mlp_w2{i}", q * D, range(0, D, PANEL), FM)

    attention(0)
    mlp(0)
    add("gla_qk", "odd_w_in", 0, range(0, D, PANEL), FM)
    add("gla_v", "odd_w_in", 0, range(D, 2 * D, PANEL), TM)
    add("gla_g", "odd_w_in", 0, range(2 * D, 3 * D, PANEL), TM)
    add("odd_out", "odd_w_out", 0, range(0, D, PANEL), FM)
    attention(1)
    mlp(1)
    base = dict(a=0, b=2048, c=3328, gm=5384)
    for n, b in enumerate("abc"):
        if b == "b":
            add("qk_b", "w_in_2q", 0, [base["b"], base["b"] + PANEL], FM)
            add("kv_b", "w_in_2", 0, [base["b"] + 512], "kv")
            add("g_b", "w_in_2", 0, [base["b"] + 768, base["b"] + 1024], TM)
        else:
            add(f"qk_{b}", "w_in_2", 0, range(base[b], base[b] + D, PANEL), FM)
            add(f"v_{b}", "w_in_2", 0, range(base[b] + D, base[b] + D + 512, PANEL), TM)
            g = base[b] + D + 512 + (8 if b == "c" else 0)
            add(f"g_{b}", "w_in_2", 0, range(g, g + 512, PANEL), TM)
        g = base["gm"] + n * D
        add(f"gm_{b}", "w_in_2", 0, range(g, g + D, PANEL), FM)
        add(f"up_{b}", f"w_up_{b}_2", 0, [0, 512], UP)
    add("w_o", "w_o_2", 0, range(0, D, PANEL), FM)
    return plan


PLAN = weight_plan()
NPANEL = len(PLAN)
FIRST_PANEL = {}
for _n, _p in enumerate(PLAN):
    FIRST_PANEL.setdefault(_p[0], _n)
CHUNKS = {FM: 2, TM: 2, FM_MEM: 2, TM_MEM: 1, UP: 4, "kv": 2}
PE_CONV = 3
DVE_CONV = KC - PE_CONV
CHUNK0, _c = [], 0
for _n, _p in enumerate(PLAN):
    if _n == FIRST_PANEL["even_out_ssm"]:
        CONV_CHUNK = _c
        _c += PE_CONV
    CHUNK0.append(_c)
    _c += CHUNKS[_p[4]]


def stage_chunk(name):
    return CHUNK0[FIRST_PANEL[name]]


def aux_plan():
    e = [("par", i) for i in range(4)] + [("x", k) for k in range(KC)] + [("dt",)]
    e += [("acs", 0)] + [("bc", 0, q) for q in range(4)]
    for c in range(TT):
        e += [("cb", c), ("xs", c, 0), ("xs", c, 1), ("bt", c)] + ([("acs", c + 1)] if c + 1 < TT else [])
        for g in range(2):
            e += [("yd", c, g)] + ([("yo", c, g)] if c else [])
        e += [("st", c, g) for g in range(2)]
        e += [("bc", c + 1, q) for q in range(4)] if c + 1 < TT else []
        e += [("yt", c, g) for g in range(2)]
    e += [("ln", "conv", i) for i in range(2)]

    def ln(name):
        return [("ln", name, i) for i in range(2)]

    def attention(i):
        out = [("mem", i, j) for j in range(4)]
        out += units("x" + str(i), range(TT), 2, 2)
        return out + [("xpv", i, j) for j in range(KC)]

    def units(name, us, ns, nt, pv=False):
        us = list(us)
        out = [(name, "S", us[0], j) for j in range(ns)]
        for n, u in enumerate(us):
            if name == "C" and u[1] == 1 and u[0] + 1 < 8:
                out += [("cb_c", u[0] + 1)]
            if n + 1 < len(us):
                out += [(name, "S", us[n + 1], j) for j in range(ns)]
            out += [(name, "T", u, j) for j in range(nt)]
            if pv:
                out += [(name, "PV", u)]
        return out

    e += ln("m0") + attention(0) + ln("a0") + ln("f0")
    e += [("glow",)]
    for hd in range(GH):
        e += [("gate", hd), ("kend", hd)]
        for t in range(TT):
            e += [("gatt", hd, t), ("gkv", hd, t, 0), ("gkv", hd, t, 1), ("go", hd, t)]
        e += [("gt", hd, j) for j in range(2)]
    e += ln("m1") + attention(1) + ln("a1") + ln("f1")
    e += [("rms", 0)]
    e += units("A", [(hd, t) for hd in range(4) for t in range(TT)], 2, 1, True) + [("At", j) for j in range(4)]
    e += units("B", [(hd, t) for hd in range(4) for t in range(TT)], 2, 1, True) + [("Bt", j) for j in range(4)]
    e += [("fc",), ("cc",), ("cb_c", 0)]
    e += units("C", [(hd, t) for hd in range(8) for t in range(TT)], 1, 1, True) + [("Ct", j) for j in range(4)]
    e += [("rms", 1)] + [("out", t, j) for t in range(TT) for j in range(2)]
    return e


AUX_PLAN = aux_plan()
AUX = {key: n for n, key in enumerate(AUX_PLAN)}
assert len(AUX) == len(AUX_PLAN)

UNITS = ([("x0", t) for t in range(TT)] + [("x1", t) for t in range(TT)]
         + [("A", (hd, t)) for hd in range(4) for t in range(TT)]
         + [("B", (hd, t)) for hd in range(4) for t in range(TT)]
         + [("C", (hd, t)) for hd in range(8) for t in range(TT)])
UNIT = {key: n for n, key in enumerate(UNITS)}

X_FILLS = ["x", "m0", "a0", "f0", "m1", "a1", "rms", "merged"]
PARAMS = [(0, "ln_g", 48), (0, "ln_b", 48),
          (1, "even_conv_ln_g", 8), (1, "even_conv_ln_b", 8), (1, "even_conv_b", 8), (1, "even_ssm_conv_b", 12),
          (1, "even_ssm_norm_g", 8), (1, "odd_b_gate", 4), (1, "odd_head_norm_g", 2), (1, "norm_gain_2", 8),
          (1, "final_gain_2", 8), (1, "subln_gain_2", 1), (1, "even_ssm_conv_w", 48),
          (2, "even_conv_w", 124), (3, "even_conv_w", 124)]
PAR_AT, _rows = {}, [0, 0, 0, 0]
for _g, _name, _n in PARAMS:
    PAR_AT.setdefault(_name, (_g, _rows[_g]))
    _rows[_g] += _n
PAR_ROWS = _rows


def stage_end_chunk(name):
    last = max(n for n, p in enumerate(PLAN) if p[0] == name)
    return CHUNK0[last] + CHUNKS[PLAN[last][4]]

UP_ORDER = [4 * half + f for half in range(2) for f in (0, 2, 1, 3)]

Y_FILLS = [("conv", 8)] + [(f"hid{i}{q}", 8) for i in range(2) for q in range(4)]
Y0, _y = {}, 0
for _name, _n in Y_FILLS:
    Y0[_name] = _y
    _y += _n

GEMM_BANKS = 4
AUX_BANKS = 4
FIRST_TAPS = 42
PE_TAPS = -(-(PE_CONV * CONV_W - FIRST_TAPS) // (2 * TT))


def build(nc, w, out):
    with ExitStack() as ctx:
        sems = {}

        def sb(name, shape, dt=F32):
            return ctx.enter_context(nc.sbuf_tensor(name, shape, dt))

        def sem(name):
            sems[name] = ctx.enter_context(nc.semaphore(name))
            return sems[name]

        raw = sb("raw", [P, RAW_SLOTS, KC, PANEL])
        w_hi = sb("w_hi", [P, W_SLOTS, KC, P], F32R)
        w_lo = sb("w_lo", [P, W_SLOTS, KC, P], F32R)
        x_hi = sb("x_hi", [P, KC, T], F32R)
        x_lo = sb("x_lo", [P, KC, T], F32R)
        y_hi = sb("y_hi", [P, KC, T], F32R)
        y_lo = sb("y_lo", [P, KC, T], F32R)
        h = sb("h", [P, KC, T])
        WN = 18432
        work = sb("work", [P, WN])
        par = sb("par", [P, sum(PAR_ROWS)])
        ident = sb("ident", [P, P])
        triu = sb("triu", [P, P])
        ones = sb("ones", [P, P])
        w_small = sb("w_small", [P, KC, 16])
        row16 = sb("row16", [P, 3, SH])
        cst = sb("cst", [P, 4])
        mxs = sb("mxs", [P, 2, 4])
        rs = sb("rs", [P, 2, 4])
        sm = sb("sm", [P, 16, SH])
        gate2 = sb("gate2", [16, 512])
        lam = sb("lam", [P, 8])

        psum = [ctx.enter_context(nc.psum_tensor(f"gemm{i}", [P, 512], F32)) for i in range(GEMM_BANKS)]
        paux = [ctx.enter_context(nc.psum_tensor(f"aux{i}", [P, 512], F32)) for i in range(AUX_BANKS)]
        h_spill = nc.dram_tensor("h_spill", [P, KC * T], F32, kind="Internal").ap()

        raw_loaded = [sem(f"raw_loaded{i}") for i in range(RAW_SLOTS)]
        w_hi_ready, w_lo_ready = sem("w_hi_ready"), sem("w_lo_ready")
        chunk_done = sem("chunk_done")
        chunk_free = [sem(f"chunk_free{i}") for i in range(GEMM_BANKS)]
        aux_done = sem("aux_done")
        aux_free = [sem(f"aux_free{i}") for i in range(AUX_BANKS)]
        x_ready, y_ready = sem("x_ready"), sem("y_ready")
        x_hi_done, y_hi_done = sem("x_hi_done"), sem("y_hi_done")
        act_step, dve_step, pool_step = sem("act_step"), sem("dve_step"), sem("pool_step")
        stage_end = sem("stage_end")
        consts_ready = sem("consts_ready")
        names = ("par_loaded x_loaded small_loaded rows_loaded spilled reloaded mem_loaded lam_loaded out_sent "
                 "dt_abs dt_soft dta_ready bcr_ready seg_ready dte_ready decay_ready m_ready xdt_ready state_ready "
                 "conv_sum xbc_conv xbc_ready gated ssm_rstd y_gated sq_ready sum_in ln_var ln_rstd ln_xn "
                 "diag_ready tap_done h_ready ln_hi hid_relu unit_max unit_exp p_ready log_ready b_ready eb_ready qkt_ready s_ready s_read "
                 "gla_rstd o_ready lam_sum lam_ready ya_rstd gate_ready y_tm_ready c_abs c_soft c_rhs merged_ready").split()
        S = {n: sem(n) for n in names}

        block = ctx.enter_context(nc.Block())

        def area(at, *shape):
            n = 1
            for s in shape:
                n *= s
            v = work[:, at:at + n]
            if len(shape) == 2:
                v = v.rearrange("p (a b) -> p a b", b=shape[1])
            elif len(shape) == 3:
                v = v.rearrange("p (a b c) -> p a b c", b=shape[1], c=shape[2])
            return v

        x_in = area(4336, TT, D)
        par_in = area(0, 4, P)
        U = area(0, KC, T + CONV_W - 1)
        XB = area(4336, XC, T + SSM_W - 1)
        TMP = area(10516, 2, T)
        CV = area(12820, 2, T)
        SG = area(13844, 2, T)
        DIAG = area(18040, 3, P)
        XS = area(11540, D)
        BT = area(12564, 2, P)
        M = area(12820, SH, P)
        XDT = area(14868, SH, SP_)
        XW = area(15892, SH, SP_)
        ST = area(16916, 2, T)
        LN = area(14848, 5, T)
        Z = h[:, :, :].rearrange("p a b -> p (a b)").rearrange("p (t n) -> p t n", n=D)
        XQ = area(0, KC, T)
        KT = area(4096, KC, MEM)
        VM = area(6144, 2, D)
        PR = area(8192, 2, XH * MEM)
        PTX = area(10240, 2, XH, T)
        mem_in = area(10240, 2, D)
        GQ = area(0, 4, T)
        GK = area(2048, 4, T)
        GVV = area(4096, TT, D)
        GG = area(8192, TT, D)
        GB, GEB, GENB = area(12288, T), area(12800, T), area(13312, T)
        GQE, GQO, GKT = area(13824, T), area(14336, T), area(14848, TT, P)
        GY = area(15360, TT, GV)
        GS = area(16384, GV)
        GA = area(16640, 2, P)
        GL = area(16896, T)
        GMASK = area(17408, T)
        QK = area(0, KC, T)
        BV = area(4096, TT, T)
        BG = area(6144, TT, T)
        MG = area(8192, KC, T)
        LAMB = area(8192, 3 * P)
        YT = area(12288, TT, T)
        EX = area(14336, 2, 2, T)
        PT = area(16384, 2, T)
        GATE = h
        NC = area(17408, T)
        RB = area(17408, 2 * P)
        R = area(17920, T)

        def par_col(name, i=0):
            g, r = PAR_AT[name]
            at = sum(PAR_ROWS[:g]) + r + i
            return par[:, at:at + 1]

        def raw_value(n):
            return 16 * sum(2 if PLAN[m][4] == UP else 4 if PLAN[m][1] == "w_in_2q" else 1
                            for m in range(n % RAW_SLOTS, n + 1, RAW_SLOTS))

        def chunk_end(n):
            return CHUNK0[n] + CHUNKS[PLAN[n][4]]

        def wait_chunk(eng, c):
            eng.wait_ge(chunk_done, c + 1)
            return psum[c % GEMM_BANKS]

        def wait_aux(eng, key):
            eng.wait_ge(aux_done, AUX[key] + 1)
            return paux[AUX[key] % AUX_BANKS]

        def chunk_read(eng, c):
            eng.wait_ge(chunk_free[c % GEMM_BANKS], c // GEMM_BANKS + 1)

        def aux_read(eng, *key):
            eng.wait_ge(aux_free[AUX[key] % AUX_BANKS], AUX[key] // AUX_BANKS + 1)

        def wait_tap(eng, n):
            if n % CONV_W == CONV_W - 1:
                eng.wait_ge(chunk_done, CONV_CHUNK + n // CONV_W + 1)
            else:
                eng.wait_ge(S["tap_done"], n - n // CONV_W + 1)

        def free_chunk(ins, c):
            ins.then_inc(chunk_free[c % GEMM_BANKS], 1)

        def free_aux(ins, key):
            ins.then_inc(aux_free[AUX[key] % AUX_BANKS], 1)

        @block.sync
        def _(sp):
            def load(n):
                stage, name, row, col, kind = PLAN[n]
                s = n % RAW_SLOTS
                if n >= RAW_SLOTS:
                    sp.wait_ge(w_lo_ready, 2 * (n - RAW_SLOTS + 1))
                if kind == UP:
                    src = w[name][0:512, col:col + 512].rearrange("(k p) n -> p k n", p=P)
                    for half in range(2):
                        sp.dma_start(raw[:, s, 4 * half:4 * half + 4, :],
                                     src[:, :, half * PANEL:(half + 1) * PANEL]).then_inc(raw_loaded[s], 16)
                    return
                if name == "w_in_2q":
                    a = (col - 2048) // PANEL
                    src = w["w_in_2"][0:D, 2048:2560].rearrange("(k p) (g j d) -> p k j g d", p=P, g=2, d=64)
                    dst = raw[:, s, :, :].rearrange("p k (j g d) -> p k j g d", g=2, d=64)
                    for j in range(2):
                        for g in range(2):
                            ins = sp.dma_start(dst[:, :, j, g, :], src[:, :, 2 * a + j, g, :])
                            ins.then_inc(raw_loaded[s], 16)
                    return
                src = w[name][row:row + D, col:col + PANEL].rearrange("(k p) n -> p k n", p=P)
                sp.dma_start(raw[:, s, :, :], src).then_inc(raw_loaded[s], 16)

            for n in range(NPANEL):
                load(n)

        @block.gpsimd
        def _(pool):
            steps = [0]

            def step(ins):
                steps[0] += 1
                ins.then_inc(pool_step, 1)
                pool.wait_ge(pool_step, steps[0])

            pool.memset(ones[:, :], 1.0)
            pool.memset(cst[:, 0:1], LN_EPS)
            pool.memset(cst[:, 1:2], RMS_EPS)
            pool.memset(ident[:, :], 0.0)
            step(pool.memset(triu[:, :], 1.0))
            step(pool.affine_select(out=ident[:, :], in_=ident[:, :], compare_op=ALU.not_equal, fill=1.0, base=0,
                                    pattern=[[-1, P]], channel_multiplier=1))
            step(pool.affine_select(out=triu[:, :], in_=triu[:, :], compare_op=ALU.is_ge, fill=0.0, base=0,
                                    pattern=[[1, P]], channel_multiplier=-1))
            pool.drain().then_inc(consts_ready, 1)
            aux_read(pool, "par", 3)
            for n in range(PE_CONV * CONV_W):
                f, i = DVE_CONV + n // CONV_W, n % CONV_W
                if n >= 3:
                    wait_tap(pool, n - 3)
                pool.tensor_scalar(DIAG[:, n % 3, :], ident[:, :], par_col("even_conv_w", i * KC + f), None, ALU.mult)\
                    .then_inc(S["diag_ready"], 1)
            pool.wait_ge(S["o_ready"], GH)
            step(pool.iota(R, [[1, T]], base=-384, channel_multiplier=-1, allow_small_or_imprecise_dtypes=True))
            step(pool.affine_select(out=R, in_=R, compare_op=ALU.is_ge, fill=NEG, base=384,
                                    pattern=[[-1, T]], channel_multiplier=1))
            step(pool.tensor_copy(RB, R[:, 256:512]))
            step(pool.affine_select(out=RB[:, 0:P], in_=RB[:, 0:P], compare_op=ALU.is_ge, fill=NEG, base=-1,
                                    pattern=[[1, P]], channel_multiplier=-1))
            pool.drain().then_inc(consts_ready, 1)

        @block.tensor
        def _(pe):
            at = dict(panel=0, chunk=0, aux=0, end=0, tap=0, conv=None, gate=0, dst=None)

            def stage_barrier():
                at["end"] += 1
                pe.drain().then_inc(stage_end, 1)
                pe.wait_ge(stage_end, 3 * at["end"])

            def next_chunk():
                c = at["chunk"]
                if c >= GEMM_BANKS:
                    pe.wait_ge(chunk_free[c % GEMM_BANKS], c // GEMM_BANKS)
                at["chunk"] += 1
                return psum[c % GEMM_BANKS]

            def next_aux(*key):
                a = at["aux"]
                assert AUX_PLAN[a] == key, (AUX_PLAN[a], key)
                if a >= AUX_BANKS:
                    pe.wait_ge(aux_free[a % AUX_BANKS], a // AUX_BANKS)
                at["aux"] += 1
                return paux[a % AUX_BANKS]

            def w_ready(upto):
                pe.wait_ge(w_lo_ready, upto)

            def product3(dst, a_hi, a_lo, b_hi, b_lo, first, last):
                pe.matmul(dst, a_hi, b_hi, start=first, stop=False)
                pe.matmul(dst, a_hi, b_lo, start=False, stop=False)
                return pe.matmul(dst, a_lo, b_hi, start=False, stop=last)

            def gemm(stage, hi, lo, ready=None, panels=None, wide=False):
                n0 = at["panel"]
                n1 = n0 + panels if panels else n0 + sum(1 for p in PLAN if p[0] == stage)
                seen = [0]

                def operand(k):
                    if ready is not None and k >= seen[0]:
                        ready(k)
                        seen[0] = k + 1

                if wide:
                    w_ready(2 * n0 + 4)
                    dst = [next_chunk() for _ in range(4)]
                    for k in range(KC):
                        operand(k)
                        for i in range(4):
                            s = (2 * n0 + i) % W_SLOTS
                            ins = product3(dst[i][:, :], w_hi[:, s, k, :], w_lo[:, s, k, :], hi[:, k, :], lo[:, k, :],
                                           k == 0, k == KC - 1)
                            if k == KC - 1:
                                ins.then_inc(chunk_done, 1)
                for n in range(n0 + 2 if wide else n0, n1):
                    kind = PLAN[n][4]
                    assert PLAN[n][0] == stage
                    if kind in (FM, FM_MEM):
                        cols = T if kind == FM else MEM
                        for s in (2 * n, 2 * n + 1):
                            w_ready(s + 1)
                            dst = next_chunk()
                            for k in range(KC):
                                operand(k)
                                ins = product3(dst[:, 0:cols], w_hi[:, s % W_SLOTS, k, :], w_lo[:, s % W_SLOTS, k, :],
                                               hi[:, k, 0:cols], lo[:, k, 0:cols], k == 0, k == KC - 1)
                            ins.then_inc(chunk_done, 1)
                    elif kind in (TM, TM_MEM):
                        w_ready(2 * n + 2)
                        a = 2 * n % W_SLOTS
                        for t2 in range(2 if kind == TM else 1):
                            dst = next_chunk()
                            for t in range(2):
                                tok = slice((2 * t2 + t) * P, (2 * t2 + t + 1) * P)
                                for k in range(KC):
                                    operand(k)
                                    ins = product3(dst[:, t * PANEL:(t + 1) * PANEL], hi[:, k, tok], lo[:, k, tok],
                                                   w_hi[:, a:a + 2, k, :], w_lo[:, a:a + 2, k, :],
                                                   k == 0, k == KC - 1)
                            ins.then_inc(chunk_done, 1)
                    elif kind == UP:
                        for s in (2 * n, 2 * n + 1):
                            w_ready(s + 1)
                            for half in range(2):
                                dst = next_chunk()
                                for k in range(4):
                                    operand(k)
                                    kk = 4 * half + k
                                    ins = product3(dst[:, :], w_hi[:, s % W_SLOTS, kk, :], w_lo[:, s % W_SLOTS, kk, :],
                                                   hi[:, k, :], lo[:, k, :], k == 0, k == 3)
                                ins.then_inc(chunk_done, 1)
                    else:
                        w_ready(2 * n + 2)
                        a = 2 * n % W_SLOTS
                        dst = next_chunk()
                        for k in range(KC):
                            ins = product3(dst[:, :], w_hi[:, a, k, :], w_lo[:, a, k, :], hi[:, k, :], lo[:, k, :],
                                           k == 0, k == KC - 1)
                        ins.then_inc(chunk_done, 1)
                        dst = next_chunk()
                        for t in range(TT):
                            tok = slice(t * P, (t + 1) * P)
                            for k in range(KC):
                                ins = product3(dst[:, tok], hi[:, k, tok], lo[:, k, tok], w_hi[:, a + 1, k, :],
                                               w_lo[:, a + 1, k, :], k == 0, k == KC - 1)
                        ins.then_inc(chunk_done, 1)
                at["panel"] = n1

            def turn(dst, src):
                return pe.transpose(dst, src, ident[0:src.shape[0], 0:src.shape[0]])

            def layer_sums(name, n):
                pe.wait_ge(S["sum_in"], KC * (n + 1))
                for i in range(2):
                    pe.matmul(next_aux("ln", name, i)[:, :], ones[:, :], LN[:, 3 + i, :], start=True, stop=True)\
                      .then_inc(aux_done, 1)

            def x_fill(name):
                return dict(ready=lambda k: pe.wait_ge(x_ready, KC * X_FILLS.index(name) + k + 1))

            def y_fill(name):
                return dict(ready=lambda k: pe.wait_ge(y_ready, Y0[name] + k + 1))

            pe.wait_ge(consts_ready, 1)
            pe.wait_ge(S["par_loaded"], 16 * len(PARAMS))
            for g in range(4):
                turn(next_aux("par", g)[:, 0:PAR_ROWS[g]], par_in[0:PAR_ROWS[g], g, :]).then_inc(aux_done, 1)
            pe.wait_ge(S["x_loaded"], 16)
            for k in range(KC):
                dst = next_aux("x", k)
                for t in range(TT):
                    ins = turn(dst[:, t * P:(t + 1) * P], x_in[:, t, k * P:(k + 1) * P])
                ins.then_inc(aux_done, 1)
            stage_barrier()

            pe.wait_ge(S["small_loaded"], 16)
            dst = next_aux("dt")
            for t in range(TT):
                for k in range(KC):
                    ins = pe.matmul(dst[:, SH * t:SH * (t + 1)], h[:, k, t * P:(t + 1) * P], w_small[:, k, :],
                                    start=(k == 0), stop=(k == KC - 1))
            ins.then_inc(aux_done, 1)
            gemm("xbc", x_hi, x_lo, **x_fill("x"))
            gemm("conv_in", x_hi, x_lo)
            gemm("z", x_hi, x_lo)

            def convolve(upto):
                while at["tap"] < min(upto, PE_CONV * CONV_W):
                    n = at["tap"]
                    f, i = DVE_CONV + n // CONV_W, n % CONV_W
                    if i == 0:
                        at["conv"] = next_chunk()
                        chunk_read(pe, stage_chunk("conv_in") + 4 * (f // 2) + f % 2)
                    pe.wait_ge(S["diag_ready"], n + 1)
                    ins = pe.matmul(at["conv"][:, :], DIAG[:, n % 3, :], U[:, f, i:i + T], start=(i == 0),
                                    stop=(i == CONV_W - 1))
                    ins.then_inc(chunk_done if i == CONV_W - 1 else S["tap_done"], 1)
                    at["tap"] += 1

            def running_sums(c):
                pe.wait_ge(S["dta_ready"], 1)
                pe.matmul(next_aux("acs", c)[:, 0:SH], triu[:, :], sm[:, c, :], start=True, stop=True)\
                  .then_inc(aux_done, 1)

            def sums_as_rows(c):
                pe.wait_ge(S["bcr_ready"], c + 1)
                for q in range(4):
                    pe.matmul(next_aux("bc", c, q)[:, :], ones[:, :], M[:, 4 * q:4 * q + 4, :], start=True, stop=True)\
                      .then_inc(aux_done, 1)

            convolve(FIRST_TAPS)
            running_sums(0)
            sums_as_rows(0)
            for c in range(TT):
                tok = slice(SSM_W - 1 + c * P, SSM_W - 1 + (c + 1) * P)
                if c == 0:
                    pe.wait_ge(S["xbc_ready"], XC)
                dst = next_aux("cb", c)
                for g in range(2):
                    ins = pe.matmul(dst[:, g * P:(g + 1) * P], XB[:, 8 + g, tok], XB[:, 10 + g, tok],
                                    start=True, stop=True)
                ins.then_inc(aux_done, 1)
                for half in range(2):
                    dst = next_aux("xs", c, half)
                    for j in range(4):
                        ins = turn(dst[:, j * P:(j + 1) * P], XB[:, 4 * half + j, tok])
                    ins.then_inc(aux_done, 1)
                dst = next_aux("bt", c)
                for g in range(2):
                    ins = turn(dst[:, g * P:(g + 1) * P], XB[:, 8 + g, tok])
                ins.then_inc(aux_done, 1)
                if c + 1 < TT:
                    running_sums(c + 1)
                convolve(at["tap"] + PE_TAPS)
                pe.wait_ge(S["m_ready"], c + 1)
                pe.wait_ge(S["xdt_ready"], c + 1)
                aux_read(pe, "bt", c)
                if c:
                    pe.wait_ge(S["state_ready"], c)
                for g in range(2):
                    dst = next_aux("yd", c, g)
                    for j in range(8):
                        ins = pe.matmul(dst[:, 64 * j:64 * j + 64], M[:, 8 * g + j, :], XDT[:, 8 * g + j, :],
                                        start=True, stop=True)
                    ins.then_inc(aux_done, 1)
                    if c:
                        pe.matmul(next_aux("yo", c, g)[:, :], XB[:, 10 + g, tok], ST[:, g, :], start=True, stop=True)\
                          .then_inc(aux_done, 1)
                for g in range(2):
                    pe.matmul(next_aux("st", c, g)[:, :], BT[:, g, :], XW[:, 8 * g:8 * g + 8, :],
                              start=True, stop=True).then_inc(aux_done, 1)
                if c + 1 < TT:
                    sums_as_rows(c + 1)
                convolve(at["tap"] + PE_TAPS)
                pe.wait_ge(S["y_gated"], c + 1)
                yv = XDT.rearrange("p a b -> p (a b)")
                for g in range(2):
                    dst = next_aux("yt", c, g)
                    for j in range(4):
                        ins = turn(dst[:, j * P:(j + 1) * P], yv[:, (4 * g + j) * P:(4 * g + j + 1) * P])
                    ins.then_inc(aux_done, 1)
            gemm("even_out_ssm", x_hi, x_lo, panels=2, ready=lambda k: aux_read(pe, "yt", TT - 1, k // 4))
            layer_sums("conv", 0)
            gemm("even_out_ssm", x_hi, x_lo, panels=2)
            gemm("even_out_conv", y_hi, y_lo, **y_fill("conv"))
            layer_sums("m0", 1)

            def cross_attention(i):
                pe.wait_ge(S["mem_loaded"], 16 * (i + 1))
                for e in range(4):
                    dst = next_aux("mem", i, e)
                    for kk in range(2):
                        for t in range(2):
                            k = 2 * e + kk
                            ins = turn(dst[:, kk * MEM + t * P:kk * MEM + (t + 1) * P], mem_in[:, t, k * P:(k + 1) * P])
                    ins.then_inc(aux_done, 1)
                gemm(f"xk{i}", y_hi, y_lo, ready=lambda k: aux_read(pe, "mem", i, k // 2))
                gemm(f"xv{i}", y_hi, y_lo)
                gemm(f"xq{i}", x_hi, x_lo, **x_fill(f"m{i}"))
                chunk_read(pe, stage_end_chunk(f"xq{i}") - 1)
                name = f"x{i}"

                def scores(t):
                    for e in range(2):
                        dst = next_aux(name, "S", t, e)
                        for hh in range(2):
                            for d in range(2):
                                k = 2 * (2 * e + hh) + d
                                ins = pe.matmul(dst[:, hh * MEM:(hh + 1) * MEM], XQ[:, k, t * P:(t + 1) * P],
                                                KT[:, k, :], start=(d == 0), stop=(d == 1))
                        ins.then_inc(aux_done, 1)

                scores(0)
                for t in range(TT):
                    if t + 1 < TT:
                        scores(t + 1)
                    pe.wait_ge(S["p_ready"], UNIT[(name, t)] + 1)
                    for m in range(2):
                        dst = next_aux(name, "T", t, m)
                        for hd in range(XH):
                            ins = turn(dst[:, hd * P:(hd + 1) * P],
                                       PR[:, t % 2, hd * MEM + m * P:hd * MEM + (m + 1) * P])
                        ins.then_inc(aux_done, 1)
                aux_read(pe, name, "T", TT - 1, 1)
                for j in range(KC):
                    dst = next_aux("xpv", i, j)
                    for m in range(2):
                        ins = pe.matmul(dst[:, :], VM[:, m, j * P:(j + 1) * P], PTX[:, m, j // 2, :],
                                        start=(m == 0), stop=(m == 1))
                    ins.then_inc(aux_done, 1)
                gemm(f"xo{i}", x_hi, x_lo, ready=lambda k: aux_read(pe, "xpv", i, k))
                layer_sums(f"a{i}", 2 + 3 * i)

            def mlp(i):
                for q in range(4):
                    gemm(f"mlp{i}", x_hi, x_lo, panels=4, wide=(q == 0), **x_fill(f"a{i}"))
                    gemm(f"mlp{i}", y_hi, y_lo, panels=4, **y_fill(f"hid{i}{q}"))
                layer_sums(f"f{i}", 3 + 3 * i)

            cross_attention(0)
            mlp(0)

            pe.wait_ge(S["small_loaded"], 32)
            gemm("gla_qk", x_hi, x_lo, wide=True, **x_fill("f0"))
            dst = next_aux("glow")
            for k in range(KC):
                ins = pe.matmul(dst[0:16, :], w_small[:, k, :], h[:, k, :], start=(k == 0), stop=(k == KC - 1))
            ins.then_inc(aux_done, 1)
            gemm("gla_v", x_hi, x_lo)
            gemm("gla_g", x_hi, x_lo)
            aux_read(pe, "glow")
            chunk_read(pe, stage_end_chunk("gla_g") - 1)
            for hd in range(GH):
                pe.matmul(next_aux("gate", hd)[:, :], gate2[:, hd * P:(hd + 1) * P], GL[0:16, :],
                          start=True, stop=True).then_inc(aux_done, 1)
                pe.wait_ge(S["qkt_ready"], hd + 1)
                dst = next_aux("kend", hd)
                for t in range(TT):
                    ins = turn(dst[:, t * P:(t + 1) * P], GK[:, hd, t * P:(t + 1) * P])
                ins.then_inc(aux_done, 1)
                for t in range(TT):
                    tok = slice(t * P, (t + 1) * P)
                    vt = GVV[:, t, hd * GV:(hd + 1) * GV]
                    u = TT * hd + t
                    pe.matmul(next_aux("gatt", hd, t)[:, 0:P], GENB[:, tok], GQ[:, hd, tok], start=True, stop=True)\
                      .then_inc(aux_done, 1)
                    if t == 0:
                        aux_read(pe, "kend", hd)
                    for half in range(2):
                        a, b = 64 * half, 64 * half + 64
                        pe.matmul(next_aux("gkv", hd, t, half)[:, 0:GV], GKT[a:b, t, :], vt[a:b, :],
                                  start=True, stop=True).then_inc(aux_done, 1)
                    aux_read(pe, "gatt", hd, t)
                    dst = next_aux("go", hd, t)
                    pe.matmul(dst[:, 0:GV], GA[:, u % 2, :], vt, start=True, stop=False)
                    if t == 0:
                        pe.wait_ge(S["s_ready"], hd + 1)
                    else:
                        aux_read(pe, "gkv", hd, t - 1, 1)
                    pe.matmul(dst[:, 0:GV], GQE[:, tok], GS, start=False, stop=False).then_inc(S["s_read"], 1)
                    aux_read(pe, "gkv", hd, t, 0)
                    pe.matmul(dst[:, 0:GV], GQO[:, tok], GS, start=False, stop=True).then_inc(aux_done, 1)
                pe.wait_ge(S["o_ready"], hd + 1)
                for j in range(2):
                    dst = next_aux("gt", hd, j)
                    for t in range(TT):
                        ins = turn(dst[:, t * P:(t + 1) * P], GY[:, t, j * P:(j + 1) * P])
                    ins.then_inc(aux_done, 1)
            gemm("odd_out", x_hi, x_lo, ready=lambda k: aux_read(pe, "gt", k // 2, k % 2))
            layer_sums("m1", 4)
            cross_attention(1)
            mlp(1)

            def square_sum(i):
                pe.wait_ge(S["sum_in"], KC * (7 + i + 1))
                pe.matmul(next_aux("rms", i)[:, :], ones[:, :], LN[:, 4, :], start=True, stop=True)\
                  .then_inc(aux_done, 1)

            def gate_products(b, upto):
                while at["gate"] < upto:
                    f, k = at["gate"] // KC, at["gate"] % KC
                    s = 2 * FIRST_PANEL[f"gm_{b}"] + f
                    if k == 0:
                        w_ready(s + 1)
                        at["dst"] = next_chunk()
                    ins = product3(at["dst"][:, :], w_hi[:, s % W_SLOTS, k, :], w_lo[:, s % W_SLOTS, k, :],
                                   x_hi[:, k, :], x_lo[:, k, :], k == 0, k == KC - 1)
                    if k == KC - 1:
                        ins.then_inc(chunk_done, 1)
                    at["gate"] += 1

            def units(b, us, scores, turns, values, before=lambda u: None):
                name = b.upper()
                at["gate"] = 0
                scores(us[0])
                for n, u in enumerate(us):
                    before(u)
                    if n + 1 < len(us):
                        scores(us[n + 1])
                    gate_products(b, KC * KC * (n + 1) // len(us))
                    if b == "a":
                        pe.wait_ge(S["p_ready"], UNIT[(name, u)] + 1)
                    else:
                        pe.wait_ge(S["unit_exp"], UNIT[(name, u)] - 2 * TT + 1)
                    turns(u, next_aux(name, "T", u, 0)).then_inc(aux_done, 1)
                    aux_read(pe, name, "T", u, 0)
                    values(u, next_aux(name, "PV", u)).then_inc(aux_done, 1)
                at["panel"] += 4

            def turned_output(name, b, n):
                pe.wait_ge(S["y_tm_ready"], n + 1)
                for j in range(4):
                    dst = next_aux(name, j)
                    for t in range(TT):
                        ins = turn(dst[:, t * P:(t + 1) * P], YT[:, t, j * P:(j + 1) * P])
                    ins.then_inc(aux_done, 1)
                gemm(f"up_{b}", y_hi, y_lo, ready=lambda k: aux_read(pe, name, k))

            square_sum(0)
            gemm("qk_a", x_hi, x_lo, wide=True, **x_fill("rms"))
            gemm("v_a", x_hi, x_lo)
            gemm("g_a", x_hi, x_lo)
            chunk_read(pe, stage_end_chunk("g_a") - 1)

            def scores_a(u):
                hd, t = u
                for m in range(2):
                    a = 64 * m
                    pe.matmul(next_aux("A", "S", u, m)[:, 0:(t + 1) * P], QK[a:a + 64, hd, t * P:(t + 1) * P],
                              QK[a:a + 64, 4 + hd, 0:(t + 1) * P], start=True, stop=True).then_inc(aux_done, 1)

            def turns_a(u, dst):
                e = UNIT[("A", u)] % 2
                for kt in range(u[1] + 1):
                    ins = turn(dst[:, kt * P:(kt + 1) * P], EX[:, e, 0, kt * P:(kt + 1) * P])
                return ins

            def values_a(u, dst):
                hd, t = u
                e = UNIT[("A", u)] % 2
                for kt in range(t + 1):
                    ins = pe.matmul(dst[:, 0:P], PT[:, e, kt * P:(kt + 1) * P], BV[:, kt, hd * P:(hd + 1) * P],
                                    start=(kt == 0), stop=(kt == t))
                return ins

            units("a", [(hd, t) for hd in range(4) for t in range(TT)], scores_a, turns_a, values_a)
            turned_output("At", "a", 0)

            gemm("qk_b", x_hi, x_lo)
            gemm("kv_b", x_hi, x_lo)
            gemm("g_b", x_hi, x_lo)
            chunk_read(pe, stage_end_chunk("g_b") - 1)

            def scores_b(u):
                j, t = u
                for g in range(2):
                    a = 64 * g
                    lo_key = max(t - 1, 0) * P
                    off = P if t == 0 else 0
                    pe.matmul(next_aux("B", "S", u, g)[:, off:256], QK[a:a + 64, j, t * P:(t + 1) * P],
                              QK[a:a + 64, 4, lo_key:(t + 1) * P], start=True, stop=True).then_inc(aux_done, 1)

            def turns_b(u, dst):
                e = UNIT[("B", u)] % 2
                for g in range(2):
                    for kk in range(1 if u[1] == 0 else 0, 2):
                        s = slice(g * 256 + kk * P, g * 256 + (kk + 1) * P)
                        ins = turn(dst[:, s], EX[:, e, 0, s])
                return ins

            def values_b(u, dst):
                j, t = u
                e = UNIT[("B", u)] % 2
                for g in range(2):
                    for kk in range(1 if t == 0 else 0, 2):
                        s = slice(g * 256 + kk * P, g * 256 + (kk + 1) * P)
                        ins = pe.matmul(dst[:, g * 64:(g + 1) * 64], PT[:, e, s],
                                        BV[:, t - 1 + kk, g * 64:(g + 1) * 64],
                                        start=(kk == (1 if t == 0 else 0)), stop=(kk == 1))
                return ins

            units("b", [(hd, t) for hd in range(4) for t in range(TT)], scores_b, turns_b, values_b)
            turned_output("Bt", "b", 1)

            gemm("qk_c", x_hi, x_lo)
            gemm("v_c", x_hi, x_lo)
            pe.wait_ge(S["small_loaded"], 48)
            dst = next_aux("fc")
            for t in range(TT):
                for k in range(KC):
                    for part in range(2):
                        xx = (x_hi, x_lo)[part][:, k, t * P:(t + 1) * P].bitcast(F32)
                        ins = pe.matmul(dst[:, 8 * t:8 * t + 8], xx, w_small[:, k, 0:8],
                                        start=(k == 0 and part == 0), stop=(k == KC - 1 and part == 1))
            ins.then_inc(aux_done, 1)
            gemm("g_c", x_hi, x_lo)
            chunk_read(pe, stage_end_chunk("g_c") - 1)
            pe.wait_ge(S["log_ready"], GH + 1)
            dst = next_aux("cc")
            for t in range(TT):
                for s in range(t + 1):
                    ins = pe.matmul(dst[:, 8 * t:8 * t + 8], (triu if s == t else ones)[:, :], sm[:, s, 0:8],
                                    start=(s == 0), stop=(s == t))
            ins.then_inc(aux_done, 1)

            def scores_c(u):
                hd, t = u
                a = 64 * (hd % 2)
                pe.matmul(next_aux("C", "S", u, 0)[:, 0:(t + 1) * P], QK[a:a + 64, hd // 2, t * P:(t + 1) * P],
                          QK[a:a + 64, 4 + hd // 2, 0:(t + 1) * P], start=True, stop=True).then_inc(aux_done, 1)

            def turns_c(u, dst):
                e = UNIT[("C", u)] % 2
                for kt in range(u[1] + 1):
                    ins = turn(dst[:, kt * P:(kt + 1) * P], EX[:, e, 0, kt * P:(kt + 1) * P])
                return ins

            def values_c(u, dst):
                hd, t = u
                e = UNIT[("C", u)] % 2
                for kt in range(t + 1):
                    ins = pe.matmul(dst[:, 0:64], PT[:, e, kt * P:(kt + 1) * P], BV[:, kt, hd * 64:(hd + 1) * 64],
                                    start=(kt == 0), stop=(kt == t))
                return ins

            def key_sums(hd):
                pe.wait_ge(S["c_rhs"], hd + 1)
                pe.matmul(next_aux("cb_c", hd)[:, :], ones[:, :], NC, start=True, stop=True).then_inc(aux_done, 1)

            def next_key_sums(u):
                if u[1] == 1 and u[0] + 1 < 8:
                    key_sums(u[0] + 1)

            key_sums(0)
            units("c", [(hd, t) for hd in range(8) for t in range(TT)], scores_c, turns_c, values_c, next_key_sums)
            turned_output("Ct", "c", 2)
            gemm("w_o", x_hi, x_lo, wide=True, ready=lambda k: pe.wait_ge(x_ready, KC * X_FILLS.index("merged") +
                                                                         UP_ORDER.index(k) + 1))
            square_sum(1)
            pe.wait_ge(S["h_ready"], KC * 9)
            for t in range(TT):
                for j in range(2):
                    dst = next_aux("out", t, j)
                    for k in range(4):
                        ins = turn(dst[:, k * P:(k + 1) * P], MG[:, 4 * j + k, t * P:(t + 1) * P])
                    ins.then_inc(aux_done, 1)
            assert at["panel"] == NPANEL and at["aux"] == len(AUX_PLAN)

        @block.scalar
        def _(act):
            at = dict(step=0, split=0, end=0, ln=0, sq=0, hr=0, xh=0, yh=0)

            def step(ins):
                at["step"] += 1
                ins.then_inc(act_step, 1)
                act.wait_ge(act_step, at["step"])

            def stage_barrier():
                at["end"] += 1
                act.drain().then_inc(stage_end, 1)
                act.wait_ge(stage_end, 3 * at["end"])

            def split_chunk():
                s = at["split"]
                if s < 2 * NPANEL:
                    n = s // 2
                    act.wait_ge(raw_loaded[n % RAW_SLOTS], raw_value(n))
                    if s >= W_SLOTS:
                        done = (s - W_SLOTS) // 2
                        if PLAN[done][4] in (FM, FM_MEM):
                            act.wait_ge(chunk_done, CHUNK0[done] + (s % 2) + 1)
                        else:
                            act.wait_ge(chunk_done, chunk_end(done))
                    act.activation(w_hi[:, s % W_SLOTS, :, :], raw[:, n % RAW_SLOTS, :, (s % 2) * P:(s % 2 + 1) * P],
                                   ACT.Copy).then_inc(w_hi_ready, 1)
                    at["split"] += 1

            def split_to(panel):
                while at["split"] < min(2 * panel + 2, 2 * NPANEL):
                    split_chunk()

            def split_more():
                split_to(at["split"] // 2)

            def split_chunks(upto):
                while at["split"] < upto:
                    split_chunk()

            def operand_hi(dst, src, done, scale=1.0):
                act.activation(dst, src, ACT.Identity, scale=scale).then_inc(done, 1)

            def squares(src, waits):
                for k in range(KC):
                    waits(k)
                    if at["sq"] % KC >= 2:
                        act.wait_ge(S["sum_in"], at["sq"] - 1)
                    act.activation(LN[:, k % 2, :], src(k), ACT.Square).then_inc(S["sq_ready"], 1)
                    at["sq"] += 1

            def logs():
                act.preload_act_table_set("natural_log_exp_and_others")

            def normalised(dst, gain, bias, func=ACT.Identity, eps=0, rms=False, hi=None, more=True):
                n = at["ln"]
                if more:
                    split_more()
                logs()
                act.wait_ge(S["ln_var"], n + 1)
                step(act.activation(LN[:, 2, :], LN[:, 1, :], ACT.Ln, bias=cst[:, eps:eps + 1]))
                act.activation(LN[:, 2, :], LN[:, 2, :], ACT.Exp, scale=-0.5).then_inc(S["ln_rstd"], 1)
                at["ln"] += 1
                for k in range(KC):
                    act.wait_ge(S["ln_xn"], KC * n + k + 1)
                    if rms:
                        act.activation(dst(k), LN[:, 3 + k % 2, :], func, scale=gain(k)).then_inc(S["h_ready"], 1)
                    else:
                        act.activation(dst(k), LN[:, 3 + k % 2, :], func, bias=bias(k), scale=gain(k))\
                           .then_inc(S["h_ready"], 1)
                    if hi is not None and k:
                        act.wait_ge(S["h_ready"], KC * n + k)
                        act.activation(hi[:, k - 1, :], dst(k - 1), ACT.Copy).then_inc(S["ln_hi"], 1)
                if hi is not None:
                    act.wait_ge(S["h_ready"], KC * (n + 1))
                    act.activation(hi[:, KC - 1, :], dst(KC - 1), ACT.Copy).then_inc(S["ln_hi"], 1)

            def residual_squares(stage, half=0, panels=4):
                def waits(k):
                    n = FIRST_PANEL[stage] + half + k // 2
                    if k % 2 == 0:
                        split_to(n + 1)
                    chunk_read(act, CHUNK0[n] + k % 2)
                squares(lambda k: h[:, k, :], waits)

            def ln_cols(i, j):
                r = (3 * i + j) * KC
                return (lambda k: par_col("ln_g", r + k)), (lambda k: par_col("ln_b", r + k))

            def layer_norm(i, j):
                g, b = ln_cols(i, j)
                normalised(lambda k: h[:, k, :], g, b, hi=None if (i, j) == (1, 2) else x_hi, more=(i, j) != (1, 2))

            count = [0, 0, 0, 0]
            for g, name, n in PARAMS:
                src = w[name]
                if name == "even_conv_w":
                    src = src.rearrange("w (c p) -> (w c) p", p=P)
                    src = src[0:124, :] if g == 2 else src[124:248, :]
                elif name == "even_ssm_conv_w":
                    src = src.rearrange("w (c p) -> (w c) p", p=P)
                elif name in ("ln_g", "ln_b"):
                    src = src.rearrange("i j (c p) -> (i j c) p", p=P)
                else:
                    src = src.rearrange("(c p) -> c p", p=P)
                act.dma_start(par_in[count[g]:count[g] + n, g, :], src).then_inc(S["par_loaded"], 16)
                count[g] += n
            act.dma_start(x_in, w["x"].rearrange("(t p) n -> p t n", p=P)).then_inc(S["x_loaded"], 16)
            act.dma_start(w_small[:, :, :], w["even_w_in"][:, 4608:4624].rearrange("(k p) n -> p k n", p=P))\
               .then_inc(S["small_loaded"], 16)
            for i, name in enumerate(("even_dt_bias", "even_a_log", "even_d_skip")):
                act.dma_start(row16[:, i, :], w[name].unsqueeze(0).broadcast_to([P, SH])).then_inc(S["rows_loaded"], 16)
            act.dma_start(gate2[:, :], w["odd_w_gate2"]).then_inc(S["rows_loaded"], 16)
            split_to(1)
            for g in range(4):
                bank = wait_aux(act, ("par", g))
                r = sum(PAR_ROWS[:g])
                free_aux(act.activation(par[:, r:r + PAR_ROWS[g]], bank[:, 0:PAR_ROWS[g]], ACT.Copy), ("par", g))
            for k in range(KC):
                bank = wait_aux(act, ("x", k))
                free_aux(act.activation(h[:, k, :], bank[:, :], ACT.Copy), ("x", k))
            act.wait_ge(S["rows_loaded"], 64)
            step(act.activation(row16[:, 1, :], row16[:, 1, :], ACT.Exp))
            stage_barrier()

            act.dma_start(h_spill, h[:, :, :].rearrange("p a b -> p (a b)")).then_inc(S["spilled"], 16)
            act.wait_ge(S["dt_abs"], 1)
            step(act.activation(work[:, 17940:18004], work[:, 17940:18004], ACT.Exp, scale=-1.0))
            act.activation(work[:, 17940:18004], work[:, 17940:18004], ACT.Ln, bias=1.0).then_inc(S["dt_soft"], 1)
            def xbc_silu(j):
                act.wait_ge(S["xbc_conv"], j + 1)
                act.activation(XB[:, j, SSM_W - 1:], TMP[:, j % 2, :], ACT.Silu).then_inc(S["xbc_ready"], 1)

            for j in range(XC):
                if j % 2 == 0:
                    split_to(FIRST_PANEL["xbc"] + j // 2 + 1)
                c = stage_chunk("xbc") + j
                bank = wait_chunk(act, c)
                free_chunk(act.activation(XB[:, j, SSM_W - 1:], bank[:, :], ACT.Copy), c)
                if j:
                    xbc_silu(j - 1)
            xbc_silu(XC - 1)
            for f in range(KC):
                split_to(FIRST_PANEL["conv_in"] + f + 2)
                c = stage_chunk("conv_in") + 4 * (f // 2) + 2 + f % 2
                bank = wait_chunk(act, c)
                if f >= 2:
                    chunk_read(act, stage_chunk("conv_in") + 4 * ((f - 2) // 2) + f % 2)
                free_chunk(act.activation(SG[:, f % 2, :], bank[:, :], ACT.Sigmoid), c)
            act.wait_ge(S["spilled"], 16)
            for n in range(4):
                split_to(FIRST_PANEL["z"] + n + 1)
                for t2 in range(2):
                    c = stage_chunk("z") + 2 * n + t2
                    bank = wait_chunk(act, c)
                    free_chunk(act.activation(Z[:, 2 * t2:2 * t2 + 2, n * PANEL:(n + 1) * PANEL],
                                              bank[:, :].rearrange("p (t n) -> p t n", t=2), ACT.Silu), c)
            logs()

            def decays(c):
                act.wait_ge(S["seg_ready"], c + 1)
                r = 8 + 4 * (c % 2)
                act.activation(sm[:, r + 1:r + 3, :], sm[:, r + 1:r + 3, :], ACT.Exp)
                act.activation(sm[:, r + 3, :], sm[:, r, :], ACT.Exp).then_inc(S["dte_ready"], 1)
                act.activation(M, M, ACT.Exp).then_inc(S["decay_ready"], 1)

            decays(0)
            for c in range(TT):
                tok = slice(c * P, (c + 1) * P)
                for half in range(2):
                    bank = wait_aux(act, ("xs", c, half))
                    free_aux(act.activation(XS[:, half * 512:(half + 1) * 512], bank[:, :], ACT.Copy), ("xs", c, half))
                bank = wait_aux(act, ("bt", c))
                free_aux(act.activation(BT.rearrange("p a b -> p (a b)"), bank[:, 0:256], ACT.Copy), ("bt", c))
                act.wait_ge(S["gated"], c + 1)
                for g in range(2):
                    ins = act.activation(XS[:, 512 * g:512 * g + 512],
                                         XDT[:, 8 * g:8 * g + 8, :].rearrange("p a b -> p (a b)"),
                                         ACT.Square, accum_out=rs[:, 0, g:g + 1])
                step(ins)
                step(act.activation(rs[:, 1, 0:2], rs[:, 0, 0:2], ACT.Ln, bias=cst[:, 0:1], scale=1.0 / 512))
                act.activation(rs[:, 1, 0:2], rs[:, 1, 0:2], ACT.Exp, scale=-0.5).then_inc(S["ssm_rstd"], 1)
                if c + 1 < TT:
                    decays(c + 1)
                for g in range(2):
                    bank = wait_aux(act, ("yt", c, g))
                    for j in range(4):
                        ins = act.activation(x_hi[:, 4 * g + j, tok], bank[:, j * P:(j + 1) * P], ACT.Identity,
                                             scale=par_col("even_ssm_norm_g", 4 * g + j))
                    ins.then_inc(x_hi_done, 1)
            split_to(FIRST_PANEL["even_out_ssm"] + 1)
            act.wait_ge(S["gated"], TT)
            act.dma_start(h[:, :, :].rearrange("p a b -> p (a b)"), h_spill).then_inc(S["reloaded"], 16)
            for f in range(DVE_CONV, KC):
                c = CONV_CHUNK + f - DVE_CONV
                bank = wait_chunk(act, c)
                free_chunk(act.activation(U[:, f, CONV_W - 1:], bank[:, :], ACT.Identity,
                                          bias=par_col("even_conv_b", f)), c)
            squares(lambda k: U[:, k, CONV_W - 1:],
                    lambda k: act.wait_ge(S["conv_sum"], k + 1) if k < DVE_CONV
                    else chunk_read(act, CONV_CHUNK + k - DVE_CONV))
            split_to(FIRST_PANEL["even_out_ssm"] + 2)
            normalised(lambda k: U[:, k, CONV_W - 1:], lambda k: par_col("even_conv_ln_g", k),
                       lambda k: par_col("even_conv_ln_b", k), ACT.Silu, hi=y_hi)
            for n in range(4):
                split_to(FIRST_PANEL["even_out_ssm"] + n + 1)
            residual_squares("even_out_conv")
            layer_norm(0, 0)

            def cross_attention(i):
                name = f"x{i}"
                act.dma_start(mem_in, w["mem"].rearrange("(t p) n -> p t n", p=P)).then_inc(S["mem_loaded"], 16)
                for e in range(4):
                    bank = wait_aux(act, ("mem", i, e))
                    operand_hi(y_hi[:, 2 * e:2 * e + 2, 0:MEM], bank[:, :].rearrange("p (a b) -> p a b", a=2), y_hi_done)
                for n in range(4):
                    split_to(FIRST_PANEL[f"xk{i}"] + n + 1)
                    for s in range(2):
                        c = stage_chunk(f"xk{i}") + 2 * n + s
                        bank = wait_chunk(act, c)
                        free_chunk(act.activation(KT[:, 2 * n + s, :], bank[:, 0:MEM], ACT.Copy), c)
                for n in range(4):
                    split_to(FIRST_PANEL[f"xv{i}"] + n + 1)
                    c = stage_chunk(f"xv{i}") + n
                    bank = wait_chunk(act, c)
                    free_chunk(act.activation(VM[:, :, n * PANEL:(n + 1) * PANEL],
                                              bank[:, :].rearrange("p (t n) -> p t n", t=2), ACT.Copy), c)
                for n in range(4):
                    split_to(FIRST_PANEL[f"xq{i}"] + n + 1)
                    for s in range(2):
                        c = stage_chunk(f"xq{i}") + 2 * n + s
                        bank = wait_chunk(act, c)
                        free_chunk(act.activation(XQ[:, 2 * n + s, :], bank[:, :], ACT.Copy, scale=1.0 / 16), c)

                def exps(t):
                    un = UNIT[(name, t)]
                    act.wait_ge(S["unit_max"], un + 1)
                    for hd in range(XH):
                        key = (name, "S", t, hd // 2)
                        ins = act.activation(PR[:, t % 2, hd * MEM:(hd + 1) * MEM],
                                             wait_aux(act, key)[:, (hd % 2) * MEM:(hd % 2 + 1) * MEM], ACT.Exp,
                                             bias=mxs[:, un % 2, hd:hd + 1], accum_out=rs[:, un % 2, hd:hd + 1])
                        if hd % 2:
                            free_aux(ins, key)

                exps(0)
                for t in range(TT):
                    if t + 1 < TT:
                        exps(t + 1)
                    for m in range(2):
                        bank = wait_aux(act, (name, "T", t, m))
                        free_aux(act.activation(PTX[:, m, :, t * P:(t + 1) * P],
                                                bank[:, :].rearrange("p (a b) -> p a b", b=P), ACT.Copy),
                                 (name, "T", t, m))
                for j in range(KC):
                    bank = wait_aux(act, ("xpv", i, j))
                    operand_hi(x_hi[:, j, :], bank[:, :], x_hi_done)
                residual_squares(f"xo{i}")
                layer_norm(i, 1)

            def mlp(i):
                st = f"mlp{i}"
                for q in range(4):
                    for k in range(KC):
                        n = FIRST_PANEL[st] + 8 * q + k // 2
                        split_to(n + 1)
                        c = CHUNK0[n] + k % 2
                        bank = wait_chunk(act, c)
                        m = 32 * i + KC * q + k
                        if m % 32 >= 2:
                            act.wait_ge(y_ready, Y0[f"hid{i}0"] + (m % 32) - 1)
                        free_chunk(act.activation(area(0, 2, T)[:, k % 2, :], bank[:, :], ACT.Relu), c)
                        chunk_read(act, c)
                        act.activation(area(0, 2, T)[:, k % 2, :], area(0, 2, T)[:, k % 2, :], ACT.Square)\
                           .then_inc(S["hid_relu"], 1)
                    if q < 3:
                        for k in range(4):
                            split_to(FIRST_PANEL[st] + 8 * q + 4 + k + 1)
                    else:
                        residual_squares(st, half=28)
                layer_norm(i, 2)

            cross_attention(0)
            act.dma_start(w_small[:, :, :], w["odd_w_in"][:, 3072:3088].rearrange("(k p) n -> p k n", p=P))\
               .then_inc(S["small_loaded"], 16)
            mlp(0)

            for j in range(KC):
                if j % 2 == 0:
                    split_to(FIRST_PANEL["gla_qk"] + j // 2 + 1)
                c = stage_chunk("gla_qk") + j
                bank = wait_chunk(act, c)
                free_chunk(act.activation((GQ if j < 4 else GK)[:, j % 4, :], bank[:, :], ACT.Copy,
                                          scale=128.0 ** -0.5 if j < 4 else 1.0), c)
            bank = wait_aux(act, ("glow",))
            free_aux(act.activation(GL[0:16, :], bank[0:16, :], ACT.Copy), ("glow",))
            for stage, dst, func in (("gla_v", GVV, ACT.Copy), ("gla_g", GG, ACT.Silu)):
                for n in range(4):
                    split_to(FIRST_PANEL[stage] + n + 1)
                    for t2 in range(2):
                        c = stage_chunk(stage) + 2 * n + t2
                        bank = wait_chunk(act, c)
                        free_chunk(act.activation(dst[:, 2 * t2:2 * t2 + 2, n * PANEL:(n + 1) * PANEL],
                                                  bank[:, :].rearrange("p (t n) -> p t n", t=2), func), c)
            logs()
            for hd in range(GH):
                act.wait_ge(S["log_ready"], hd + 1)
                step(act.activation(GEB, GEB, ACT.Exp, scale=-1.0))
                act.activation(GEB, GEB, ACT.Ln, bias=1.0).then_inc(S["eb_ready"], 1)
                act.wait_ge(S["b_ready"], hd + 1)
                act.activation(GEB, GB, ACT.Exp)
                act.activation(GENB, GB, ACT.Exp, scale=-1.0)
                for n in range(8):
                    ins = act.activation(GKT.rearrange("p a b -> p (a b)")[:, 64 * n:64 * n + 64],
                                         GB[:, 64 * n:64 * n + 64], ACT.Exp, scale=-1.0,
                                         bias=GB[:, 64 * n + 63:64 * n + 64])
                ins.then_inc(S["eb_ready"], 1)
                bank = wait_aux(act, ("kend", hd))
                free_aux(act.activation(GKT.rearrange("p a b -> p (a b)"), bank[:, :], ACT.Copy), ("kend", hd))
                for t in range(TT):
                    aux_read(act, "go", hd, t)
                    step(act.activation(area(17920, GV), GY[:, t, :], ACT.Square, accum_out=rs[:, 0, 0:1]))
                    step(act.activation(rs[:, 1, 0:1], rs[:, 0, 0:1], ACT.Ln, bias=cst[:, 0:1], scale=1.0 / GV))
                    act.activation(rs[:, 1, 0:1], rs[:, 1, 0:1], ACT.Exp, scale=-0.5).then_inc(S["gla_rstd"], 1)
                for j in range(2):
                    bank = wait_aux(act, ("gt", hd, j))
                    operand_hi(x_hi[:, 2 * hd + j, :], bank[:, :], x_hi_done, par_col("odd_head_norm_g", j))
            residual_squares("odd_out")
            layer_norm(1, 0)
            cross_attention(1)
            act.dma_start(w_small[:, :, 0:8], w["w_in_2"][:, 4864:4872].rearrange("(k p) n -> p k n", p=P))\
               .then_inc(S["small_loaded"], 16)
            act.dma_start(row16[:, 0, 0:8], w["b_forget_2"].unsqueeze(0).broadcast_to([P, 8]))\
               .then_inc(S["lam_loaded"], 16)
            act.dma_start(row16[:, 1, 0:8], w["sinks_2"].unsqueeze(0).broadcast_to([P, 8]))\
               .then_inc(S["lam_loaded"], 16)
            mlp(1)

            act.wait_ge(S["h_ready"], KC * 7)
            act.dma_start(h_spill, h[:, :, :].rearrange("p a b -> p (a b)")).then_inc(S["spilled"], 16)
            for i, n_ in enumerate(("lambda_q1_2", "lambda_k1_2", "lambda_q2_2", "lambda_k2_2")):
                act.dma_start(LAMB[:, 64 * i:64 * i + 64], w[n_].unsqueeze(0).broadcast_to([P, 64]))\
                   .then_inc(S["lam_loaded"], 16)
            act.wait_ge(S["lam_sum"], 1)
            act.activation(lam[:, 0:2], lam[:, 0:2], ACT.Exp).then_inc(S["lam_ready"], 1)

            squares(lambda k: h[:, k, :], lambda k: None)
            normalised(lambda k: x_hi[:, k, :], lambda k: par_col("norm_gain_2", k), None, eps=1, rms=True)
            for n_, b in enumerate("abc"):
                scale = 1.0 / 8
                nq = 4
                for j in range(4 if b == "b" else KC):
                    if j % 2 == 0:
                        split_to(FIRST_PANEL[f"qk_{b}"] + j // 2 + 1)
                    c = stage_chunk(f"qk_{b}") + j
                    bank = wait_chunk(act, c)
                    free_chunk(act.activation(QK[:, j, :], bank[:, :], ACT.Copy, scale=scale if j < nq else 1.0), c)
                if b == "b":
                    split_to(FIRST_PANEL["kv_b"] + 1)
                    c = stage_chunk("kv_b")
                    bank = wait_chunk(act, c)
                    free_chunk(act.activation(QK[:, 4, :], bank[:, :], ACT.Copy), c)
                    bank = wait_chunk(act, c + 1)
                    free_chunk(act.activation(BV[:, :, 0:P], bank[:, :].rearrange("p (t n) -> p t n", n=P),
                                              ACT.Copy), c + 1)
                for stage, dst, func in ((f"v_{b}", BV, ACT.Copy), (f"g_{b}", BG, ACT.Silu)):
                    if stage not in FIRST_PANEL:
                        continue
                    for n in range(2):
                        split_to(FIRST_PANEL[stage] + n + 1)
                        for t2 in range(2):
                            c = stage_chunk(stage) + 2 * n + t2
                            bank = wait_chunk(act, c)
                            free_chunk(act.activation(dst[:, 2 * t2:2 * t2 + 2, n * PANEL:(n + 1) * PANEL],
                                                      bank[:, :].rearrange("p (t n) -> p t n", t=2), func), c)
                logs()
                if b == "c":
                    act.wait_ge(S["c_abs"], 1)
                    step(act.activation(sm[:, 12:14, :], sm[:, 12:14, :], ACT.Exp, scale=-1.0))
                    act.activation(sm[:, 12:14, :], sm[:, 12:14, :], ACT.Ln, bias=1.0).then_inc(S["c_soft"], 1)
                us = [(hd, t) for hd in range(8 if b == "c" else 4) for t in range(TT)]
                B = b.upper()

                def exps(u):
                    un = UNIT[(B, u)]
                    e = un % 2
                    act.wait_ge(S["unit_max"], un + 1)
                    if b == "a":
                        for m in range(2):
                            v = EX[:, e, m, 0:(u[1] + 1) * P]
                            ins = act.activation(v, v, ACT.Exp, bias=mxs[:, e, m:m + 1], accum_out=rs[:, e, m:m + 1])
                    elif b == "b":
                        for g in range(2):
                            v = EX[:, e, 0, g * 256 + (P if u[1] == 0 else 0):(g + 1) * 256]
                            act.activation(v, v, ACT.Exp, bias=mxs[:, e, g:g + 1], accum_out=rs[:, e, g:g + 1])
                            hd = u[0] + 4 * g
                            ins = act.activation(rs[:, e, 2 + g:3 + g], row16[:, 1, hd:hd + 1], ACT.Exp,
                                                 bias=mxs[:, e, g:g + 1])
                    else:
                        v = EX[:, e, 0, 0:(u[1] + 1) * P]
                        ins = act.activation(v, v, ACT.Exp, bias=mxs[:, e, 0:1], accum_out=rs[:, e, 0:1])
                    ins.then_inc(S["unit_exp"], 1)

                def square_unit(n):
                    hd, t = us[n]
                    aux_read(act, "A", "PV", us[n])
                    col = t * 4 + hd
                    step(act.activation(PT[:, UNIT[("A", us[n])] % 2, 0:P], YT[:, t, hd * P:(hd + 1) * P], ACT.Square,
                                        accum_out=sm[:, 8, col:col + 1]))

                per = len(us) // KC
                first = FIRST_PANEL[f"gm_{b}"]
                split_chunks(2 * first + W_SLOTS)
                exps(us[0])
                for n, u in enumerate(us):
                    if n + 1 < len(us):
                        exps(us[n + 1])
                    if b == "a" and n:
                        square_unit(n - 1)
                    e = UNIT[(B, u)] % 2
                    bank = wait_aux(act, (B, "T", u, 0))
                    if b == "b":
                        lo = P if u[1] == 0 else 0
                        src = bank[:, :].rearrange("p (g n) -> p g n", g=2)[:, :, lo:]
                        dst = PT[:, e, :].rearrange("p (g n) -> p g n", g=2)[:, :, lo:]
                    else:
                        src, dst = bank[:, 0:(u[1] + 1) * P], PT[:, e, 0:(u[1] + 1) * P]
                    free_aux(act.activation(dst, src, ACT.Copy), (B, "T", u, 0))
                    if n % per == per - 1:
                        f = n // per
                        if f == 0 and b == "a":
                            act.wait_ge(S["spilled"], 32)
                        elif f == 0:
                            chunk_read(act, CHUNK0[FIRST_PANEL[f"up_{'abc'[n_ - 1]}"]] + 7)
                            if n_ == 2:
                                act.wait_ge(S["merged_ready"], KC)
                        c = stage_chunk(f"gm_{b}") + f
                        bank = wait_chunk(act, c)
                        free_chunk(act.activation(GATE[:, f, :], bank[:, :], ACT.Copy), c)
                        split_chunks(2 * first + W_SLOTS + f + 1)
                if b == "a":
                    square_unit(len(us) - 1)
                    step(act.activation(sm[:, 9, :], sm[:, 8, :], ACT.Ln, bias=cst[:, 0:1], scale=1.0 / P))
                    act.activation(sm[:, 9, :], sm[:, 9, :], ACT.Exp, scale=-0.5).then_inc(S["ya_rstd"], 1)
                for k in range(KC):
                    chunk_read(act, stage_chunk(f"gm_{b}") + k)
                    act.activation(GATE[:, k, :], GATE[:, k, :], ACT.Sigmoid).then_inc(S["gate_ready"], 1)
                for j in range(4):
                    bank = wait_aux(act, (B + "t", j))
                    operand_hi(y_hi[:, j, :], bank[:, :], y_hi_done, lam[:, 3:4] if b == "a" else 1.0)
            split_to(FIRST_PANEL["w_o"])
            for k, f in enumerate(UP_ORDER):
                act.wait_ge(S["merged_ready"], KC + k + 1)
                operand_hi(x_hi[:, f, :], MG[:, f, :], x_hi_done)
            act.dma_start(h[:, :, :].rearrange("p a b -> p (a b)"), h_spill).then_inc(S["reloaded"], 16)
            residual_squares("w_o")
            normalised(lambda k: MG[:, k, :], lambda k: par_col("final_gain_2", k), None, eps=1, rms=True)
            for t in range(TT):
                for j in range(2):
                    bank = wait_aux(act, ("out", t, j))
                    free_aux(act.activation(area(0, TT, D)[:, t, 512 * j:512 * j + 512], bank[:, :], ACT.Copy),
                             ("out", t, j))
                aux_read(act, "out", t, 1)
                act.dma_start(out[t * P:(t + 1) * P, :], area(0, TT, D)[:, t, :]).then_inc(S["out_sent"], 16)
            act.wait_ge(S["out_sent"], 16 * TT)

        @block.vector
        def _(dve):
            at = dict(step=0, split=0, prod=0, end=0, ln=0, sq=0, hr=0, xh=0, yh=0, lh=0)

            def step(ins):
                at["step"] += 1
                ins.then_inc(dve_step, 1)
                dve.wait_ge(dve_step, at["step"])

            def stage_barrier():
                at["end"] += 1
                dve.drain().then_inc(stage_end, 1)
                dve.wait_ge(stage_end, 3 * at["end"])

            def split_chunk():
                s = at["split"]
                if s < 2 * NPANEL:
                    dve.wait_ge(w_hi_ready, s + 1)
                    half = slice((s % 2) * P, (s % 2 + 1) * P)
                    dve.tensor_tensor(w_lo[:, s % W_SLOTS, :, :], raw[:, s // 2 % RAW_SLOTS, :, half],
                                      w_hi[:, s % W_SLOTS, :, :].bitcast(F32), ALU.subtract).then_inc(w_lo_ready, 1)
                    at["split"] += 1

            def split_chunks(upto):
                while at["split"] < upto:
                    split_chunk()

            def split_to(panel):
                while at["split"] < min(2 * panel + 2, 2 * NPANEL):
                    split_chunk()

            def operand(hi, lo, src, ready):
                step(dve.tensor_copy(hi, src))
                dve.tensor_tensor(lo, src, hi.bitcast(F32), ALU.subtract).then_inc(ready, 1)

            def operand_lo(hi, lo, src, hi_sem, which, scale=None):
                at[which] += 1
                dve.wait_ge(hi_sem, at[which])
                if scale is None:
                    return dve.tensor_tensor(lo, src, hi.bitcast(F32), ALU.subtract)
                return dve.scalar_tensor_tensor(lo, src, scale, hi.bitcast(F32), ALU.mult, ALU.subtract)

            def accumulate(k, src, mean=True):
                at["sq"] += 1
                dve.wait_ge(S["sq_ready"], at["sq"])
                sq = LN[:, k % 2, :]
                if k == 0:
                    if mean:
                        dve.tensor_copy(LN[:, 3, :], src)
                    ins = dve.tensor_copy(LN[:, 4, :], sq)
                else:
                    if mean:
                        dve.tensor_tensor(LN[:, 3, :], LN[:, 3, :], src, ALU.add)
                    ins = dve.tensor_tensor(LN[:, 4, :], LN[:, 4, :], sq, ALU.add)
                ins.then_inc(S["sum_in"], 1)
                dve.wait_ge(S["sum_in"], at["sq"])

            def normalise(name, src, finish, center=True, lag=2, more=True):
                n = at["ln"]
                at["ln"] += 1
                if center:
                    bank = wait_aux(dve, ("ln", name, 0))
                    free_aux(dve.tensor_scalar(LN[:, 0, :], bank[:, :], 1.0 / D, None, ALU.mult), ("ln", name, 0))
                    aux_read(dve, "ln", name, 0)
                    step(dve.tensor_tensor(LN[:, 1, :], LN[:, 0, :], LN[:, 0, :], ALU.mult))
                    bank = wait_aux(dve, ("ln", name, 1))
                    free_aux(dve.scalar_tensor_tensor(LN[:, 1, :], bank[:, :], 1.0 / D, LN[:, 1, :], ALU.mult,
                                                      ALU.subtract), ("ln", name, 1))
                    aux_read(dve, "ln", name, 1)
                    dve.tensor_scalar(LN[:, 1, :], LN[:, 1, :], 0.0, None, ALU.max).then_inc(S["ln_var"], 1)
                else:
                    bank = wait_aux(dve, ("rms", name))
                    free_aux(dve.tensor_scalar(LN[:, 1, :], bank[:, :], 1.0 / D, None, ALU.mult), ("rms", name))
                    aux_read(dve, "rms", name)
                    dve.engine_nop().then_inc(S["ln_var"], 1)
                if more:
                    split_to(at["split"] // 2)
                dve.wait_ge(S["ln_rstd"], n + 1)
                for k in range(KC + lag):
                    if k < KC:
                        xn = LN[:, 3 + k % 2, :]
                        if center:
                            step(dve.tensor_tensor(xn, src(k), LN[:, 0, :], ALU.subtract))
                            dve.tensor_tensor(xn, xn, LN[:, 2, :], ALU.mult).then_inc(S["ln_xn"], 1)
                        else:
                            dve.tensor_tensor(xn, src(k), LN[:, 2, :], ALU.mult).then_inc(S["ln_xn"], 1)
                    if k and k <= KC:
                        at["hr"] += 1
                        dve.wait_ge(S["h_ready"], at["hr"])
                    if k >= lag:
                        finish(k - lag)

            def rest(hi, lo, src, ready):
                def finish(k):
                    at["lh"] += 1
                    dve.wait_ge(S["ln_hi"], at["lh"])
                    dve.tensor_tensor(lo[:, k, :], src(k), hi[:, k, :].bitcast(F32), ALU.subtract).then_inc(ready, 1)
                return finish

            to_x = rest(x_hi, x_lo, lambda k: h[:, k, :], x_ready)

            def residual(stage, half=0, scale=None, sums=None, chunks=range(KC)):
                for k in chunks:
                    n = FIRST_PANEL[stage] + half + k // 2
                    if k % 2 == 0:
                        split_to(n + 1)
                    c = CHUNK0[n] + k % 2
                    bank = wait_chunk(dve, c)
                    if scale is None:
                        free_chunk(dve.tensor_tensor(h[:, k, :], h[:, k, :], bank[:, :], ALU.add), c)
                    else:
                        free_chunk(dve.scalar_tensor_tensor(h[:, k, :], h[:, k, :], scale, bank[:, :], ALU.mult,
                                                            ALU.add), c)
                    if sums is not None:
                        if k:
                            accumulate(k - 1, h[:, k - 1, :], sums)
                        if k == KC - 1:
                            chunk_read(dve, c)
                            accumulate(k, h[:, k, :], sums)

            def spread(v, n):
                return v.unsqueeze(2).broadcast_to([P, v.shape[1], n])

            def over(v, n):
                return v.unsqueeze(1).broadcast_to([P, n, v.shape[1]])

            split_to(1)
            for k in range(KC):
                aux_read(dve, "x", k)
                operand(x_hi[:, k, :], x_lo[:, k, :], h[:, k, :], x_ready)
            stage_barrier()

            step(dve.memset(U[:, :, 0:CONV_W - 1], 0.0))
            step(dve.memset(XB[:, :, 0:SSM_W - 1], 0.0))
            bank = wait_aux(dve, ("dt",))
            soft = area(17940, TT, SH)
            dt = sm[:, 4:8, :]
            free_aux(dve.tensor_tensor(dt, bank[:, 0:TT * SH].rearrange("p (t n) -> p t n", n=SH),
                                       over(row16[:, 0, :], TT), ALU.add), ("dt",))
            aux_read(dve, "dt")
            dve.scalar_tensor_tensor(soft, dt, -1.0, dt, ALU.mult, ALU.max).then_inc(S["dt_abs"], 1)
            dve.wait_ge(S["dt_soft"], 1)
            step(dve.scalar_tensor_tensor(dt, dt, 0.0, soft, ALU.max, ALU.add))
            dve.scalar_tensor_tensor(sm[:, 0:4, :], dt, -1.0, over(row16[:, 1, :], TT), ALU.mult, ALU.mult)\
               .then_inc(S["dta_ready"], 1)
            for j in range(XC):
                if j % 2 == 0:
                    split_to(FIRST_PANEL["xbc"] + j // 2 + 1)
                chunk_read(dve, stage_chunk("xbc") + j)
                if j >= 2:
                    dve.wait_ge(S["xbc_ready"], j - 1)
                tmp = TMP[:, j % 2, :]
                step(dve.tensor_scalar(tmp, XB[:, j, 0:T], par_col("even_ssm_conv_w", j),
                                       par_col("even_ssm_conv_b", j), ALU.mult, ALU.add))
                for i in range(1, SSM_W):
                    ins = dve.scalar_tensor_tensor(tmp, XB[:, j, i:i + T], par_col("even_ssm_conv_w", i * XC + j), tmp,
                                                   ALU.mult, ALU.add)
                    if i < SSM_W - 1:
                        step(ins)
                ins.then_inc(S["xbc_conv"], 1)

            def side_work():
                f = at["prod"]
                if f < KC and at["split"] >= 2 * (FIRST_PANEL["conv_in"] + f + 2) + 2:
                    c = stage_chunk("conv_in") + 4 * (f // 2) + f % 2
                    chunk_read(dve, c + 2)
                    bank = wait_chunk(dve, c)
                    free_chunk(dve.tensor_tensor(U[:, f, CONV_W - 1:], bank[:, :], SG[:, f % 2, :], ALU.mult), c)
                    at["prod"] += 1
                elif f < KC or at["split"] < 2 * FIRST_PANEL["even_out_ssm"]:
                    split_chunk()

            for f0 in range(0, DVE_CONV, 2):
                fs = range(f0, min(f0 + 2, DVE_CONV))
                added = {}
                while at["prod"] < fs[-1] + 1:
                    side_work()
                for i in range(CONV_W):
                    for f in fs:
                        acc = CV[:, f % 2, :]
                        last = i == CONV_W - 1
                        if i == 0:
                            chunk_read(dve, stage_chunk("conv_in") + 4 * (f // 2) + f % 2)
                            at["step"] += 1
                            dve.tensor_scalar(acc, U[:, f, 0:T], par_col("even_conv_w", f), par_col("even_conv_b", f),
                                              ALU.mult, ALU.add).then_inc(dve_step, 1)
                        else:
                            dve.wait_ge(dve_step, added[f])
                            ins = dve.scalar_tensor_tensor(U[:, f, CONV_W - 1:] if last else acc, U[:, f, i:i + T],
                                                           par_col("even_conv_w", i * KC + f), acc, ALU.mult, ALU.add)
                            if last:
                                ins.then_inc(S["conv_sum"], 1)
                            else:
                                at["step"] += 1
                                ins.then_inc(dve_step, 1)
                        added[f] = at["step"]
                    if i % 2 == 0:
                        side_work()
                dve.wait_ge(S["conv_sum"], fs[-1] + 1)
            while at["prod"] < KC:
                side_work()
            split_to(FIRST_PANEL["even_out_ssm"])
            tri2 = over(triu[:, :], 2)
            cb = TMP[:, 0, 0:2 * P].rearrange("p (a b) -> p a b", b=P)

            def sums_spread(c):
                r = 8 + 4 * (c % 2)
                bank = wait_aux(dve, ("acs", c))
                free_aux(dve.tensor_copy(sm[:, r, :], bank[:, 0:SH]), ("acs", c))
                aux_read(dve, "acs", c)
                if c:
                    wait_aux(dve, ("yd", c - 1, 1))
                dve.tensor_tensor(M, over(ident[:, :], SH), spread(sm[:, r, :], P), ALU.mult)\
                   .then_inc(S["bcr_ready"], 1)

            def differences(c):
                r = 8 + 4 * (c % 2)
                for q in range(4):
                    bank = wait_aux(dve, ("bc", c, q))
                    rows = bank[:, :].rearrange("p (a b) -> p a b", b=P)
                    hs = slice(4 * q, 4 * q + 4)
                    dve.tensor_tensor(sm[:, r + 1, hs], rows[:, :, P - 1], sm[:, r, hs], ALU.subtract)
                    dve.tensor_copy(sm[:, r + 2, hs], rows[:, :, P - 1])
                    for j in range(4):
                        hd = 4 * q + j
                        ins = dve.tensor_scalar(M[:, hd, :], rows[:, j, :], sm[:, r, hd:hd + 1], 0.0, ALU.subtract,
                                                ALU.min)
                    free_aux(ins, ("bc", c, q))
                aux_read(dve, "bc", c, 3)
                dve.engine_nop().then_inc(S["seg_ready"], 1)

            sums_spread(0)
            differences(0)
            for c in range(TT):
                tok = slice(c * P, (c + 1) * P)
                r = 8 + 4 * (c % 2)
                if c == 0:
                    dve.wait_ge(S["xbc_ready"], XC)
                bank = wait_aux(dve, ("cb", c))
                free_aux(dve.tensor_tensor(cb, bank[:, 0:2 * P].rearrange("p (a b) -> p a b", b=P), tri2, ALU.mult),
                         ("cb", c))
                aux_read(dve, "cb", c)
                aux_read(dve, "bt", c)
                xs = XS.rearrange("p (a b) -> p a b", b=SP_)
                step(dve.tensor_tensor(XDT, xs, spread(sm[:, 4 + c, :], SP_), ALU.mult))
                dve.wait_ge(S["dte_ready"], c + 1)
                dve.tensor_tensor(XW, XDT, spread(sm[:, r + 1, :], SP_), ALU.mult).then_inc(S["xdt_ready"], 1)
                dve.wait_ge(S["decay_ready"], c + 1)
                for g in range(2):
                    m8 = M[:, 8 * g:8 * g + 8, :]
                    ins = dve.tensor_tensor(m8, m8, over(cb[:, g, :], 8), ALU.mult)
                ins.then_inc(S["m_ready"], 1)
                dve.wait_ge(S["m_ready"], c + 1)
                skip = TMP.rearrange("p a b -> p (a b)").rearrange("p (a b) -> p a b", b=SP_)
                step(dve.tensor_tensor(skip, xs, spread(row16[:, 2, :], SP_), ALU.mult))
                wait_aux(dve, ("yd", c, 1))
                if c + 1 < TT:
                    sums_spread(c + 1)
                for g in range(2):
                    y8 = XDT[:, 8 * g:8 * g + 8, :]
                    bank = wait_aux(dve, ("yd", c, g))
                    free_aux(dve.tensor_tensor(y8, bank[:, :].rearrange("p (a b) -> p a b", b=SP_),
                                               skip[:, 8 * g:8 * g + 8, :], ALU.add), ("yd", c, g))
                    if c:
                        bank = wait_aux(dve, ("yo", c, g))
                        aux_read(dve, "yd", c, g)
                        free_aux(dve.tensor_tensor(skip[:, 8 * g:8 * g + 8, :],
                                                   bank[:, :].rearrange("p (a b) -> p a b", b=SP_),
                                                   spread(sm[:, r + 3, 8 * g:8 * g + 8], SP_), ALU.mult), ("yo", c, g))
                if c:
                    aux_read(dve, "yo", c, 1)
                    step(dve.tensor_tensor(XDT, XDT, skip, ALU.add))
                else:
                    aux_read(dve, "yd", c, 1)
                if c == 0:
                    chunk_read(dve, stage_end_chunk("z") - 1)
                dve.tensor_tensor(XDT.rearrange("p a b -> p (a b)"), XDT.rearrange("p a b -> p (a b)"), Z[:, c, :],
                                  ALU.mult).then_inc(S["gated"], 1)
                st8 = ST.rearrange("p a b -> p (a b)").rearrange("p (a b) -> p a b", b=SP_)
                if c:
                    step(dve.tensor_tensor(st8, st8, spread(sm[:, r + 2, :], SP_), ALU.mult))
                for g in range(2):
                    bank = wait_aux(dve, ("st", c, g))
                    if c:
                        free_aux(dve.tensor_tensor(ST[:, g, :], ST[:, g, :], bank[:, :], ALU.add), ("st", c, g))
                    else:
                        free_aux(dve.tensor_copy(ST[:, g, :], bank[:, :]), ("st", c, g))
                aux_read(dve, "st", c, 1)
                dve.engine_nop().then_inc(S["state_ready"], 1)
                if c + 1 < TT:
                    differences(c + 1)
                dve.wait_ge(S["ssm_rstd"], c + 1)
                dve.wait_ge(S["gated"], c + 1)
                for g in range(2):
                    y8 = XDT[:, 8 * g:8 * g + 8, :]
                    ins = dve.tensor_scalar(y8, y8, rs[:, 1, g:g + 1], None, ALU.mult)
                ins.then_inc(S["y_gated"], 1)
                for g in range(2):
                    bank = wait_aux(dve, ("yt", c, g))
                    at["xh"] += 1
                    dve.wait_ge(x_hi_done, at["xh"])
                    for j in range(4):
                        k = 4 * g + j
                        ins = dve.scalar_tensor_tensor(x_lo[:, k, tok], bank[:, j * P:(j + 1) * P],
                                                       par_col("even_ssm_norm_g", k), x_hi[:, k, tok].bitcast(F32),
                                                       ALU.mult, ALU.subtract)
                    free_aux(ins, ("yt", c, g))
            split_to(FIRST_PANEL["even_out_ssm"] + 1)
            for k in range(KC):
                accumulate(k, U[:, k, CONV_W - 1:])
            dve.wait_ge(S["reloaded"], 16)
            residual("even_out_ssm", scale=ALPHA, chunks=range(0, 4))
            normalise("conv", lambda k: U[:, k, CONV_W - 1:],
                      rest(y_hi, y_lo, lambda k: U[:, k, CONV_W - 1:], y_ready))
            residual("even_out_ssm", scale=ALPHA, chunks=range(4, KC))
            residual("even_out_conv", sums=True)
            normalise("m0", lambda k: h[:, k, :], to_x)

            def cross_attention(i):
                name = f"x{i}"
                for e in range(4):
                    bank = wait_aux(dve, ("mem", i, e))
                    s = slice(2 * e, 2 * e + 2)
                    free_aux(operand_lo(y_hi[:, s, 0:MEM], y_lo[:, s, 0:MEM],
                                        bank[:, :].rearrange("p (a b) -> p a b", a=2), y_hi_done, "yh"), ("mem", i, e))
                for stage in ("xk", "xv", "xq"):
                    for n in range(4):
                        split_to(FIRST_PANEL[f"{stage}{i}"] + n + 1)

                def maxima(t):
                    e2 = UNIT[(name, t)] % 2
                    for e in range(2):
                        bank = wait_aux(dve, (name, "S", t, e))
                        ins = dve.tensor_reduce(mxs[:, e2, 2 * e:2 * e + 2],
                                                bank[:, :].rearrange("p (a b) -> p a b", b=MEM), AX.X, ALU.max,
                                                negate=True)
                    ins.then_inc(S["unit_max"], 1)

                maxima(0)
                for t in range(TT):
                    if t + 1 < TT:
                        maxima(t + 1)
                    e2 = UNIT[(name, t)] % 2
                    aux_read(dve, name, "S", t, 1)
                    step(dve.reciprocal(rs[:, e2, :], rs[:, e2, :]))
                    pr = PR[:, t % 2, :].rearrange("p (a b) -> p a b", b=MEM)
                    dve.tensor_tensor(pr, pr, spread(rs[:, e2, :], MEM), ALU.mult).then_inc(S["p_ready"], 1)
                for j in range(KC):
                    bank = wait_aux(dve, ("xpv", i, j))
                    free_aux(operand_lo(x_hi[:, j, :], x_lo[:, j, :], bank[:, :], x_hi_done, "xh"), ("xpv", i, j))
                residual(f"xo{i}", scale=ALPHA, sums=True)
                normalise(f"a{i}", lambda k: h[:, k, :], to_x)

            def mlp(i):
                st = f"mlp{i}"
                for q in range(4):
                    for k in range(KC):
                        split_to(FIRST_PANEL[st] + 8 * q + k // 2 + 1)
                        dve.wait_ge(S["hid_relu"], 32 * i + KC * q + k + 1)
                        operand(y_hi[:, k, :], y_lo[:, k, :], area(0, 2, T)[:, k % 2, :], y_ready)
                    residual(st, half=8 * q + 4, scale=ALPHA if q == 0 else None, sums=True if q == 3 else None)
                normalise(f"f{i}", lambda k: h[:, k, :], to_x if i == 0 else lambda k: None, more=i == 0)

            cross_attention(0)
            mlp(0)

            block_mask = area(18176, P)
            step(dve.memset(GA, 0.0))
            step(dve.tensor_copy(block_mask, triu[:, :]))
            step(dve.memset(block_mask[0:64, 64:128], 0.0))
            step(dve.memset(GMASK, 1.0))
            step(dve.memset(GMASK.rearrange("p (a b) -> p a b", b=64)[:, :, 0:1], 0.0))
            step(dve.memset(GQE, 0.0))
            step(dve.memset(GQO, 0.0))
            for stage in ("gla_qk", "gla_v", "gla_g"):
                for n in range(4):
                    split_to(FIRST_PANEL[stage] + n + 1)
            for hd in range(GH):
                bank = wait_aux(dve, ("gate", hd))
                free_aux(dve.tensor_scalar(GENB, bank[:, :], par_col("odd_b_gate", hd), None, ALU.add), ("gate", hd))
                aux_read(dve, "gate", hd)
                dve.scalar_tensor_tensor(GEB, GENB, -1.0, GENB, ALU.mult, ALU.max).then_inc(S["log_ready"], 1)
                dve.wait_ge(S["eb_ready"], 2 * hd + 1)
                step(dve.scalar_tensor_tensor(GENB, GENB, 0.0, GEB, ALU.min, ALU.subtract))
                step(dve.tensor_scalar(GENB, GENB, 1.0 / 16, None, ALU.mult))
                dve.tensor_tensor_scan(GB, GMASK, GENB, 0.0, ALU.mult, ALU.add).then_inc(S["b_ready"], 1)
                dve.wait_ge(S["eb_ready"], 2 * hd + 2)
                q = GQ[:, hd, :]
                step(dve.tensor_tensor(q, q, GEB, ALU.mult))
                for n, dst in enumerate((GQE, GQO)):
                    part = (lambda v: v.rearrange("p (t a b) -> p t a b", a=2, b=64)[:, :, n, :])
                    dve.tensor_copy(part(dst), part(q))
                dve.tensor_tensor(GENB, GK[:, hd, :], GENB, ALU.mult)
                step(dve.memset(GS, 0.0))
                dve.engine_nop().then_inc(S["s_ready"], 1)
                dve.tensor_tensor(GK[:, hd, :], GK[:, hd, :], GKT.rearrange("p a b -> p (a b)"), ALU.mult)\
                   .then_inc(S["qkt_ready"], 1)
                for t in range(TT):
                    u = TT * hd + t
                    bank = wait_aux(dve, ("gatt", hd, t))
                    free_aux(dve.copy_predicated(GA[:, u % 2, :], block_mask.bitcast(mybir.dt.uint32), bank[:, 0:P]),
                             ("gatt", hd, t))
                    kv = wait_aux(dve, ("gkv", hd, t, 0))
                    dve.wait_ge(S["s_read"], u + 1)
                    free_aux(dve.scalar_tensor_tensor(GS, GS, GEB[:, P * t + 63:P * t + 64], kv[:, 0:GV], ALU.mult,
                                                      ALU.add), ("gkv", hd, t, 0))
                    bank = wait_aux(dve, ("go", hd, t))
                    kv = wait_aux(dve, ("gkv", hd, t, 1))
                    aux_read(dve, "gkv", hd, t, 0)
                    free_aux(dve.scalar_tensor_tensor(GS, GS, GEB[:, P * t + 127:P * t + 128], kv[:, 0:GV],
                                                      ALU.mult, ALU.add), ("gkv", hd, t, 1))
                    free_aux(dve.tensor_copy(GY[:, t, :], bank[:, 0:GV]), ("go", hd, t))
                    dve.wait_ge(S["gla_rstd"], u + 1)
                    aux_read(dve, "go", hd, t)
                    ins = dve.scalar_tensor_tensor(GY[:, t, :], GY[:, t, :], rs[:, 1, 0:1],
                                                   GG[:, t, hd * GV:(hd + 1) * GV], ALU.mult, ALU.mult)
                ins.then_inc(S["o_ready"], 1)
                for j in range(2):
                    bank = wait_aux(dve, ("gt", hd, j))
                    k = 2 * hd + j
                    free_aux(operand_lo(x_hi[:, k, :], x_lo[:, k, :], bank[:, :], x_hi_done, "xh",
                                        par_col("odd_head_norm_g", j)), ("gt", hd, j))
            residual("odd_out", scale=ALPHA, sums=True)
            normalise("m1", lambda k: h[:, k, :], to_x)
            cross_attention(1)
            mlp(1)

            dve.wait_ge(S["lam_loaded"], 16 * 6)
            lq = LAMB[:, 0:256].rearrange("p (a b c) -> p a b c", a=2, b=2)
            prod = LAMB[:, 256:384].rearrange("p (a b) -> p a b", a=2)
            step(dve.tensor_tensor(prod, lq[:, :, 0, :], lq[:, :, 1, :], ALU.mult))
            dve.tensor_reduce(lam[:, 0:2], prod, AX.X, ALU.add).then_inc(S["lam_sum"], 1)
            dve.wait_ge(S["lam_ready"], 1)
            step(dve.tensor_tensor(lam[:, 2:3], lam[:, 1:2], lam[:, 0:1], ALU.subtract))
            step(dve.tensor_scalar(lam[:, 2:3], lam[:, 2:3], -0.2, None, ALU.add))
            step(dve.tensor_scalar(lam[:, 3:4], par_col("subln_gain_2"), 0.8, None, ALU.mult))
            for k in range(KC):
                accumulate(k, None, False)

            def rms_lo(k):
                dve.scalar_tensor_tensor(x_lo[:, k, :], LN[:, 3 + k % 2, :], par_col("norm_gain_2", k),
                                         x_hi[:, k, :].bitcast(F32), ALU.mult, ALU.subtract).then_inc(x_ready, 1)
                dve.wait_ge(x_ready, KC * X_FILLS.index("rms") + k + 1)

            normalise(0, lambda k: h[:, k, :], rms_lo, center=False, lag=1)
            dve.wait_ge(consts_ready, 2)
            for n_, b in enumerate("abc"):
                B = b.upper()
                for stage in (f"qk_{b}", f"kv_{b}", f"v_{b}", f"g_{b}"):
                    if stage in FIRST_PANEL:
                        for n in range(FIRST_PANEL[stage], len(PLAN)):
                            if PLAN[n][0] == stage:
                                split_to(n + 1)
                if b == "c":
                    bank = wait_aux(dve, ("fc",))
                    z = sm[:, 0:4, 0:8]
                    zabs = sm[:, 12:14, :].rearrange("p a b -> p (a b)").rearrange("p (a b) -> p a b", b=8)
                    free_aux(dve.tensor_tensor(z, bank[:, 0:32].rearrange("p (a b) -> p a b", b=8),
                                               over(row16[:, 0, 0:8], 4), ALU.add), ("fc",))
                    aux_read(dve, "fc")
                    dve.scalar_tensor_tensor(zabs, z, -1.0, z, ALU.mult, ALU.max).then_inc(S["c_abs"], 1)
                    dve.wait_ge(S["c_soft"], 1)
                    dve.scalar_tensor_tensor(z, z, 0.0, zabs, ALU.min, ALU.subtract).then_inc(S["log_ready"], 1)
                    bank = wait_aux(dve, ("cc",))
                    free_aux(dve.tensor_copy(sm[:, 4:8, 0:8], bank[:, 0:32].rearrange("p (a b) -> p a b", b=8)),
                             ("cc",))
                    aux_read(dve, "cc")
                    step(dve.tensor_scalar(R[:, 0:P], R[:, 384:512], NEG / 10, NEG, ALU.is_le, ALU.mult))

                def maxima(u):
                    e = UNIT[(B, u)] % 2
                    hd, t = u
                    n = (t + 1) * P
                    if b == "a":
                        for m in range(2):
                            bank = wait_aux(dve, ("A", "S", u, m))
                            free_aux(dve.scalar_tensor_tensor(EX[:, e, m, 0:n], R[:, 512 - n:512], 0.25 ** (hd + 1),
                                                              bank[:, 0:n], ALU.mult, ALU.add), ("A", "S", u, m))
                        aux_read(dve, "A", "S", u, 1)
                        ins = dve.tensor_reduce(mxs[:, e, 0:2], EX[:, e, :, 0:n], AX.X, ALU.max, negate=True)
                    elif b == "b":
                        off = P if t == 0 else 0
                        for g in range(2):
                            bank = wait_aux(dve, ("B", "S", u, g))
                            s = slice(g * 256 + off, (g + 1) * 256)
                            free_aux(dve.scalar_tensor_tensor(EX[:, e, 0, s], RB[:, off:256],
                                                              0.5 ** (hd + 4 * g + 1), bank[:, off:256],
                                                              ALU.mult, ALU.add), ("B", "S", u, g))
                        aux_read(dve, "B", "S", u, 1)
                        m = mxs[:, e, 0:2]
                        step(dve.tensor_reduce(m, EX[:, e, 0, :].rearrange("p (a b) -> p a b", a=2)[:, :, off:],
                                               AX.X, ALU.max))
                        step(dve.tensor_tensor(m, m, row16[:, 1, hd:hd + 5:4], ALU.max))
                        ins = dve.tensor_scalar(m, m, -1.0, None, ALU.mult)
                    else:
                        bank = wait_aux(dve, ("C", "S", u, 0))
                        free_aux(dve.scalar_tensor_tensor(EX[:, e, 0, 0:n], EX[:, hd % 2, 1, 0:n], sm[:, 4 + t, hd:hd + 1],
                                                          bank[:, 0:n], ALU.add, ALU.add), ("C", "S", u, 0))
                        aux_read(dve, "C", "S", u, 0)
                        diag = EX[:, e, 0, n - P:n]
                        step(dve.tensor_tensor(diag, diag, R[:, 0:P], ALU.add))
                        ins = dve.tensor_reduce(mxs[:, e, 0:1], EX[:, e, 0, 0:n], AX.X, ALU.max, negate=True)
                    ins.then_inc(S["unit_max"], 1)

                def weights(u):
                    un = UNIT[(B, u)]
                    e = un % 2
                    n = (u[1] + 1) * P
                    dve.wait_ge(S["unit_exp"], un - 2 * TT + 1)
                    if b == "a":
                        step(dve.reciprocal(rs[:, e, 2:4], rs[:, e, 0:2]))
                        step(dve.scalar_tensor_tensor(rs[:, e, 1:2], rs[:, e, 0:1], rs[:, e, 3:4], lam[:, 2:3],
                                                      ALU.mult, ALU.mult))
                        dve.scalar_tensor_tensor(EX[:, e, 0, 0:n], EX[:, e, 1, 0:n], rs[:, e, 1:2], EX[:, e, 0, 0:n],
                                                 ALU.mult, ALU.add).then_inc(S["p_ready"], 1)
                    elif b == "b":
                        step(dve.tensor_tensor(rs[:, e, 0:2], rs[:, e, 0:2], rs[:, e, 2:4], ALU.add))
                        step(dve.reciprocal(rs[:, e, 2:4], rs[:, e, 0:2]))
                    else:
                        step(dve.reciprocal(rs[:, e, 2:3], rs[:, e, 0:1]))

                def values(u, last):
                    hd, t = u
                    e = UNIT[(B, u)] % 2
                    bank = wait_aux(dve, (B, "PV", u))
                    if b == "a":
                        ins = dve.tensor_scalar(YT[:, t, hd * P:(hd + 1) * P], bank[:, 0:P], rs[:, e, 2:3], None,
                                                ALU.mult)
                    elif b == "b":
                        for g in range(2):
                            s = slice(256 * g + 64 * hd, 256 * g + 64 * hd + 64)
                            ins = dve.scalar_tensor_tensor(YT[:, t, s], bank[:, 64 * g:64 * g + 64],
                                                           rs[:, e, 2 + g:3 + g], BG[:, t, s], ALU.mult, ALU.mult)
                    else:
                        s = slice(64 * hd, 64 * hd + 64)
                        ins = dve.scalar_tensor_tensor(YT[:, t, s], bank[:, 0:64], rs[:, e, 2:3], BG[:, t, s],
                                                       ALU.mult, ALU.mult)
                    free_aux(ins, (B, "PV", u))
                    if last and b != "a":
                        aux_read(dve, B, "PV", u)
                        dve.engine_nop().then_inc(S["y_tm_ready"], 1)

                def spread_sums(hd):
                    if hd:
                        wait_aux(dve, ("cb_c", hd - 1))
                    dve.tensor_tensor(NC.rearrange("p (a b) -> p a b", b=P), over(ident[:, :], TT),
                                      spread(sm[:, 4:8, hd], P), ALU.mult).then_inc(S["c_rhs"], 1)

                def key_sums(hd):
                    bank = wait_aux(dve, ("cb_c", hd))
                    free_aux(dve.tensor_scalar(EX[:, hd % 2, 1, :], bank[:, :], -1.0, None, ALU.mult), ("cb_c", hd))
                    aux_read(dve, "cb_c", hd)

                us = [(hd, t) for hd in range(8 if b == "c" else 4) for t in range(TT)]
                per = len(us) // KC
                split_chunks(2 * FIRST_PANEL[f"gm_{b}"] + W_SLOTS)
                if b == "c":
                    spread_sums(0)
                    key_sums(0)
                maxima(us[0])
                for n, u in enumerate(us):
                    ahead = b == "c" and u[1] == 1 and u[0] + 1 < 8
                    if ahead:
                        spread_sums(u[0] + 1)
                    if n + 1 < len(us):
                        maxima(us[n + 1])
                    weights(u)
                    if n % per == per - 1:
                        split_chunks(2 * FIRST_PANEL[f"gm_{b}"] + W_SLOTS + n // per)
                    values(u, u == us[-1])
                    if ahead:
                        key_sums(u[0] + 1)
                split_chunks(2 * FIRST_PANEL[f"gm_{b}"] + W_SLOTS + KC)
                if b == "a":
                    dve.wait_ge(S["ya_rstd"], 1)
                    rows = YT.rearrange("p t (h d) -> p t h d", d=P)
                    for t in range(TT):
                        at["step"] += 1
                        dve.tensor_tensor(rows[:, t], rows[:, t], spread(sm[:, 9, 4 * t:4 * t + 4], P), ALU.mult)\
                           .then_inc(dve_step, 1)
                    dve.wait_ge(dve_step, at["step"])
                    for t in range(TT):
                        ins = dve.tensor_tensor(YT[:, t, :], YT[:, t, :], BG[:, t, :], ALU.mult)
                    ins.then_inc(S["y_tm_ready"], 1)
                for j in range(4):
                    bank = wait_aux(dve, (B + "t", j))
                    free_aux(operand_lo(y_hi[:, j, :], y_lo[:, j, :], bank[:, :], y_hi_done, "yh",
                                        lam[:, 3:4] if b == "a" else None), (B + "t", j))
                for i, f in enumerate(UP_ORDER):
                    n0 = FIRST_PANEL[f"up_{b}"]
                    split_to(n0 + i // 4)
                    dve.wait_ge(S["gate_ready"], KC * (n_ + 1))
                    c = CHUNK0[n0] + i
                    bank = wait_chunk(dve, c)
                    m = MG[:, f, :]
                    if n_ == 0:
                        free_chunk(dve.tensor_tensor(m, bank[:, :], GATE[:, f, :], ALU.mult), c)
                    else:
                        free_chunk(dve.tensor_tensor(GATE[:, f, :], bank[:, :], GATE[:, f, :], ALU.mult), c)
                        chunk_read(dve, c)
                        dve.tensor_tensor(m, m, GATE[:, f, :], ALU.add).then_inc(S["merged_ready"], 1)
            split_to(FIRST_PANEL["w_o"])
            for f in UP_ORDER:
                operand_lo(x_hi[:, f, :], x_lo[:, f, :], MG[:, f, :], x_hi_done, "xh").then_inc(x_ready, 1)
            dve.wait_ge(S["reloaded"], 32)
            residual("w_o", sums=False)
            normalise(1, lambda k: h[:, k, :], lambda k: None, center=False)


def build_program(nc, shapes):
    t = {n: nc.dram_tensor(f"in_{n}_dram", s, F32, kind="ExternalInput").ap() for n, s in shapes}
    out = nc.dram_tensor("out_0_dram", (1, T, D), F32, kind="ExternalOutput").ap()
    w = {}
    for n, a in t.items():
        if n.startswith(("xa_w", "mlp_w")):
            for i in range(2):
                w[f"{n}{i}"] = a[i]
        elif n in ("ln_g", "ln_b", "final_gain_2"):
            w[n] = a
        else:
            w[n] = a[0]
    build(nc, w, out[0])


def kernel(**inputs):
    import numpy as _np
    import concourse.bacc as _bacc
    from concourse.bass_utils import run_bass_kernel_spmd as _run

    nc = _bacc.Bacc("TRN2", target_bir_lowering=False, num_devices=1)
    arrays = {f"in_{n}_dram": _np.ascontiguousarray(a) for n, a in inputs.items()}
    build_program(nc, [(n, a.shape) for n, a in inputs.items()])
    r = _run(nc, [arrays], core_ids=[0])
    return r.results[0]["out_0_dram"]
```

```python
from contextlib import ExitStack

import concourse.bass as bass
from concourse import mybir

F32 = mybir.dt.float32
F32R = mybir.dt.float32r
ALU = mybir.AluOpType
ACT = mybir.ActivationFunctionType
AX = mybir.AxisListType

P = 128
T = 512
TT = T // P
D = 1024
KC = D // P
PANEL = 256
LN_EPS = 1e-5
RMS_EPS = 1e-6
ALPHA = 4.0 ** 0.25
NEG = -1.0e30

CONV_W = 31
SSM_W = 4
SH = 16
SP_ = 64
XBC = 1536
XC = XBC // P

MEM = 256
XH = 4
GH = 4
GV = 256

RAW_SLOTS = 2
W_SLOTS = 4
LEAD = 3

FM, TM, TM_MEM, FM_MEM, UP = "fm", "tm", "tm_mem", "fm_mem", "up"


def weight_plan():
    plan = []

    def add(stage, weight, row, cols, kind):
        for c in cols:
            plan.append((stage, weight, row, c, kind))

    add("xbc", "even_w_in", 0, range(3 * D, 3 * D + XBC, PANEL), FM)
    for j in range(4):
        add("conv_in", "even_w_in", 0, [j * PANEL, D + j * PANEL], FM)
    add("z", "even_w_in", 0, range(2 * D, 3 * D, PANEL), TM)
    add("even_out_ssm", "even_w_out", D, range(0, D, PANEL), FM)
    add("even_out_conv", "even_w_out", 0, range(0, D, PANEL), FM)

    def attention(i):
        add(f"xk{i}", f"xa_w_k{i}", 0, range(0, D, PANEL), FM_MEM)
        add(f"xv{i}", f"xa_w_v{i}", 0, range(0, D, PANEL), TM_MEM)
        add(f"xq{i}", f"xa_w_q{i}", 0, range(0, D, PANEL), FM)
        add(f"xo{i}", f"xa_w_o{i}", 0, range(0, D, PANEL), FM)

    def mlp(i):
        for q in range(4):
            add(f"mlp{i}", f"mlp_w1{i}", 0, range(q * D, (q + 1) * D, PANEL), FM)
            add(f"mlp{i}", f"mlp_w2{i}", q * D, range(0, D, PANEL), FM)

    attention(0)
    mlp(0)
    add("gla_qk", "odd_w_in", 0, range(0, D, PANEL), FM)
    for hd in range(GH):
        add("gla_v", "odd_w_in", 0, [D + GV * hd], TM)
        add("gla_g", "odd_w_in", 0, [2 * D + GV * hd], TM)
    add("odd_out", "odd_w_out", 0, range(0, D, PANEL), FM)
    attention(1)
    mlp(1)
    base = dict(a=0, b=2048, c=3328, gm=5384)
    for n, b in enumerate("abc"):
        if b == "b":
            add("qk_b", "w_in_2q", 0, [base["b"], base["b"] + PANEL], FM)
            add("kv_b", "w_in_2", 0, [base["b"] + 512], "kv")
            add("g_b", "w_in_2", 0, [base["b"] + 768, base["b"] + 1024], TM)
        else:
            add(f"qk_{b}", "w_in_2", 0, range(base[b], base[b] + D, PANEL), FM)
            add(f"v_{b}", "w_in_2", 0, range(base[b] + D, base[b] + D + 512, PANEL), TM)
            g = base[b] + D + 512 + (8 if b == "c" else 0)
            add(f"g_{b}", "w_in_2", 0, range(g, g + 512, PANEL), TM)
        g = base["gm"] + n * D
        add(f"gm_{b}", "w_in_2", 0, range(g, g + D, PANEL), FM)
        add(f"up_{b}", f"w_up_{b}_2", 0, [0, 512], UP)
    add("w_o", "w_o_2", 0, range(0, D, PANEL), FM)
    return plan


PLAN = weight_plan()
NPANEL = len(PLAN)
FIRST_PANEL = {}
for _n, _p in enumerate(PLAN):
    FIRST_PANEL.setdefault(_p[0], _n)
CHUNKS = {FM: 2, TM: 2, FM_MEM: 2, TM_MEM: 1, UP: 4, "kv": 2}
PE_CONV = 3
DVE_CONV = KC - PE_CONV
CHUNK0, _c = [], 0
for _n, _p in enumerate(PLAN):
    if _n == FIRST_PANEL["even_out_ssm"]:
        CONV_CHUNK = _c
        _c += PE_CONV
    CHUNK0.append(_c)
    _c += CHUNKS[_p[4]]


def stage_chunk(name):
    return CHUNK0[FIRST_PANEL[name]]


AHEAD = dict(a=1, b=2, c=2)

def aux_plan():
    e = [("par", i) for i in range(4)] + [("x", k) for k in range(KC)] + [("dt",)]
    e += [("acs", 0)] + [("bc", 0, q) for q in range(4)]
    for c in range(TT):
        e += [("cb", c), ("xs", c, 0), ("xs", c, 1), ("bt", c)] + ([("acs", c + 1)] if c + 1 < TT else [])
        for g in range(2):
            e += [("yd", c, g)] + ([("yo", c, g)] if c else [])
        e += [("st", c, g) for g in range(2)]
        e += [("bc", c + 1, q) for q in range(4)] if c + 1 < TT else []
        e += [("yt", c, g) for g in range(2)]
    e += [("ln", "conv", i) for i in range(2)]

    def ln(name):
        return [("ln", name, i) for i in range(2)]

    def attention(i):
        out = [("mem", i, j) for j in range(4)]
        out += units("x" + str(i), range(TT), 2, 2)
        return out + [("xpv", i, j) for j in range(KC)]

    def units(name, us, ns, nt, pv=False):
        us = list(us)
        ahead = AHEAD.get(name.lower(), 1)
        out = [(name, "S", u, j) for u in us[:ahead] for j in range(ns)]
        for n, u in enumerate(us):
            if name == "C" and u[1] == 1 and u[0] + 1 < 8:
                out += [("cb_c", u[0] + 1)]
            turns = [(name, "T", u, j) for j in range(nt)]
            scores = [(name, "S", us[n + ahead], j) for j in range(ns)] if n + ahead < len(us) else []
            out += turns + scores if ahead == 2 else scores + turns
            if pv:
                out += [(name, "PV", u)]
        return out

    e += ln("m0") + attention(0) + ln("a0") + ln("f0")
    e += [("glow",), ("gate", 0), ("kend", 0)]
    for hd in range(GH):
        e += [("gate", hd + 1)] if hd + 1 < GH else []
        for t in range(TT):
            e += [("gatt", hd, t), ("gkv", hd, t, 0)] + ([("gkv", hd, t, 1)] if t + 1 < TT else [])
            e += [("go", hd, t - 1)] if t else [("gt", hd - 1, j) for j in range(2)] if hd else []
        e += [("go", hd, TT - 1)]
        e += [("kend", hd + 1)] if hd + 1 < GH else [("gt", hd, j) for j in range(2)]
    e += ln("m1") + attention(1) + ln("a1") + ln("f1")
    e += [("rms", 0)]
    e += units("A", [(hd, t) for hd in range(4) for t in range(TT)], 2, 1, True) + [("At", j) for j in range(4)]
    e += units("B", [(hd, t) for hd in range(4) for t in range(TT)], 2, 1, True) + [("Bt", j) for j in range(4)]
    e += [("fc",), ("cc",), ("cb_c", 0)]
    e += units("C", [(hd, t) for hd in range(8) for t in range(TT)], 1, 1, True) + [("Ct", j) for j in range(4)]
    e += [("rms", 1)] + [("out", t, j) for t in range(TT) for j in range(2)]
    return e


AUX_PLAN = aux_plan()
AUX = {key: n for n, key in enumerate(AUX_PLAN)}
assert len(AUX) == len(AUX_PLAN)

UNITS = ([("x0", t) for t in range(TT)] + [("x1", t) for t in range(TT)]
         + [("A", (hd, t)) for hd in range(4) for t in range(TT)]
         + [("B", (hd, t)) for hd in range(4) for t in range(TT)]
         + [("C", (hd, t)) for hd in range(8) for t in range(TT)])
UNIT = {key: n for n, key in enumerate(UNITS)}

X_FILLS = ["x", "m0", "a0", "f0", "m1", "a1", "rms", "merged"]
PARAMS = [(0, "ln_g", 48), (0, "ln_b", 48),
          (1, "even_conv_ln_g", 8), (1, "even_conv_ln_b", 8), (1, "even_conv_b", 8), (1, "even_ssm_conv_b", 12),
          (1, "even_ssm_norm_g", 8), (1, "odd_b_gate", 4), (1, "odd_head_norm_g", 2), (1, "norm_gain_2", 8),
          (1, "final_gain_2", 8), (1, "subln_gain_2", 1), (1, "even_ssm_conv_w", 48),
          (2, "even_conv_w", 124), (3, "even_conv_w", 124)]
PAR_AT, _rows = {}, [0, 0, 0, 0]
for _g, _name, _n in PARAMS:
    PAR_AT.setdefault(_name, (_g, _rows[_g]))
    _rows[_g] += _n
PAR_ROWS = _rows


def stage_end_chunk(name):
    last = max(n for n, p in enumerate(PLAN) if p[0] == name)
    return CHUNK0[last] + CHUNKS[PLAN[last][4]]

UP_ORDER = [4 * half + f for half in range(2) for f in (0, 2, 1, 3)]

Y_FILLS = [("conv", 8)] + [(f"hid{i}{q}", 8) for i in range(2) for q in range(4)]
Y0, _y = {}, 0
for _name, _n in Y_FILLS:
    Y0[_name] = _y
    _y += _n

GEMM_BANKS = 4
AUX_BANKS = 4
FIRST_TAPS = 42
PE_TAPS = -(-(PE_CONV * CONV_W - FIRST_TAPS) // (2 * TT))


def build(nc, w, out):
    with ExitStack() as ctx:
        sems = {}

        def sb(name, shape, dt=F32):
            return ctx.enter_context(nc.sbuf_tensor(name, shape, dt))

        def sem(name):
            sems[name] = ctx.enter_context(nc.semaphore(name))
            return sems[name]

        raw = sb("raw", [P, RAW_SLOTS, KC, PANEL])
        w_hi = sb("w_hi", [P, W_SLOTS, KC, P], F32R)
        w_lo = sb("w_lo", [P, W_SLOTS, KC, P], F32R)
        x_hi = sb("x_hi", [P, KC, T], F32R)
        x_lo = sb("x_lo", [P, KC, T], F32R)
        y_hi = sb("y_hi", [P, KC, T], F32R)
        y_lo = sb("y_lo", [P, KC, T], F32R)
        h = sb("h", [P, KC, T])
        WN = 18432
        work = sb("work", [P, WN])
        par = sb("par", [P, sum(PAR_ROWS)])
        ident = sb("ident", [P, P])
        triu = sb("triu", [P, P])
        ones = sb("ones", [P, P])
        w_small = sb("w_small", [P, KC, 16])
        row16 = sb("row16", [P, 3, SH])
        cst = sb("cst", [P, 4])
        mxs = sb("mxs", [P, 3, 4])
        rs = sb("rs", [P, 3, 4])
        sm = sb("sm", [P, 16, SH])
        gate2 = sb("gate2", [16, 512])
        lam = sb("lam", [P, 8])

        psum = [ctx.enter_context(nc.psum_tensor(f"gemm{i}", [P, 512], F32)) for i in range(GEMM_BANKS)]
        paux = [ctx.enter_context(nc.psum_tensor(f"aux{i}", [P, 512], F32)) for i in range(AUX_BANKS)]
        h_spill = nc.dram_tensor("h_spill", [P, KC * T], F32, kind="Internal").ap()

        raw_loaded = [sem(f"raw_loaded{i}") for i in range(RAW_SLOTS)]
        w_hi_ready, w_lo_ready = sem("w_hi_ready"), sem("w_lo_ready")
        chunk_done = sem("chunk_done")
        chunk_free = [sem(f"chunk_free{i}") for i in range(GEMM_BANKS)]
        aux_done = sem("aux_done")
        aux_free = [sem(f"aux_free{i}") for i in range(AUX_BANKS)]
        x_ready, y_ready = sem("x_ready"), sem("y_ready")
        x_hi_done, y_hi_done = sem("x_hi_done"), sem("y_hi_done")
        act_step, dve_step, pool_step = sem("act_step"), sem("dve_step"), sem("pool_step")
        stage_end = sem("stage_end")
        consts_ready = sem("consts_ready")
        names = ("par_loaded x_loaded small_loaded rows_loaded spilled reloaded mem_loaded lam_loaded out_sent "
                 "dt_abs dt_soft dta_ready seg_ready dte_ready decay_ready m_ready xdt_ready state_ready "
                 "conv_sum xbc_conv xbc_ready gated ssm_rstd y_gated sq_ready sum_in ln_var ln_rstd ln_xn "
                 "diag_ready tap_done h_ready ln_hi hid_relu unit_max unit_exp p_ready log_ready b_ready eb_ready qkt_ready s_ready s_read "
                 "gla_rstd o_ready lam_sum lam_ready ya_rstd gate_ready y_tm_ready c_abs c_soft merged_ready").split()
        S = {n: sem(n) for n in names}

        block = ctx.enter_context(nc.Block())

        def area(at, *shape):
            n = 1
            for s in shape:
                n *= s
            v = work[:, at:at + n]
            if len(shape) == 2:
                v = v.rearrange("p (a b) -> p a b", b=shape[1])
            elif len(shape) == 3:
                v = v.rearrange("p (a b c) -> p a b c", b=shape[1], c=shape[2])
            return v

        x_in = area(4336, TT, D)
        par_in = area(0, 4, P)
        U = area(0, KC, T + CONV_W - 1)
        XB = area(4336, XC, T + SSM_W - 1)
        TMP = area(10516, 2, T)
        CV = area(12820, 2, T)
        SG = area(13844, 2, T)
        DIAG = area(18040, 3, P)
        XS = area(11540, D)
        BT = area(12564, 2, P)
        M = area(12820, SH, P)
        XDT = area(14868, SH, SP_)
        XW = area(15892, SH, SP_)
        ST = area(16916, 2, T)
        LN = area(14848, 5, T)
        Z = h[:, :, :].rearrange("p a b -> p (a b)").rearrange("p (t n) -> p t n", n=D)
        XQ = area(0, KC, T)
        KT = area(4096, KC, MEM)
        VM = area(6144, 2, D)
        PR = area(8192, 2, XH * MEM)
        PTX = area(10240, 2, XH, T)
        mem_in = area(10240, 2, D)
        GQ = area(0, 4, T)
        GK = area(2048, 4, T)
        GVV = area(4096, 2, TT, GV)
        GG = area(6144, 2, TT, GV)
        GEB, GENB = [area(8192, T), area(12800, T)], [area(8704, T), area(13312, T)]
        GQE, GQO = [area(9216, T), area(13824, T)], [area(9728, T), area(14336, T)]
        GKT = [area(10240, TT, P), area(14848, TT, P)]
        GS = area(10752, 4, GV)
        GB = area(12288, T)
        GY = area(15360, TT, GV)
        GA = area(16640, 2, P)
        GL = area(16896, T)
        GMASK = area(17408, T)
        QK = area(0, KC, T)
        BV = area(4096, TT, T)
        BG = area(6144, TT, T)
        MG = area(8192, KC, T)
        LAMB = area(8192, 3 * P)
        YT = area(12288, TT, T)
        EX = area(14336, 2, 2, T)
        PT = area(16384, 2, T)
        GATE = h
        NC = area(17408, T)
        RB = area(17408, 2 * P)
        R = area(17920, T)

        def unit_slot(b, u):
            return UNIT[(b.upper(), u)] % (AHEAD[b] + 1)

        def unit_row(b, u):
            return (EX[:, 0, 0, :], EX[:, 1, 0, :], EX[:, 0, 1, :] if b == "b" else NC)[unit_slot(b, u)]

        def par_col(name, i=0):
            g, r = PAR_AT[name]
            at = sum(PAR_ROWS[:g]) + r + i
            return par[:, at:at + 1]

        def raw_value(n):
            return 16 * sum(2 if PLAN[m][4] == UP else 4 if PLAN[m][1] == "w_in_2q" else 1
                            for m in range(n % RAW_SLOTS, n + 1, RAW_SLOTS))

        def chunk_end(n):
            return CHUNK0[n] + CHUNKS[PLAN[n][4]]

        def wait_chunk(eng, c):
            eng.wait_ge(chunk_done, c + 1)
            return psum[c % GEMM_BANKS]

        def wait_aux(eng, key):
            eng.wait_ge(aux_done, AUX[key] + 1)
            return paux[AUX[key] % AUX_BANKS]

        def chunk_read(eng, c):
            eng.wait_ge(chunk_free[c % GEMM_BANKS], c // GEMM_BANKS + 1)

        def aux_read(eng, *key):
            eng.wait_ge(aux_free[AUX[key] % AUX_BANKS], AUX[key] // AUX_BANKS + 1)

        def wait_tap(eng, n):
            if n % CONV_W == CONV_W - 1:
                eng.wait_ge(chunk_done, CONV_CHUNK + n // CONV_W + 1)
            else:
                eng.wait_ge(S["tap_done"], n - n // CONV_W + 1)

        def free_chunk(ins, c):
            ins.then_inc(chunk_free[c % GEMM_BANKS], 1)

        def free_aux(ins, key):
            ins.then_inc(aux_free[AUX[key] % AUX_BANKS], 1)

        @block.sync
        def _(sp):
            def load(n):
                stage, name, row, col, kind = PLAN[n]
                s = n % RAW_SLOTS
                if n >= RAW_SLOTS:
                    sp.wait_ge(w_lo_ready, 2 * (n - RAW_SLOTS + 1))
                if kind == UP:
                    src = w[name][0:512, col:col + 512].rearrange("(k p) n -> p k n", p=P)
                    for half in range(2):
                        sp.dma_start(raw[:, s, 4 * half:4 * half + 4, :],
                                     src[:, :, half * PANEL:(half + 1) * PANEL]).then_inc(raw_loaded[s], 16)
                    return
                if name == "w_in_2q":
                    a = (col - 2048) // PANEL
                    src = w["w_in_2"][0:D, 2048:2560].rearrange("(k p) (g j d) -> p k j g d", p=P, g=2, d=64)
                    dst = raw[:, s, :, :].rearrange("p k (j g d) -> p k j g d", g=2, d=64)
                    for j in range(2):
                        for g in range(2):
                            ins = sp.dma_start(dst[:, :, j, g, :], src[:, :, 2 * a + j, g, :])
                            ins.then_inc(raw_loaded[s], 16)
                    return
                src = w[name][row:row + D, col:col + PANEL].rearrange("(k p) n -> p k n", p=P)
                sp.dma_start(raw[:, s, :, :], src).then_inc(raw_loaded[s], 16)

            for n in range(NPANEL):
                load(n)

        @block.gpsimd
        def _(pool):
            steps = [0]

            def step(ins):
                steps[0] += 1
                ins.then_inc(pool_step, 1)
                pool.wait_ge(pool_step, steps[0])

            pool.memset(ones[:, :], 1.0)
            pool.memset(cst[:, 0:1], LN_EPS)
            pool.memset(cst[:, 1:2], RMS_EPS)
            pool.memset(ident[:, :], 0.0)
            step(pool.memset(triu[:, :], 1.0))
            step(pool.affine_select(out=ident[:, :], in_=ident[:, :], compare_op=ALU.not_equal, fill=1.0, base=0,
                                    pattern=[[-1, P]], channel_multiplier=1))
            step(pool.affine_select(out=triu[:, :], in_=triu[:, :], compare_op=ALU.is_ge, fill=0.0, base=0,
                                    pattern=[[1, P]], channel_multiplier=-1))
            pool.drain().then_inc(consts_ready, 1)
            aux_read(pool, "par", 3)
            for n in range(PE_CONV * CONV_W):
                f, i = DVE_CONV + n // CONV_W, n % CONV_W
                if n >= 3:
                    wait_tap(pool, n - 3)
                pool.tensor_scalar(DIAG[:, n % 3, :], ident[:, :], par_col("even_conv_w", i * KC + f), None, ALU.mult)\
                    .then_inc(S["diag_ready"], 1)
            pool.wait_ge(S["o_ready"], GH)
            step(pool.iota(R, [[1, T]], base=-384, channel_multiplier=-1, allow_small_or_imprecise_dtypes=True))
            step(pool.affine_select(out=R, in_=R, compare_op=ALU.is_ge, fill=NEG, base=384,
                                    pattern=[[-1, T]], channel_multiplier=1))
            step(pool.tensor_copy(RB, R[:, 256:512]))
            step(pool.affine_select(out=RB[:, 0:P], in_=RB[:, 0:P], compare_op=ALU.is_ge, fill=NEG, base=-1,
                                    pattern=[[1, P]], channel_multiplier=-1))
            pool.drain().then_inc(consts_ready, 1)

        @block.tensor
        def _(pe):
            at = dict(panel=0, chunk=0, aux=0, end=0, tap=0, conv=None, gate=0, dst=None)

            def stage_barrier():
                at["end"] += 1
                pe.drain().then_inc(stage_end, 1)
                pe.wait_ge(stage_end, 3 * at["end"])

            def next_chunk():
                c = at["chunk"]
                if c >= GEMM_BANKS:
                    pe.wait_ge(chunk_free[c % GEMM_BANKS], c // GEMM_BANKS)
                at["chunk"] += 1
                return psum[c % GEMM_BANKS]

            def next_aux(*key):
                a = at["aux"]
                assert AUX_PLAN[a] == key, (AUX_PLAN[a], key)
                if a >= AUX_BANKS:
                    pe.wait_ge(aux_free[a % AUX_BANKS], a // AUX_BANKS)
                at["aux"] += 1
                return paux[a % AUX_BANKS]

            def w_ready(upto):
                pe.wait_ge(w_lo_ready, upto)

            def product3(dst, a_hi, a_lo, b_hi, b_lo, first, last):
                pe.matmul(dst, a_hi, b_hi, start=first, stop=False)
                pe.matmul(dst, a_hi, b_lo, start=False, stop=False)
                return pe.matmul(dst, a_lo, b_hi, start=False, stop=last)

            def gemm(stage, hi, lo, ready=None, panels=None, wide=False):
                n0 = at["panel"]
                n1 = n0 + panels if panels else n0 + sum(1 for p in PLAN if p[0] == stage)
                seen = [0]

                def operand(k):
                    if ready is not None and k >= seen[0]:
                        ready(k)
                        seen[0] = k + 1

                if wide:
                    w_ready(2 * n0 + 4)
                    dst = [next_chunk() for _ in range(4)]
                    for k in range(KC):
                        operand(k)
                        for i in range(4):
                            s = (2 * n0 + i) % W_SLOTS
                            ins = product3(dst[i][:, :], w_hi[:, s, k, :], w_lo[:, s, k, :], hi[:, k, :], lo[:, k, :],
                                           k == 0, k == KC - 1)
                            if k == KC - 1:
                                ins.then_inc(chunk_done, 1)
                for n in range(n0 + 2 if wide else n0, n1):
                    kind = PLAN[n][4]
                    assert PLAN[n][0] == stage
                    if kind in (FM, FM_MEM):
                        cols = T if kind == FM else MEM
                        for s in (2 * n, 2 * n + 1):
                            w_ready(s + 1)
                            dst = next_chunk()
                            for k in range(KC):
                                operand(k)
                                ins = product3(dst[:, 0:cols], w_hi[:, s % W_SLOTS, k, :], w_lo[:, s % W_SLOTS, k, :],
                                               hi[:, k, 0:cols], lo[:, k, 0:cols], k == 0, k == KC - 1)
                            ins.then_inc(chunk_done, 1)
                    elif kind in (TM, TM_MEM):
                        w_ready(2 * n + 2)
                        a = 2 * n % W_SLOTS
                        for t2 in range(2 if kind == TM else 1):
                            dst = next_chunk()
                            for t in range(2):
                                tok = slice((2 * t2 + t) * P, (2 * t2 + t + 1) * P)
                                for k in range(KC):
                                    operand(k)
                                    ins = product3(dst[:, t * PANEL:(t + 1) * PANEL], hi[:, k, tok], lo[:, k, tok],
                                                   w_hi[:, a:a + 2, k, :], w_lo[:, a:a + 2, k, :],
                                                   k == 0, k == KC - 1)
                            ins.then_inc(chunk_done, 1)
                    elif kind == UP:
                        for s in (2 * n, 2 * n + 1):
                            w_ready(s + 1)
                            for half in range(2):
                                dst = next_chunk()
                                for k in range(4):
                                    operand(k)
                                    kk = 4 * half + k
                                    ins = product3(dst[:, :], w_hi[:, s % W_SLOTS, kk, :], w_lo[:, s % W_SLOTS, kk, :],
                                                   hi[:, k, :], lo[:, k, :], k == 0, k == 3)
                                ins.then_inc(chunk_done, 1)
                    else:
                        w_ready(2 * n + 2)
                        a = 2 * n % W_SLOTS
                        dst = next_chunk()
                        for k in range(KC):
                            ins = product3(dst[:, :], w_hi[:, a, k, :], w_lo[:, a, k, :], hi[:, k, :], lo[:, k, :],
                                           k == 0, k == KC - 1)
                        ins.then_inc(chunk_done, 1)
                        dst = next_chunk()
                        for t in range(TT):
                            tok = slice(t * P, (t + 1) * P)
                            for k in range(KC):
                                ins = product3(dst[:, tok], hi[:, k, tok], lo[:, k, tok], w_hi[:, a + 1, k, :],
                                               w_lo[:, a + 1, k, :], k == 0, k == KC - 1)
                        ins.then_inc(chunk_done, 1)
                at["panel"] = n1

            def turn(dst, src):
                return pe.transpose(dst, src, ident[0:src.shape[0], 0:src.shape[0]])

            def layer_sums(name, n):
                pe.wait_ge(S["sum_in"], KC * (n + 1))
                for i in range(2):
                    pe.matmul(next_aux("ln", name, i)[:, :], ones[:, :], LN[:, 3 + i, :], start=True, stop=True)\
                      .then_inc(aux_done, 1)

            def x_fill(name):
                return dict(ready=lambda k: pe.wait_ge(x_ready, KC * X_FILLS.index(name) + k + 1))

            def y_fill(name):
                return dict(ready=lambda k: pe.wait_ge(y_ready, Y0[name] + k + 1))

            pe.wait_ge(consts_ready, 1)
            pe.wait_ge(S["par_loaded"], 16 * len(PARAMS))
            for g in range(4):
                turn(next_aux("par", g)[:, 0:PAR_ROWS[g]], par_in[0:PAR_ROWS[g], g, :]).then_inc(aux_done, 1)
            pe.wait_ge(S["x_loaded"], 16)
            for k in range(KC):
                dst = next_aux("x", k)
                for t in range(TT):
                    ins = turn(dst[:, t * P:(t + 1) * P], x_in[:, t, k * P:(k + 1) * P])
                ins.then_inc(aux_done, 1)
            stage_barrier()

            pe.wait_ge(S["small_loaded"], 16)
            dst = next_aux("dt")
            for t in range(TT):
                for k in range(KC):
                    ins = pe.matmul(dst[:, SH * t:SH * (t + 1)], h[:, k, t * P:(t + 1) * P], w_small[:, k, :],
                                    start=(k == 0), stop=(k == KC - 1))
            ins.then_inc(aux_done, 1)
            gemm("xbc", x_hi, x_lo, **x_fill("x"))
            gemm("conv_in", x_hi, x_lo)
            gemm("z", x_hi, x_lo)

            def convolve(upto):
                while at["tap"] < min(upto, PE_CONV * CONV_W):
                    n = at["tap"]
                    f, i = DVE_CONV + n // CONV_W, n % CONV_W
                    if i == 0:
                        at["conv"] = next_chunk()
                        chunk_read(pe, stage_chunk("conv_in") + 4 * (f // 2) + f % 2)
                    pe.wait_ge(S["diag_ready"], n + 1)
                    ins = pe.matmul(at["conv"][:, :], DIAG[:, n % 3, :], U[:, f, i:i + T], start=(i == 0),
                                    stop=(i == CONV_W - 1))
                    ins.then_inc(chunk_done if i == CONV_W - 1 else S["tap_done"], 1)
                    at["tap"] += 1

            def running_sums(c):
                pe.wait_ge(S["dta_ready"], 1)
                pe.matmul(next_aux("acs", c)[:, 0:SH], triu[:, :], sm[:, c, :], start=True, stop=True)\
                  .then_inc(aux_done, 1)

            def sums_as_rows(c):
                for q in range(4):
                    dst = next_aux("bc", c, q)
                    for j in range(4):
                        hd = 4 * q + j
                        ins = pe.matmul(dst[:, j * P:(j + 1) * P], sm[:, c, hd:hd + 1].broadcast_to([P, P]),
                                        triu[:, :], start=True, stop=True)
                    ins.then_inc(aux_done, 1)

            convolve(FIRST_TAPS)
            running_sums(0)
            sums_as_rows(0)
            for c in range(TT):
                tok = slice(SSM_W - 1 + c * P, SSM_W - 1 + (c + 1) * P)
                if c == 0:
                    pe.wait_ge(S["xbc_ready"], XC)
                dst = next_aux("cb", c)
                for g in range(2):
                    ins = pe.matmul(dst[:, g * P:(g + 1) * P], XB[:, 8 + g, tok], XB[:, 10 + g, tok],
                                    start=True, stop=True)
                ins.then_inc(aux_done, 1)
                for half in range(2):
                    dst = next_aux("xs", c, half)
                    for j in range(4):
                        ins = turn(dst[:, j * P:(j + 1) * P], XB[:, 4 * half + j, tok])
                    ins.then_inc(aux_done, 1)
                dst = next_aux("bt", c)
                for g in range(2):
                    ins = turn(dst[:, g * P:(g + 1) * P], XB[:, 8 + g, tok])
                ins.then_inc(aux_done, 1)
                if c + 1 < TT:
                    running_sums(c + 1)
                convolve(at["tap"] + PE_TAPS)
                pe.wait_ge(S["m_ready"], c + 1)
                pe.wait_ge(S["xdt_ready"], c + 1)
                aux_read(pe, "bt", c)
                if c:
                    pe.wait_ge(S["state_ready"], c)
                for g in range(2):
                    dst = next_aux("yd", c, g)
                    for j in range(8):
                        ins = pe.matmul(dst[:, 64 * j:64 * j + 64], M[:, 8 * g + j, :], XDT[:, 8 * g + j, :],
                                        start=True, stop=True)
                    ins.then_inc(aux_done, 1)
                    if c:
                        pe.matmul(next_aux("yo", c, g)[:, :], XB[:, 10 + g, tok], ST[:, g, :], start=True, stop=True)\
                          .then_inc(aux_done, 1)
                for g in range(2):
                    pe.matmul(next_aux("st", c, g)[:, :], BT[:, g, :], XW[:, 8 * g:8 * g + 8, :],
                              start=True, stop=True).then_inc(aux_done, 1)
                if c + 1 < TT:
                    sums_as_rows(c + 1)
                convolve(at["tap"] + PE_TAPS)
                pe.wait_ge(S["y_gated"], c + 1)
                yv = XDT.rearrange("p a b -> p (a b)")
                for g in range(2):
                    dst = next_aux("yt", c, g)
                    for j in range(4):
                        ins = turn(dst[:, j * P:(j + 1) * P], yv[:, (4 * g + j) * P:(4 * g + j + 1) * P])
                    ins.then_inc(aux_done, 1)
            gemm("even_out_ssm", x_hi, x_lo, panels=2, ready=lambda k: aux_read(pe, "yt", TT - 1, k // 4))
            layer_sums("conv", 0)
            gemm("even_out_ssm", x_hi, x_lo, panels=2)
            gemm("even_out_conv", y_hi, y_lo, **y_fill("conv"))
            layer_sums("m0", 1)

            def cross_attention(i):
                pe.wait_ge(S["mem_loaded"], 16 * (i + 1))
                for e in range(4):
                    dst = next_aux("mem", i, e)
                    for kk in range(2):
                        for t in range(2):
                            k = 2 * e + kk
                            ins = turn(dst[:, kk * MEM + t * P:kk * MEM + (t + 1) * P], mem_in[:, t, k * P:(k + 1) * P])
                    ins.then_inc(aux_done, 1)
                gemm(f"xk{i}", y_hi, y_lo, ready=lambda k: aux_read(pe, "mem", i, k // 2))
                gemm(f"xv{i}", y_hi, y_lo)
                gemm(f"xq{i}", x_hi, x_lo, **x_fill(f"m{i}"))
                chunk_read(pe, stage_end_chunk(f"xq{i}") - 1)
                name = f"x{i}"

                def scores(t):
                    for e in range(2):
                        dst = next_aux(name, "S", t, e)
                        for hh in range(2):
                            for d in range(2):
                                k = 2 * (2 * e + hh) + d
                                ins = pe.matmul(dst[:, hh * MEM:(hh + 1) * MEM], XQ[:, k, t * P:(t + 1) * P],
                                                KT[:, k, :], start=(d == 0), stop=(d == 1))
                        ins.then_inc(aux_done, 1)

                scores(0)
                for t in range(TT):
                    if t + 1 < TT:
                        scores(t + 1)
                    pe.wait_ge(S["p_ready"], UNIT[(name, t)] + 1)
                    for m in range(2):
                        dst = next_aux(name, "T", t, m)
                        for hd in range(XH):
                            ins = turn(dst[:, hd * P:(hd + 1) * P],
                                       PR[:, t % 2, hd * MEM + m * P:hd * MEM + (m + 1) * P])
                        ins.then_inc(aux_done, 1)
                aux_read(pe, name, "T", TT - 1, 1)
                for j in range(KC):
                    dst = next_aux("xpv", i, j)
                    for m in range(2):
                        ins = pe.matmul(dst[:, :], VM[:, m, j * P:(j + 1) * P], PTX[:, m, j // 2, :],
                                        start=(m == 0), stop=(m == 1))
                    ins.then_inc(aux_done, 1)
                gemm(f"xo{i}", x_hi, x_lo, ready=lambda k: aux_read(pe, "xpv", i, k))
                layer_sums(f"a{i}", 2 + 3 * i)

            def mlp(i):
                for q in range(4):
                    gemm(f"mlp{i}", x_hi, x_lo, panels=4, wide=(q == 0), **x_fill(f"a{i}"))
                    gemm(f"mlp{i}", y_hi, y_lo, panels=4, **y_fill(f"hid{i}{q}"))
                layer_sums(f"f{i}", 3 + 3 * i)

            cross_attention(0)
            mlp(0)

            pe.wait_ge(S["small_loaded"], 32)
            gemm("gla_qk", x_hi, x_lo, wide=True, **x_fill("f0"))
            dst = next_aux("glow")
            for k in range(KC):
                ins = pe.matmul(dst[0:16, :], w_small[:, k, :], h[:, k, :], start=(k == 0), stop=(k == KC - 1))
            ins.then_inc(aux_done, 1)

            def gate(hd):
                pe.matmul(next_aux("gate", hd)[:, :], gate2[:, hd * P:(hd + 1) * P], GL[0:16, :],
                          start=True, stop=True).then_inc(aux_done, 1)

            def keys_to_end(hd):
                pe.wait_ge(S["qkt_ready"], hd + 1)
                dst = next_aux("kend", hd)
                for t in range(TT):
                    ins = turn(dst[:, t * P:(t + 1) * P], GK[:, hd, t * P:(t + 1) * P])
                ins.then_inc(aux_done, 1)

            def turned_head(hd):
                pe.wait_ge(S["o_ready"], hd + 1)
                for j in range(2):
                    dst = next_aux("gt", hd, j)
                    for t in range(TT):
                        ins = turn(dst[:, t * P:(t + 1) * P], GY[:, t, j * P:(j + 1) * P])
                    ins.then_inc(aux_done, 1)

            def value_gate_products(hd, upto):
                while hd < GH and at["gate"] < upto:
                    i, step_ = at["gate"] // 16, at["gate"] % 16
                    t, k = step_ // KC, step_ % KC
                    n = FIRST_PANEL["gla_v"] + 2 * hd + i // 2
                    tok = slice((2 * (i % 2) + t) * P, (2 * (i % 2) + t + 1) * P)
                    if step_ == 0:
                        w_ready(2 * n + 2)
                        at["dst"] = next_chunk()
                    a = 2 * n % W_SLOTS
                    ins = product3(at["dst"][:, t * GV:(t + 1) * GV], x_hi[:, k, tok], x_lo[:, k, tok],
                                   w_hi[:, a:a + 2, k, :], w_lo[:, a:a + 2, k, :], k == 0, k == KC - 1)
                    if step_ == 15:
                        ins.then_inc(chunk_done, 1)
                    at["gate"] += 1

            def tile_products(hd, t):
                e, tok = hd % 2, slice(t * P, (t + 1) * P)
                pe.matmul(next_aux("gatt", hd, t)[:, 0:P], GENB[e][:, tok], GQ[:, hd, tok], start=True, stop=True)\
                  .then_inc(aux_done, 1)
                if t == 0:
                    aux_read(pe, "kend", hd)
                    chunk_read(pe, stage_chunk("gla_v") + 4 * hd + 1)
                for half in range(2 if t + 1 < TT else 1):
                    a, b = 64 * half, 64 * half + 64
                    pe.matmul(next_aux("gkv", hd, t, half)[:, 0:GV], GKT[e][a:b, t, :], GVV[a:b, e, t, :],
                              start=True, stop=True).then_inc(aux_done, 1)

            def tile_output(hd, t):
                e, tok = hd % 2, slice(t * P, (t + 1) * P)
                aux_read(pe, "gatt", hd, t)
                dst = next_aux("go", hd, t)
                pe.matmul(dst[:, 0:GV], GA[:, t % 2, :], GVV[:, e, t, :], start=True, stop=False)
                if t:
                    aux_read(pe, "gkv", hd, t - 1, 1)
                    pe.matmul(dst[:, 0:GV], GQE[e][:, tok], GS[:, 2 * t % 4, :], start=False, stop=False)
                aux_read(pe, "gkv", hd, t, 0)
                pe.matmul(dst[:, 0:GV], GQO[e][:, tok], GS[:, (2 * t + 1) % 4, :], start=False, stop=True)\
                  .then_inc(aux_done, 1)

            aux_read(pe, "glow")
            gate(0)
            gemm("gla_v", x_hi, x_lo, panels=1)
            gemm("gla_g", x_hi, x_lo, panels=1)
            keys_to_end(0)
            for hd in range(GH):
                at["gate"] = 0
                if hd + 1 < GH:
                    gate(hd + 1)
                for t in range(TT):
                    tile_products(hd, t)
                    value_gate_products(hd + 1, 16 * t + 10)
                    if t:
                        tile_output(hd, t - 1)
                    elif hd:
                        turned_head(hd - 1)
                    value_gate_products(hd + 1, 16 * t + 16)
                tile_output(hd, TT - 1)
                if hd + 1 < GH:
                    at["panel"] += 2
                    keys_to_end(hd + 1)
            turned_head(GH - 1)
            gemm("odd_out", y_hi, y_lo, ready=lambda k: aux_read(pe, "gt", k // 2, k % 2))
            layer_sums("m1", 4)
            cross_attention(1)
            mlp(1)

            def square_sum(i):
                pe.wait_ge(S["sum_in"], KC * (7 + i + 1))
                pe.matmul(next_aux("rms", i)[:, :], ones[:, :], LN[:, 4, :], start=True, stop=True)\
                  .then_inc(aux_done, 1)

            def gate_products(b, upto):
                while at["gate"] < upto:
                    f, k = at["gate"] // KC, at["gate"] % KC
                    s = 2 * FIRST_PANEL[f"gm_{b}"] + f
                    if k == 0:
                        w_ready(s + 1)
                        at["dst"] = next_chunk()
                    ins = product3(at["dst"][:, :], w_hi[:, s % W_SLOTS, k, :], w_lo[:, s % W_SLOTS, k, :],
                                   x_hi[:, k, :], x_lo[:, k, :], k == 0, k == KC - 1)
                    if k == KC - 1:
                        ins.then_inc(chunk_done, 1)
                    at["gate"] += 1

            def units(b, us, scores, turns, values, before=lambda u: None):
                name = b.upper()
                at["gate"] = 0
                for u in us[:AHEAD[b]]:
                    scores(u)
                for n, u in enumerate(us):
                    before(u)
                    if b == "a":
                        if n + 1 < len(us):
                            scores(us[n + 1])
                        gate_products(b, KC * KC * (2 * n + 1) // (2 * len(us)))
                        pe.wait_ge(S["p_ready"], UNIT[(name, u)] + 1)
                    else:
                        pe.wait_ge(S["unit_exp"], UNIT[(name, u)] - 2 * TT + 1)
                    turns(u, next_aux(name, "T", u, 0)).then_inc(aux_done, 1)
                    if b != "a" and n + 2 < len(us):
                        scores(us[n + 2])
                    gate_products(b, KC * KC * (n + 1) // len(us))
                    aux_read(pe, name, "T", u, 0)
                    values(u, next_aux(name, "PV", u)).then_inc(aux_done, 1)
                at["panel"] += 4

            def turned_output(name, b, n):
                pe.wait_ge(S["y_tm_ready"], n + 1)
                for j in range(4):
                    dst = next_aux(name, j)
                    for t in range(TT):
                        ins = turn(dst[:, t * P:(t + 1) * P], YT[:, t, j * P:(j + 1) * P])
                    ins.then_inc(aux_done, 1)
                gemm(f"up_{b}", y_hi, y_lo, ready=lambda k: aux_read(pe, name, k))

            square_sum(0)
            gemm("qk_a", x_hi, x_lo, wide=True, **x_fill("rms"))
            gemm("v_a", x_hi, x_lo)
            gemm("g_a", x_hi, x_lo)
            chunk_read(pe, stage_end_chunk("g_a") - 1)

            def scores_a(u):
                hd, t = u
                for m in range(2):
                    a = 64 * m
                    pe.matmul(next_aux("A", "S", u, m)[:, 0:(t + 1) * P], QK[a:a + 64, hd, t * P:(t + 1) * P],
                              QK[a:a + 64, 4 + hd, 0:(t + 1) * P], start=True, stop=True).then_inc(aux_done, 1)

            def turns_a(u, dst):
                e = UNIT[("A", u)] % 2
                for kt in range(u[1] + 1):
                    ins = turn(dst[:, kt * P:(kt + 1) * P], EX[:, e, 0, kt * P:(kt + 1) * P])
                return ins

            def values_a(u, dst):
                hd, t = u
                e = UNIT[("A", u)] % 2
                for kt in range(t + 1):
                    ins = pe.matmul(dst[:, 0:P], PT[:, e, kt * P:(kt + 1) * P], BV[:, kt, hd * P:(hd + 1) * P],
                                    start=(kt == 0), stop=(kt == t))
                return ins

            units("a", [(hd, t) for hd in range(4) for t in range(TT)], scores_a, turns_a, values_a)
            turned_output("At", "a", 0)

            gemm("qk_b", x_hi, x_lo)
            gemm("kv_b", x_hi, x_lo)
            gemm("g_b", x_hi, x_lo)
            chunk_read(pe, stage_end_chunk("g_b") - 1)

            def scores_b(u):
                j, t = u
                for g in range(2):
                    a = 64 * g
                    lo_key = max(t - 1, 0) * P
                    off = P if t == 0 else 0
                    pe.matmul(next_aux("B", "S", u, g)[:, off:256], QK[a:a + 64, j, t * P:(t + 1) * P],
                              QK[a:a + 64, 4, lo_key:(t + 1) * P], start=True, stop=True).then_inc(aux_done, 1)

            def turns_b(u, dst):
                row = unit_row("b", u)
                for g in range(2):
                    for kk in range(1 if u[1] == 0 else 0, 2):
                        s = slice(g * 256 + kk * P, g * 256 + (kk + 1) * P)
                        ins = turn(dst[:, s], row[:, s])
                return ins

            def values_b(u, dst):
                j, t = u
                e = UNIT[("B", u)] % 2
                for g in range(2):
                    for kk in range(1 if t == 0 else 0, 2):
                        s = slice(g * 256 + kk * P, g * 256 + (kk + 1) * P)
                        ins = pe.matmul(dst[:, g * 64:(g + 1) * 64], PT[:, e, s],
                                        BV[:, t - 1 + kk, g * 64:(g + 1) * 64],
                                        start=(kk == (1 if t == 0 else 0)), stop=(kk == 1))
                return ins

            units("b", [(hd, t) for hd in range(4) for t in range(TT)], scores_b, turns_b, values_b)
            turned_output("Bt", "b", 1)

            gemm("qk_c", x_hi, x_lo)
            gemm("v_c", x_hi, x_lo)
            pe.wait_ge(S["small_loaded"], 48)
            dst = next_aux("fc")
            for t in range(TT):
                for k in range(KC):
                    for part in range(2):
                        xx = (x_hi, x_lo)[part][:, k, t * P:(t + 1) * P].bitcast(F32)
                        ins = pe.matmul(dst[:, 8 * t:8 * t + 8], xx, w_small[:, k, 0:8],
                                        start=(k == 0 and part == 0), stop=(k == KC - 1 and part == 1))
            ins.then_inc(aux_done, 1)
            gemm("g_c", x_hi, x_lo)
            chunk_read(pe, stage_end_chunk("g_c") - 1)
            pe.wait_ge(S["log_ready"], GH + 1)
            dst = next_aux("cc")
            for t in range(TT):
                for s in range(t + 1):
                    ins = pe.matmul(dst[:, 8 * t:8 * t + 8], (triu if s == t else ones)[:, :], sm[:, s, 0:8],
                                    start=(s == 0), stop=(s == t))
            ins.then_inc(aux_done, 1)

            def scores_c(u):
                hd, t = u
                a = 64 * (hd % 2)
                pe.matmul(next_aux("C", "S", u, 0)[:, 0:(t + 1) * P], QK[a:a + 64, hd // 2, t * P:(t + 1) * P],
                          QK[a:a + 64, 4 + hd // 2, 0:(t + 1) * P], start=True, stop=True).then_inc(aux_done, 1)

            def turns_c(u, dst):
                row = unit_row("c", u)
                for kt in range(u[1] + 1):
                    ins = turn(dst[:, kt * P:(kt + 1) * P], row[:, kt * P:(kt + 1) * P])
                return ins

            def values_c(u, dst):
                hd, t = u
                e = UNIT[("C", u)] % 2
                for kt in range(t + 1):
                    ins = pe.matmul(dst[:, 0:64], PT[:, e, kt * P:(kt + 1) * P], BV[:, kt, hd * 64:(hd + 1) * 64],
                                    start=(kt == 0), stop=(kt == t))
                return ins

            def key_sums(hd):
                dst = next_aux("cb_c", hd)
                for t in range(TT):
                    for s in range(t + 1):
                        ins = pe.matmul(dst[:, t * P:(t + 1) * P], sm[:, s, hd:hd + 1].broadcast_to([P, P]),
                                        (triu if s == t else ones)[:, :], start=(s == 0), stop=(s == t))
                ins.then_inc(aux_done, 1)

            def next_key_sums(u):
                if u[1] == 1 and u[0] + 1 < 8:
                    key_sums(u[0] + 1)

            key_sums(0)
            units("c", [(hd, t) for hd in range(8) for t in range(TT)], scores_c, turns_c, values_c, next_key_sums)
            turned_output("Ct", "c", 2)
            gemm("w_o", x_hi, x_lo, wide=True, ready=lambda k: pe.wait_ge(x_ready, KC * X_FILLS.index("merged") +
                                                                         UP_ORDER.index(k) + 1))
            square_sum(1)
            pe.wait_ge(S["h_ready"], KC * 9)
            for t in range(TT):
                for j in range(2):
                    dst = next_aux("out", t, j)
                    for k in range(4):
                        ins = turn(dst[:, k * P:(k + 1) * P], MG[:, 4 * j + k, t * P:(t + 1) * P])
                    ins.then_inc(aux_done, 1)
            assert at["panel"] == NPANEL and at["aux"] == len(AUX_PLAN)

        @block.scalar
        def _(act):
            at = dict(step=0, split=0, end=0, ln=0, sq=0, hr=0, xh=0, yh=0)

            def step(ins):
                at["step"] += 1
                ins.then_inc(act_step, 1)
                act.wait_ge(act_step, at["step"])

            def stage_barrier():
                at["end"] += 1
                act.drain().then_inc(stage_end, 1)
                act.wait_ge(stage_end, 3 * at["end"])

            def split_chunk():
                s = at["split"]
                if s < 2 * NPANEL:
                    n = s // 2
                    act.wait_ge(raw_loaded[n % RAW_SLOTS], raw_value(n))
                    if s >= W_SLOTS:
                        done = (s - W_SLOTS) // 2
                        if PLAN[done][4] in (FM, FM_MEM):
                            act.wait_ge(chunk_done, CHUNK0[done] + (s % 2) + 1)
                        else:
                            act.wait_ge(chunk_done, chunk_end(done))
                    act.activation(w_hi[:, s % W_SLOTS, :, :], raw[:, n % RAW_SLOTS, :, (s % 2) * P:(s % 2 + 1) * P],
                                   ACT.Copy).then_inc(w_hi_ready, 1)
                    at["split"] += 1

            def split_to(panel):
                while at["split"] < min(2 * panel + 2, 2 * NPANEL):
                    split_chunk()

            def split_more():
                split_to(at["split"] // 2)

            def split_chunks(upto):
                while at["split"] < upto:
                    split_chunk()

            def operand_hi(dst, src, done, scale=1.0):
                act.activation(dst, src, ACT.Identity, scale=scale).then_inc(done, 1)

            def squares(src, waits):
                for k in range(KC):
                    waits(k)
                    if at["sq"] % KC >= 2:
                        act.wait_ge(S["sum_in"], at["sq"] - 1)
                    act.activation(LN[:, k % 2, :], src(k), ACT.Square).then_inc(S["sq_ready"], 1)
                    at["sq"] += 1

            def logs():
                act.preload_act_table_set("natural_log_exp_and_others")

            def normalised(dst, gain, bias, func=ACT.Identity, eps=0, rms=False, hi=None, more=True):
                n = at["ln"]
                if more:
                    split_more()
                logs()
                act.wait_ge(S["ln_var"], n + 1)
                step(act.activation(LN[:, 2, :], LN[:, 1, :], ACT.Ln, bias=cst[:, eps:eps + 1]))
                act.activation(LN[:, 2, :], LN[:, 2, :], ACT.Exp, scale=-0.5).then_inc(S["ln_rstd"], 1)
                at["ln"] += 1
                for k in range(KC):
                    act.wait_ge(S["ln_xn"], KC * n + k + 1)
                    if rms:
                        act.activation(dst(k), LN[:, 3 + k % 2, :], func, scale=gain(k)).then_inc(S["h_ready"], 1)
                    else:
                        act.activation(dst(k), LN[:, 3 + k % 2, :], func, bias=bias(k), scale=gain(k))\
                           .then_inc(S["h_ready"], 1)
                    if hi is not None and k:
                        act.wait_ge(S["h_ready"], KC * n + k)
                        act.activation(hi[:, k - 1, :], dst(k - 1), ACT.Copy).then_inc(S["ln_hi"], 1)
                if hi is not None:
                    act.wait_ge(S["h_ready"], KC * (n + 1))
                    act.activation(hi[:, KC - 1, :], dst(KC - 1), ACT.Copy).then_inc(S["ln_hi"], 1)

            def residual_squares(stage, half=0, panels=4):
                def waits(k):
                    n = FIRST_PANEL[stage] + half + k // 2
                    if k % 2 == 0:
                        split_to(n + 1)
                    chunk_read(act, CHUNK0[n] + k % 2)
                squares(lambda k: h[:, k, :], waits)

            def ln_cols(i, j):
                r = (3 * i + j) * KC
                return (lambda k: par_col("ln_g", r + k)), (lambda k: par_col("ln_b", r + k))

            def layer_norm(i, j):
                g, b = ln_cols(i, j)
                normalised(lambda k: h[:, k, :], g, b, hi=None if (i, j) == (1, 2) else x_hi, more=(i, j) != (1, 2))

            count = [0, 0, 0, 0]
            for g, name, n in PARAMS:
                src = w[name]
                if name == "even_conv_w":
                    src = src.rearrange("w (c p) -> (w c) p", p=P)
                    src = src[0:124, :] if g == 2 else src[124:248, :]
                elif name == "even_ssm_conv_w":
                    src = src.rearrange("w (c p) -> (w c) p", p=P)
                elif name in ("ln_g", "ln_b"):
                    src = src.rearrange("i j (c p) -> (i j c) p", p=P)
                else:
                    src = src.rearrange("(c p) -> c p", p=P)
                act.dma_start(par_in[count[g]:count[g] + n, g, :], src).then_inc(S["par_loaded"], 16)
                count[g] += n
            act.dma_start(x_in, w["x"].rearrange("(t p) n -> p t n", p=P)).then_inc(S["x_loaded"], 16)
            act.dma_start(w_small[:, :, :], w["even_w_in"][:, 4608:4624].rearrange("(k p) n -> p k n", p=P))\
               .then_inc(S["small_loaded"], 16)
            for i, name in enumerate(("even_dt_bias", "even_a_log", "even_d_skip")):
                act.dma_start(row16[:, i, :], w[name].unsqueeze(0).broadcast_to([P, SH])).then_inc(S["rows_loaded"], 16)
            act.dma_start(gate2[:, :], w["odd_w_gate2"]).then_inc(S["rows_loaded"], 16)
            split_to(1)
            for g in range(4):
                bank = wait_aux(act, ("par", g))
                r = sum(PAR_ROWS[:g])
                free_aux(act.activation(par[:, r:r + PAR_ROWS[g]], bank[:, 0:PAR_ROWS[g]], ACT.Copy), ("par", g))
            for k in range(KC):
                bank = wait_aux(act, ("x", k))
                free_aux(act.activation(h[:, k, :], bank[:, :], ACT.Copy), ("x", k))
            act.wait_ge(S["rows_loaded"], 64)
            step(act.activation(row16[:, 1, :], row16[:, 1, :], ACT.Exp))
            stage_barrier()

            act.dma_start(h_spill, h[:, :, :].rearrange("p a b -> p (a b)")).then_inc(S["spilled"], 16)
            act.wait_ge(S["dt_abs"], 1)
            step(act.activation(work[:, 17940:18004], work[:, 17940:18004], ACT.Exp, scale=-1.0))
            act.activation(work[:, 17940:18004], work[:, 17940:18004], ACT.Ln, bias=1.0).then_inc(S["dt_soft"], 1)
            def xbc_silu(j):
                act.wait_ge(S["xbc_conv"], j + 1)
                act.activation(XB[:, j, SSM_W - 1:], TMP[:, j % 2, :], ACT.Silu).then_inc(S["xbc_ready"], 1)

            for j in range(XC):
                if j % 2 == 0:
                    split_to(FIRST_PANEL["xbc"] + j // 2 + 1)
                c = stage_chunk("xbc") + j
                bank = wait_chunk(act, c)
                free_chunk(act.activation(XB[:, j, SSM_W - 1:], bank[:, :], ACT.Copy), c)
                if j:
                    xbc_silu(j - 1)
            xbc_silu(XC - 1)
            for f in range(KC):
                split_to(FIRST_PANEL["conv_in"] + f + 2)
                c = stage_chunk("conv_in") + 4 * (f // 2) + 2 + f % 2
                bank = wait_chunk(act, c)
                if f >= 2:
                    chunk_read(act, stage_chunk("conv_in") + 4 * ((f - 2) // 2) + f % 2)
                free_chunk(act.activation(SG[:, f % 2, :], bank[:, :], ACT.Sigmoid), c)
            act.wait_ge(S["spilled"], 16)
            for n in range(4):
                split_to(FIRST_PANEL["z"] + n + 1)
                for t2 in range(2):
                    c = stage_chunk("z") + 2 * n + t2
                    bank = wait_chunk(act, c)
                    free_chunk(act.activation(Z[:, 2 * t2:2 * t2 + 2, n * PANEL:(n + 1) * PANEL],
                                              bank[:, :].rearrange("p (t n) -> p t n", t=2), ACT.Silu), c)
            logs()

            def decays(c):
                act.wait_ge(S["seg_ready"], c + 1)
                r = 8 + 4 * (c % 2)
                act.activation(sm[:, r + 1:r + 3, :], sm[:, r + 1:r + 3, :], ACT.Exp)
                act.activation(sm[:, r + 3, :], sm[:, r, :], ACT.Exp).then_inc(S["dte_ready"], 1)
                act.activation(M, M, ACT.Exp).then_inc(S["decay_ready"], 1)

            decays(0)
            for c in range(TT):
                tok = slice(c * P, (c + 1) * P)
                for half in range(2):
                    bank = wait_aux(act, ("xs", c, half))
                    free_aux(act.activation(XS[:, half * 512:(half + 1) * 512], bank[:, :], ACT.Copy), ("xs", c, half))
                bank = wait_aux(act, ("bt", c))
                free_aux(act.activation(BT.rearrange("p a b -> p (a b)"), bank[:, 0:256], ACT.Copy), ("bt", c))
                act.wait_ge(S["gated"], c + 1)
                for g in range(2):
                    ins = act.activation(XS[:, 512 * g:512 * g + 512],
                                         XDT[:, 8 * g:8 * g + 8, :].rearrange("p a b -> p (a b)"),
                                         ACT.Square, accum_out=rs[:, 0, g:g + 1])
                step(ins)
                step(act.activation(rs[:, 1, 0:2], rs[:, 0, 0:2], ACT.Ln, bias=cst[:, 0:1], scale=1.0 / 512))
                act.activation(rs[:, 1, 0:2], rs[:, 1, 0:2], ACT.Exp, scale=-0.5).then_inc(S["ssm_rstd"], 1)
                if c + 1 < TT:
                    decays(c + 1)
                for g in range(2):
                    bank = wait_aux(act, ("yt", c, g))
                    for j in range(4):
                        ins = act.activation(x_hi[:, 4 * g + j, tok], bank[:, j * P:(j + 1) * P], ACT.Identity,
                                             scale=par_col("even_ssm_norm_g", 4 * g + j))
                    ins.then_inc(x_hi_done, 1)
            split_to(FIRST_PANEL["even_out_ssm"] + 1)
            act.wait_ge(S["gated"], TT)
            act.dma_start(h[:, :, :].rearrange("p a b -> p (a b)"), h_spill).then_inc(S["reloaded"], 16)
            for f in range(DVE_CONV, KC):
                c = CONV_CHUNK + f - DVE_CONV
                bank = wait_chunk(act, c)
                free_chunk(act.activation(U[:, f, CONV_W - 1:], bank[:, :], ACT.Identity,
                                          bias=par_col("even_conv_b", f)), c)
            squares(lambda k: U[:, k, CONV_W - 1:],
                    lambda k: act.wait_ge(S["conv_sum"], k + 1) if k < DVE_CONV
                    else chunk_read(act, CONV_CHUNK + k - DVE_CONV))
            split_to(FIRST_PANEL["even_out_ssm"] + 2)
            normalised(lambda k: U[:, k, CONV_W - 1:], lambda k: par_col("even_conv_ln_g", k),
                       lambda k: par_col("even_conv_ln_b", k), ACT.Silu, hi=y_hi)
            for n in range(4):
                split_to(FIRST_PANEL["even_out_ssm"] + n + 1)
            residual_squares("even_out_conv")
            layer_norm(0, 0)

            def cross_attention(i):
                name = f"x{i}"
                act.dma_start(mem_in, w["mem"].rearrange("(t p) n -> p t n", p=P)).then_inc(S["mem_loaded"], 16)
                for e in range(4):
                    bank = wait_aux(act, ("mem", i, e))
                    operand_hi(y_hi[:, 2 * e:2 * e + 2, 0:MEM], bank[:, :].rearrange("p (a b) -> p a b", a=2), y_hi_done)
                for n in range(4):
                    split_to(FIRST_PANEL[f"xk{i}"] + n + 1)
                    for s in range(2):
                        c = stage_chunk(f"xk{i}") + 2 * n + s
                        bank = wait_chunk(act, c)
                        free_chunk(act.activation(KT[:, 2 * n + s, :], bank[:, 0:MEM], ACT.Copy), c)
                for n in range(4):
                    split_to(FIRST_PANEL[f"xv{i}"] + n + 1)
                    c = stage_chunk(f"xv{i}") + n
                    bank = wait_chunk(act, c)
                    free_chunk(act.activation(VM[:, :, n * PANEL:(n + 1) * PANEL],
                                              bank[:, :].rearrange("p (t n) -> p t n", t=2), ACT.Copy), c)
                for n in range(4):
                    split_to(FIRST_PANEL[f"xq{i}"] + n + 1)
                    for s in range(2):
                        c = stage_chunk(f"xq{i}") + 2 * n + s
                        bank = wait_chunk(act, c)
                        free_chunk(act.activation(XQ[:, 2 * n + s, :], bank[:, :], ACT.Copy, scale=1.0 / 16), c)

                def exps(t):
                    un = UNIT[(name, t)]
                    act.wait_ge(S["unit_max"], un + 1)
                    for hd in range(XH):
                        key = (name, "S", t, hd // 2)
                        ins = act.activation(PR[:, t % 2, hd * MEM:(hd + 1) * MEM],
                                             wait_aux(act, key)[:, (hd % 2) * MEM:(hd % 2 + 1) * MEM], ACT.Exp,
                                             bias=mxs[:, un % 2, hd:hd + 1], accum_out=rs[:, un % 2, hd:hd + 1])
                        if hd % 2:
                            free_aux(ins, key)

                exps(0)
                for t in range(TT):
                    if t + 1 < TT:
                        exps(t + 1)
                    for m in range(2):
                        bank = wait_aux(act, (name, "T", t, m))
                        free_aux(act.activation(PTX[:, m, :, t * P:(t + 1) * P],
                                                bank[:, :].rearrange("p (a b) -> p a b", b=P), ACT.Copy),
                                 (name, "T", t, m))
                for j in range(KC):
                    bank = wait_aux(act, ("xpv", i, j))
                    operand_hi(x_hi[:, j, :], bank[:, :], x_hi_done)
                residual_squares(f"xo{i}")
                layer_norm(i, 1)

            def mlp(i):
                st = f"mlp{i}"
                for q in range(4):
                    for k in range(KC):
                        n = FIRST_PANEL[st] + 8 * q + k // 2
                        split_to(n + 1)
                        c = CHUNK0[n] + k % 2
                        bank = wait_chunk(act, c)
                        m = 32 * i + KC * q + k
                        if m % 32 >= 2:
                            act.wait_ge(y_ready, Y0[f"hid{i}0"] + (m % 32) - 1)
                        free_chunk(act.activation(area(0, 2, T)[:, k % 2, :], bank[:, :], ACT.Relu), c)
                        chunk_read(act, c)
                        act.activation(area(0, 2, T)[:, k % 2, :], area(0, 2, T)[:, k % 2, :], ACT.Square)\
                           .then_inc(S["hid_relu"], 1)
                    if q < 3:
                        for k in range(4):
                            split_to(FIRST_PANEL[st] + 8 * q + 4 + k + 1)
                    else:
                        residual_squares(st, half=28)
                layer_norm(i, 2)

            cross_attention(0)
            act.dma_start(w_small[:, :, :], w["odd_w_in"][:, 3072:3088].rearrange("(k p) n -> p k n", p=P))\
               .then_inc(S["small_loaded"], 16)
            mlp(0)

            for j in range(KC):
                if j % 2 == 0:
                    split_to(FIRST_PANEL["gla_qk"] + j // 2 + 1)
                c = stage_chunk("gla_qk") + j
                bank = wait_chunk(act, c)
                free_chunk(act.activation((GQ if j < 4 else GK)[:, j % 4, :], bank[:, :], ACT.Copy,
                                          scale=128.0 ** -0.5 if j < 4 else 1.0), c)
            bank = wait_aux(act, ("glow",))
            free_aux(act.activation(GL[0:16, :], bank[0:16, :], ACT.Copy), ("glow",))

            def gate_log(hd):
                act.wait_ge(S["log_ready"], hd + 1)
                b = GEB[hd % 2]
                step(act.activation(b, b, ACT.Exp, scale=-1.0))
                act.activation(b, b, ACT.Ln, bias=1.0).then_inc(S["eb_ready"], 1)

            def gate_exps(hd):
                e = hd % 2
                act.wait_ge(S["b_ready"], hd + 1)
                act.activation(GEB[e], GB, ACT.Exp)
                act.activation(GENB[e], GB, ACT.Exp, scale=-1.0)
                for n in range(8):
                    ins = act.activation(GKT[e].rearrange("p a b -> p (a b)")[:, 64 * n:64 * n + 64],
                                         GB[:, 64 * n:64 * n + 64], ACT.Exp, scale=-1.0,
                                         bias=GB[:, 64 * n + 63:64 * n + 64])
                ins.then_inc(S["eb_ready"], 1)

            def turned_keys(hd):
                bank = wait_aux(act, ("kend", hd))
                free_aux(act.activation(GKT[hd % 2].rearrange("p a b -> p (a b)"), bank[:, :], ACT.Copy),
                         ("kend", hd))

            def panel_rows(hd, i):
                c = stage_chunk("gla_v") + 4 * hd + i
                bank = wait_chunk(act, c)
                free_chunk(act.activation((GVV, GVV, GG, GG)[i][:, hd % 2, 2 * (i % 2):2 * (i % 2) + 2, :],
                                          bank[:, :].rearrange("p (t n) -> p t n", t=2),
                                          ACT.Copy if i < 2 else ACT.Silu), c)

            def square_tile(hd, t):
                aux_read(act, "go", hd, t)
                step(act.activation(area(17920, GV), GY[:, t, :], ACT.Square,
                                    accum_out=sm[:, 8, TT * hd + t:TT * hd + t + 1]))

            def head_operand(hd):
                for j in range(2):
                    bank = wait_aux(act, ("gt", hd, j))
                    operand_hi(y_hi[:, 2 * hd + j, :], bank[:, :], x_hi_done, par_col("odd_head_norm_g", j))

            first = FIRST_PANEL["gla_v"]
            split_to(first + 1)
            logs()
            gate_log(0)
            for i in range(2):
                panel_rows(0, i)
            gate_exps(0)
            for i in range(2, 4):
                panel_rows(0, i)
            logs()
            split_to(first + 2)
            turned_keys(0)
            for hd in range(GH):
                for t in range(TT):
                    if t:
                        square_tile(hd, t - 1)
                    elif hd:
                        head_operand(hd - 1)
                    if t == 0:
                        split_to(first + 2 * hd + 3)
                    if hd + 1 < GH:
                        if t < 2:
                            panel_rows(hd + 1, t)
                        if t == 0:
                            gate_log(hd + 1)
                        if t == 1:
                            gate_exps(hd + 1)
                        if t == 2:
                            split_to(first + 2 * hd + 4)
                square_tile(hd, TT - 1)
                cols = slice(TT * hd, TT * hd + TT)
                step(act.activation(sm[:, 9, cols], sm[:, 8, cols], ACT.Ln, bias=cst[:, 0:1], scale=1.0 / GV))
                act.activation(sm[:, 9, cols], sm[:, 9, cols], ACT.Exp, scale=-0.5).then_inc(S["gla_rstd"], 1)
                if hd + 1 < GH:
                    turned_keys(hd + 1)
                    if hd:
                        act.wait_ge(S["o_ready"], hd)
                    for i in range(2, 4):
                        panel_rows(hd + 1, i)
                    logs()
            head_operand(GH - 1)
            residual_squares("odd_out")
            layer_norm(1, 0)
            cross_attention(1)
            act.dma_start(w_small[:, :, 0:8], w["w_in_2"][:, 4864:4872].rearrange("(k p) n -> p k n", p=P))\
               .then_inc(S["small_loaded"], 16)
            act.dma_start(row16[:, 0, 0:8], w["b_forget_2"].unsqueeze(0).broadcast_to([P, 8]))\
               .then_inc(S["lam_loaded"], 16)
            act.dma_start(row16[:, 1, 0:8], w["sinks_2"].unsqueeze(0).broadcast_to([P, 8]))\
               .then_inc(S["lam_loaded"], 16)
            mlp(1)

            act.wait_ge(S["h_ready"], KC * 7)
            act.dma_start(h_spill, h[:, :, :].rearrange("p a b -> p (a b)")).then_inc(S["spilled"], 16)
            for i, n_ in enumerate(("lambda_q1_2", "lambda_k1_2", "lambda_q2_2", "lambda_k2_2")):
                act.dma_start(LAMB[:, 64 * i:64 * i + 64], w[n_].unsqueeze(0).broadcast_to([P, 64]))\
                   .then_inc(S["lam_loaded"], 16)
            act.wait_ge(S["lam_sum"], 1)
            act.activation(lam[:, 0:2], lam[:, 0:2], ACT.Exp).then_inc(S["lam_ready"], 1)

            squares(lambda k: h[:, k, :], lambda k: None)
            normalised(lambda k: x_hi[:, k, :], lambda k: par_col("norm_gain_2", k), None, eps=1, rms=True)
            for n_, b in enumerate("abc"):
                scale = 1.0 / 8
                nq = 4
                for j in range(4 if b == "b" else KC):
                    if j % 2 == 0:
                        split_to(FIRST_PANEL[f"qk_{b}"] + j // 2 + 1)
                    c = stage_chunk(f"qk_{b}") + j
                    bank = wait_chunk(act, c)
                    free_chunk(act.activation(QK[:, j, :], bank[:, :], ACT.Copy, scale=scale if j < nq else 1.0), c)
                if b == "b":
                    split_to(FIRST_PANEL["kv_b"] + 1)
                    c = stage_chunk("kv_b")
                    bank = wait_chunk(act, c)
                    free_chunk(act.activation(QK[:, 4, :], bank[:, :], ACT.Copy), c)
                    bank = wait_chunk(act, c + 1)
                    free_chunk(act.activation(BV[:, :, 0:P], bank[:, :].rearrange("p (t n) -> p t n", n=P),
                                              ACT.Copy), c + 1)
                for stage, dst, func in ((f"v_{b}", BV, ACT.Copy), (f"g_{b}", BG, ACT.Silu)):
                    if stage not in FIRST_PANEL:
                        continue
                    for n in range(2):
                        split_to(FIRST_PANEL[stage] + n + 1)
                        for t2 in range(2):
                            c = stage_chunk(stage) + 2 * n + t2
                            bank = wait_chunk(act, c)
                            free_chunk(act.activation(dst[:, 2 * t2:2 * t2 + 2, n * PANEL:(n + 1) * PANEL],
                                                      bank[:, :].rearrange("p (t n) -> p t n", t=2), func), c)
                logs()
                if b == "c":
                    act.wait_ge(S["c_abs"], 1)
                    step(act.activation(sm[:, 12:14, :], sm[:, 12:14, :], ACT.Exp, scale=-1.0))
                    act.activation(sm[:, 12:14, :], sm[:, 12:14, :], ACT.Ln, bias=1.0).then_inc(S["c_soft"], 1)
                us = [(hd, t) for hd in range(8 if b == "c" else 4) for t in range(TT)]
                B = b.upper()

                def exps(u):
                    e = unit_slot(b, u)
                    hd, t = u
                    act.wait_ge(S["unit_max"], UNIT[(B, u)] + 1)
                    if b == "a":
                        for m in range(2):
                            v = EX[:, e, m, 0:(t + 1) * P]
                            ins = act.activation(v, v, ACT.Exp, bias=mxs[:, e, m:m + 1], accum_out=rs[:, e, m:m + 1])
                    elif b == "b":
                        for g in range(2):
                            v = unit_row(b, u)[:, g * 256 + (P if t == 0 else 0):(g + 1) * 256]
                            act.activation(v, v, ACT.Exp, bias=mxs[:, e, g:g + 1], accum_out=rs[:, e, g:g + 1])
                            ins = act.activation(rs[:, e, 2 + g:3 + g], row16[:, 1, hd + 4 * g:hd + 4 * g + 1],
                                                 ACT.Exp, bias=mxs[:, e, g:g + 1])
                    else:
                        v = unit_row(b, u)[:, 0:(t + 1) * P]
                        ins = act.activation(v, v, ACT.Exp, bias=mxs[:, e, 0:1], accum_out=rs[:, e, 0:1])
                    ins.then_inc(S["unit_exp"], 1)

                def square_unit(n):
                    hd, t = us[n]
                    aux_read(act, "A", "PV", us[n])
                    col = t * 4 + hd
                    step(act.activation(PT[:, UNIT[("A", us[n])] % 2, 0:P], YT[:, t, hd * P:(hd + 1) * P], ACT.Square,
                                        accum_out=sm[:, 8, col:col + 1]))

                per = len(us) // KC
                first = FIRST_PANEL[f"gm_{b}"]
                split_chunks(2 * first + W_SLOTS)
                for u in us[:AHEAD[b]]:
                    exps(u)
                for n, u in enumerate(us):
                    if b == "a":
                        if n + 1 < len(us):
                            exps(us[n + 1])
                        if n:
                            square_unit(n - 1)
                    e = UNIT[(B, u)] % 2
                    bank = wait_aux(act, (B, "T", u, 0))
                    if b == "b":
                        lo = P if u[1] == 0 else 0
                        src = bank[:, :].rearrange("p (g n) -> p g n", g=2)[:, :, lo:]
                        dst = PT[:, e, :].rearrange("p (g n) -> p g n", g=2)[:, :, lo:]
                    else:
                        src, dst = bank[:, 0:(u[1] + 1) * P], PT[:, e, 0:(u[1] + 1) * P]
                    free_aux(act.activation(dst, src, ACT.Copy), (B, "T", u, 0))
                    if b != "a" and n + 2 < len(us):
                        exps(us[n + 2])
                    if n % per == per - 1:
                        f = n // per
                        if f == 0 and b == "a":
                            act.wait_ge(S["spilled"], 32)
                        elif f == 0:
                            chunk_read(act, CHUNK0[FIRST_PANEL[f"up_{'abc'[n_ - 1]}"]] + 7)
                            if n_ == 2:
                                act.wait_ge(S["merged_ready"], KC)
                        c = stage_chunk(f"gm_{b}") + f
                        bank = wait_chunk(act, c)
                        free_chunk(act.activation(GATE[:, f, :], bank[:, :], ACT.Copy), c)
                        split_chunks(2 * first + W_SLOTS + f + 1)
                if b == "a":
                    square_unit(len(us) - 1)
                    step(act.activation(sm[:, 9, :], sm[:, 8, :], ACT.Ln, bias=cst[:, 0:1], scale=1.0 / P))
                    act.activation(sm[:, 9, :], sm[:, 9, :], ACT.Exp, scale=-0.5).then_inc(S["ya_rstd"], 1)
                for k in range(KC):
                    chunk_read(act, stage_chunk(f"gm_{b}") + k)
                    act.activation(GATE[:, k, :], GATE[:, k, :], ACT.Sigmoid).then_inc(S["gate_ready"], 1)
                for j in range(4):
                    bank = wait_aux(act, (B + "t", j))
                    operand_hi(y_hi[:, j, :], bank[:, :], y_hi_done, lam[:, 3:4] if b == "a" else 1.0)
            split_to(FIRST_PANEL["w_o"])
            for k, f in enumerate(UP_ORDER):
                act.wait_ge(S["merged_ready"], KC + k + 1)
                operand_hi(x_hi[:, f, :], MG[:, f, :], x_hi_done)
            act.dma_start(h[:, :, :].rearrange("p a b -> p (a b)"), h_spill).then_inc(S["reloaded"], 16)
            residual_squares("w_o")
            normalised(lambda k: MG[:, k, :], lambda k: par_col("final_gain_2", k), None, eps=1, rms=True)
            for t in range(TT):
                for j in range(2):
                    bank = wait_aux(act, ("out", t, j))
                    free_aux(act.activation(area(0, TT, D)[:, t, 512 * j:512 * j + 512], bank[:, :], ACT.Copy),
                             ("out", t, j))
                aux_read(act, "out", t, 1)
                act.dma_start(out[t * P:(t + 1) * P, :], area(0, TT, D)[:, t, :]).then_inc(S["out_sent"], 16)
            act.wait_ge(S["out_sent"], 16 * TT)

        @block.vector
        def _(dve):
            at = dict(step=0, split=0, prod=0, end=0, ln=0, sq=0, hr=0, xh=0, yh=0, lh=0)

            def step(ins):
                at["step"] += 1
                ins.then_inc(dve_step, 1)
                dve.wait_ge(dve_step, at["step"])

            def stage_barrier():
                at["end"] += 1
                dve.drain().then_inc(stage_end, 1)
                dve.wait_ge(stage_end, 3 * at["end"])

            def split_chunk():
                s = at["split"]
                if s < 2 * NPANEL:
                    dve.wait_ge(w_hi_ready, s + 1)
                    half = slice((s % 2) * P, (s % 2 + 1) * P)
                    dve.tensor_tensor(w_lo[:, s % W_SLOTS, :, :], raw[:, s // 2 % RAW_SLOTS, :, half],
                                      w_hi[:, s % W_SLOTS, :, :].bitcast(F32), ALU.subtract).then_inc(w_lo_ready, 1)
                    at["split"] += 1

            def split_chunks(upto):
                while at["split"] < upto:
                    split_chunk()

            def split_to(panel):
                while at["split"] < min(2 * panel + 2, 2 * NPANEL):
                    split_chunk()

            def operand(hi, lo, src, ready):
                step(dve.tensor_copy(hi, src))
                dve.tensor_tensor(lo, src, hi.bitcast(F32), ALU.subtract).then_inc(ready, 1)

            def operand_lo(hi, lo, src, hi_sem, which, scale=None):
                at[which] += 1
                dve.wait_ge(hi_sem, at[which])
                if scale is None:
                    return dve.tensor_tensor(lo, src, hi.bitcast(F32), ALU.subtract)
                return dve.scalar_tensor_tensor(lo, src, scale, hi.bitcast(F32), ALU.mult, ALU.subtract)

            def accumulate(k, src, mean=True):
                at["sq"] += 1
                dve.wait_ge(S["sq_ready"], at["sq"])
                sq = LN[:, k % 2, :]
                if k == 0:
                    if mean:
                        dve.tensor_copy(LN[:, 3, :], src)
                    ins = dve.tensor_copy(LN[:, 4, :], sq)
                else:
                    if mean:
                        dve.tensor_tensor(LN[:, 3, :], LN[:, 3, :], src, ALU.add)
                    ins = dve.tensor_tensor(LN[:, 4, :], LN[:, 4, :], sq, ALU.add)
                ins.then_inc(S["sum_in"], 1)
                dve.wait_ge(S["sum_in"], at["sq"])

            def normalise(name, src, finish, center=True, lag=2, more=True):
                n = at["ln"]
                at["ln"] += 1
                if center:
                    bank = wait_aux(dve, ("ln", name, 0))
                    free_aux(dve.tensor_scalar(LN[:, 0, :], bank[:, :], 1.0 / D, None, ALU.mult), ("ln", name, 0))
                    aux_read(dve, "ln", name, 0)
                    step(dve.tensor_tensor(LN[:, 1, :], LN[:, 0, :], LN[:, 0, :], ALU.mult))
                    bank = wait_aux(dve, ("ln", name, 1))
                    free_aux(dve.scalar_tensor_tensor(LN[:, 1, :], bank[:, :], 1.0 / D, LN[:, 1, :], ALU.mult,
                                                      ALU.subtract), ("ln", name, 1))
                    aux_read(dve, "ln", name, 1)
                    dve.tensor_scalar(LN[:, 1, :], LN[:, 1, :], 0.0, None, ALU.max).then_inc(S["ln_var"], 1)
                else:
                    bank = wait_aux(dve, ("rms", name))
                    free_aux(dve.tensor_scalar(LN[:, 1, :], bank[:, :], 1.0 / D, None, ALU.mult), ("rms", name))
                    aux_read(dve, "rms", name)
                    dve.engine_nop().then_inc(S["ln_var"], 1)
                if more:
                    split_to(at["split"] // 2)
                dve.wait_ge(S["ln_rstd"], n + 1)
                for k in range(KC + lag):
                    if k < KC:
                        xn = LN[:, 3 + k % 2, :]
                        if center:
                            step(dve.tensor_tensor(xn, src(k), LN[:, 0, :], ALU.subtract))
                            dve.tensor_tensor(xn, xn, LN[:, 2, :], ALU.mult).then_inc(S["ln_xn"], 1)
                        else:
                            dve.tensor_tensor(xn, src(k), LN[:, 2, :], ALU.mult).then_inc(S["ln_xn"], 1)
                    if k and k <= KC:
                        at["hr"] += 1
                        dve.wait_ge(S["h_ready"], at["hr"])
                    if k >= lag:
                        finish(k - lag)

            def rest(hi, lo, src, ready):
                def finish(k):
                    at["lh"] += 1
                    dve.wait_ge(S["ln_hi"], at["lh"])
                    dve.tensor_tensor(lo[:, k, :], src(k), hi[:, k, :].bitcast(F32), ALU.subtract).then_inc(ready, 1)
                return finish

            to_x = rest(x_hi, x_lo, lambda k: h[:, k, :], x_ready)

            def residual(stage, half=0, scale=None, sums=None, chunks=range(KC)):
                for k in chunks:
                    n = FIRST_PANEL[stage] + half + k // 2
                    if k % 2 == 0:
                        split_to(n + 1)
                    c = CHUNK0[n] + k % 2
                    bank = wait_chunk(dve, c)
                    if scale is None:
                        free_chunk(dve.tensor_tensor(h[:, k, :], h[:, k, :], bank[:, :], ALU.add), c)
                    else:
                        free_chunk(dve.scalar_tensor_tensor(h[:, k, :], h[:, k, :], scale, bank[:, :], ALU.mult,
                                                            ALU.add), c)
                    if sums is not None:
                        if k:
                            accumulate(k - 1, h[:, k - 1, :], sums)
                        if k == KC - 1:
                            chunk_read(dve, c)
                            accumulate(k, h[:, k, :], sums)

            def spread(v, n):
                return v.unsqueeze(2).broadcast_to([P, v.shape[1], n])

            def over(v, n):
                return v.unsqueeze(1).broadcast_to([P, n, v.shape[1]])

            split_to(1)
            for k in range(KC):
                aux_read(dve, "x", k)
                operand(x_hi[:, k, :], x_lo[:, k, :], h[:, k, :], x_ready)
            stage_barrier()

            step(dve.memset(U[:, :, 0:CONV_W - 1], 0.0))
            step(dve.memset(XB[:, :, 0:SSM_W - 1], 0.0))
            bank = wait_aux(dve, ("dt",))
            soft = area(17940, TT, SH)
            dt = sm[:, 4:8, :]
            free_aux(dve.tensor_tensor(dt, bank[:, 0:TT * SH].rearrange("p (t n) -> p t n", n=SH),
                                       over(row16[:, 0, :], TT), ALU.add), ("dt",))
            aux_read(dve, "dt")
            dve.scalar_tensor_tensor(soft, dt, -1.0, dt, ALU.mult, ALU.max).then_inc(S["dt_abs"], 1)
            dve.wait_ge(S["dt_soft"], 1)
            step(dve.scalar_tensor_tensor(dt, dt, 0.0, soft, ALU.max, ALU.add))
            dve.scalar_tensor_tensor(sm[:, 0:4, :], dt, -1.0, over(row16[:, 1, :], TT), ALU.mult, ALU.mult)\
               .then_inc(S["dta_ready"], 1)
            for j in range(XC):
                if j % 2 == 0:
                    split_to(FIRST_PANEL["xbc"] + j // 2 + 1)
                chunk_read(dve, stage_chunk("xbc") + j)
                if j >= 2:
                    dve.wait_ge(S["xbc_ready"], j - 1)
                tmp = TMP[:, j % 2, :]
                step(dve.tensor_scalar(tmp, XB[:, j, 0:T], par_col("even_ssm_conv_w", j),
                                       par_col("even_ssm_conv_b", j), ALU.mult, ALU.add))
                for i in range(1, SSM_W):
                    ins = dve.scalar_tensor_tensor(tmp, XB[:, j, i:i + T], par_col("even_ssm_conv_w", i * XC + j), tmp,
                                                   ALU.mult, ALU.add)
                    if i < SSM_W - 1:
                        step(ins)
                ins.then_inc(S["xbc_conv"], 1)

            def side_work():
                f = at["prod"]
                if f < KC and at["split"] >= 2 * (FIRST_PANEL["conv_in"] + f + 2) + 2:
                    c = stage_chunk("conv_in") + 4 * (f // 2) + f % 2
                    chunk_read(dve, c + 2)
                    bank = wait_chunk(dve, c)
                    free_chunk(dve.tensor_tensor(U[:, f, CONV_W - 1:], bank[:, :], SG[:, f % 2, :], ALU.mult), c)
                    at["prod"] += 1
                elif f < KC or at["split"] < 2 * FIRST_PANEL["even_out_ssm"]:
                    split_chunk()

            for f0 in range(0, DVE_CONV, 2):
                fs = range(f0, min(f0 + 2, DVE_CONV))
                added = {}
                while at["prod"] < fs[-1] + 1:
                    side_work()
                for i in range(CONV_W):
                    for f in fs:
                        acc = CV[:, f % 2, :]
                        last = i == CONV_W - 1
                        if i == 0:
                            chunk_read(dve, stage_chunk("conv_in") + 4 * (f // 2) + f % 2)
                            at["step"] += 1
                            dve.tensor_scalar(acc, U[:, f, 0:T], par_col("even_conv_w", f), par_col("even_conv_b", f),
                                              ALU.mult, ALU.add).then_inc(dve_step, 1)
                        else:
                            dve.wait_ge(dve_step, added[f])
                            ins = dve.scalar_tensor_tensor(U[:, f, CONV_W - 1:] if last else acc, U[:, f, i:i + T],
                                                           par_col("even_conv_w", i * KC + f), acc, ALU.mult, ALU.add)
                            if last:
                                ins.then_inc(S["conv_sum"], 1)
                            else:
                                at["step"] += 1
                                ins.then_inc(dve_step, 1)
                        added[f] = at["step"]
                    if i % 2 == 0:
                        side_work()
                dve.wait_ge(S["conv_sum"], fs[-1] + 1)
            while at["prod"] < KC:
                side_work()
            split_to(FIRST_PANEL["even_out_ssm"])
            tri2 = over(triu[:, :], 2)
            cb = TMP[:, 0, 0:2 * P].rearrange("p (a b) -> p a b", b=P)

            def tile_sums(c):
                r = 8 + 4 * (c % 2)
                bank = wait_aux(dve, ("acs", c))
                free_aux(dve.tensor_copy(sm[:, r, :], bank[:, 0:SH]), ("acs", c))
                aux_read(dve, "acs", c)

            def differences(c):
                r = 8 + 4 * (c % 2)
                for q in range(4):
                    bank = wait_aux(dve, ("bc", c, q))
                    rows = bank[:, :].rearrange("p (a b) -> p a b", b=P)
                    hs = slice(4 * q, 4 * q + 4)
                    dve.tensor_tensor(sm[:, r + 1, hs], rows[:, :, P - 1], sm[:, r, hs], ALU.subtract)
                    dve.tensor_copy(sm[:, r + 2, hs], rows[:, :, P - 1])
                    for j in range(4):
                        hd = 4 * q + j
                        ins = dve.tensor_scalar(M[:, hd, :], rows[:, j, :], sm[:, r, hd:hd + 1], 0.0, ALU.subtract,
                                                ALU.min)
                    free_aux(ins, ("bc", c, q))
                aux_read(dve, "bc", c, 3)
                dve.engine_nop().then_inc(S["seg_ready"], 1)

            tile_sums(0)
            differences(0)
            for c in range(TT):
                tok = slice(c * P, (c + 1) * P)
                r = 8 + 4 * (c % 2)
                if c == 0:
                    dve.wait_ge(S["xbc_ready"], XC)
                bank = wait_aux(dve, ("cb", c))
                free_aux(dve.tensor_tensor(cb, bank[:, 0:2 * P].rearrange("p (a b) -> p a b", b=P), tri2, ALU.mult),
                         ("cb", c))
                aux_read(dve, "cb", c)
                aux_read(dve, "bt", c)
                xs = XS.rearrange("p (a b) -> p a b", b=SP_)
                step(dve.tensor_tensor(XDT, xs, spread(sm[:, 4 + c, :], SP_), ALU.mult))
                dve.wait_ge(S["dte_ready"], c + 1)
                dve.tensor_tensor(XW, XDT, spread(sm[:, r + 1, :], SP_), ALU.mult).then_inc(S["xdt_ready"], 1)
                dve.wait_ge(S["decay_ready"], c + 1)
                for g in range(2):
                    m8 = M[:, 8 * g:8 * g + 8, :]
                    ins = dve.tensor_tensor(m8, m8, over(cb[:, g, :], 8), ALU.mult)
                ins.then_inc(S["m_ready"], 1)
                dve.wait_ge(S["m_ready"], c + 1)
                skip = TMP.rearrange("p a b -> p (a b)").rearrange("p (a b) -> p a b", b=SP_)
                step(dve.tensor_tensor(skip, xs, spread(row16[:, 2, :], SP_), ALU.mult))
                wait_aux(dve, ("yd", c, 1))
                if c + 1 < TT:
                    tile_sums(c + 1)
                for g in range(2):
                    y8 = XDT[:, 8 * g:8 * g + 8, :]
                    bank = wait_aux(dve, ("yd", c, g))
                    free_aux(dve.tensor_tensor(y8, bank[:, :].rearrange("p (a b) -> p a b", b=SP_),
                                               skip[:, 8 * g:8 * g + 8, :], ALU.add), ("yd", c, g))
                    if c:
                        bank = wait_aux(dve, ("yo", c, g))
                        aux_read(dve, "yd", c, g)
                        free_aux(dve.tensor_tensor(skip[:, 8 * g:8 * g + 8, :],
                                                   bank[:, :].rearrange("p (a b) -> p a b", b=SP_),
                                                   spread(sm[:, r + 3, 8 * g:8 * g + 8], SP_), ALU.mult), ("yo", c, g))
                if c:
                    aux_read(dve, "yo", c, 1)
                    step(dve.tensor_tensor(XDT, XDT, skip, ALU.add))
                else:
                    aux_read(dve, "yd", c, 1)
                if c == 0:
                    chunk_read(dve, stage_end_chunk("z") - 1)
                dve.tensor_tensor(XDT.rearrange("p a b -> p (a b)"), XDT.rearrange("p a b -> p (a b)"), Z[:, c, :],
                                  ALU.mult).then_inc(S["gated"], 1)
                st8 = ST.rearrange("p a b -> p (a b)").rearrange("p (a b) -> p a b", b=SP_)
                if c:
                    step(dve.tensor_tensor(st8, st8, spread(sm[:, r + 2, :], SP_), ALU.mult))
                for g in range(2):
                    bank = wait_aux(dve, ("st", c, g))
                    if c:
                        free_aux(dve.tensor_tensor(ST[:, g, :], ST[:, g, :], bank[:, :], ALU.add), ("st", c, g))
                    else:
                        free_aux(dve.tensor_copy(ST[:, g, :], bank[:, :]), ("st", c, g))
                aux_read(dve, "st", c, 1)
                dve.engine_nop().then_inc(S["state_ready"], 1)
                if c + 1 < TT:
                    differences(c + 1)
                dve.wait_ge(S["ssm_rstd"], c + 1)
                dve.wait_ge(S["gated"], c + 1)
                for g in range(2):
                    y8 = XDT[:, 8 * g:8 * g + 8, :]
                    ins = dve.tensor_scalar(y8, y8, rs[:, 1, g:g + 1], None, ALU.mult)
                ins.then_inc(S["y_gated"], 1)
                for g in range(2):
                    bank = wait_aux(dve, ("yt", c, g))
                    at["xh"] += 1
                    dve.wait_ge(x_hi_done, at["xh"])
                    for j in range(4):
                        k = 4 * g + j
                        ins = dve.scalar_tensor_tensor(x_lo[:, k, tok], bank[:, j * P:(j + 1) * P],
                                                       par_col("even_ssm_norm_g", k), x_hi[:, k, tok].bitcast(F32),
                                                       ALU.mult, ALU.subtract)
                    free_aux(ins, ("yt", c, g))
            split_to(FIRST_PANEL["even_out_ssm"] + 1)
            for k in range(KC):
                accumulate(k, U[:, k, CONV_W - 1:])
            dve.wait_ge(S["reloaded"], 16)
            residual("even_out_ssm", scale=ALPHA, chunks=range(0, 4))
            normalise("conv", lambda k: U[:, k, CONV_W - 1:],
                      rest(y_hi, y_lo, lambda k: U[:, k, CONV_W - 1:], y_ready))
            residual("even_out_ssm", scale=ALPHA, chunks=range(4, KC))
            residual("even_out_conv", sums=True)
            normalise("m0", lambda k: h[:, k, :], to_x)

            def cross_attention(i):
                name = f"x{i}"
                for e in range(4):
                    bank = wait_aux(dve, ("mem", i, e))
                    s = slice(2 * e, 2 * e + 2)
                    free_aux(operand_lo(y_hi[:, s, 0:MEM], y_lo[:, s, 0:MEM],
                                        bank[:, :].rearrange("p (a b) -> p a b", a=2), y_hi_done, "yh"), ("mem", i, e))
                for stage in ("xk", "xv", "xq"):
                    for n in range(4):
                        split_to(FIRST_PANEL[f"{stage}{i}"] + n + 1)

                def maxima(t):
                    e2 = UNIT[(name, t)] % 2
                    for e in range(2):
                        bank = wait_aux(dve, (name, "S", t, e))
                        ins = dve.tensor_reduce(mxs[:, e2, 2 * e:2 * e + 2],
                                                bank[:, :].rearrange("p (a b) -> p a b", b=MEM), AX.X, ALU.max,
                                                negate=True)
                    ins.then_inc(S["unit_max"], 1)

                maxima(0)
                for t in range(TT):
                    if t + 1 < TT:
                        maxima(t + 1)
                    e2 = UNIT[(name, t)] % 2
                    aux_read(dve, name, "S", t, 1)
                    step(dve.reciprocal(rs[:, e2, :], rs[:, e2, :]))
                    pr = PR[:, t % 2, :].rearrange("p (a b) -> p a b", b=MEM)
                    dve.tensor_tensor(pr, pr, spread(rs[:, e2, :], MEM), ALU.mult).then_inc(S["p_ready"], 1)
                for j in range(KC):
                    bank = wait_aux(dve, ("xpv", i, j))
                    free_aux(operand_lo(x_hi[:, j, :], x_lo[:, j, :], bank[:, :], x_hi_done, "xh"), ("xpv", i, j))
                residual(f"xo{i}", scale=ALPHA, sums=True)
                normalise(f"a{i}", lambda k: h[:, k, :], to_x)

            def mlp(i):
                st = f"mlp{i}"
                for q in range(4):
                    for k in range(KC):
                        split_to(FIRST_PANEL[st] + 8 * q + k // 2 + 1)
                        dve.wait_ge(S["hid_relu"], 32 * i + KC * q + k + 1)
                        operand(y_hi[:, k, :], y_lo[:, k, :], area(0, 2, T)[:, k % 2, :], y_ready)
                    residual(st, half=8 * q + 4, scale=ALPHA if q == 0 else None, sums=True if q == 3 else None)
                normalise(f"f{i}", lambda k: h[:, k, :], to_x if i == 0 else lambda k: None, more=i == 0)

            cross_attention(0)
            mlp(0)

            block_mask = area(18176, P)
            step(dve.memset(GA, 0.0))
            step(dve.tensor_copy(block_mask, triu[:, :]))
            step(dve.memset(block_mask[0:64, 64:128], 0.0))
            step(dve.memset(GMASK, 1.0))
            step(dve.memset(GMASK.rearrange("p (a b) -> p a b", b=64)[:, :, 0:1], 0.0))
            for e in range(2):
                step(dve.memset(GQE[e], 0.0))
                step(dve.memset(GQO[e], 0.0))
            for n in range(4):
                split_to(FIRST_PANEL["gla_qk"] + n + 1)

            def gate_abs(hd):
                e = hd % 2
                bank = wait_aux(dve, ("gate", hd))
                free_aux(dve.tensor_scalar(GENB[e], bank[:, :], par_col("odd_b_gate", hd), None, ALU.add),
                         ("gate", hd))
                aux_read(dve, "gate", hd)
                dve.scalar_tensor_tensor(GEB[e], GENB[e], -1.0, GENB[e], ALU.mult, ALU.max)\
                   .then_inc(S["log_ready"], 1)

            def gate_sums(hd):
                e = hd % 2
                dve.wait_ge(S["eb_ready"], 2 * hd + 1)
                step(dve.scalar_tensor_tensor(GENB[e], GENB[e], 0.0, GEB[e], ALU.min, ALU.subtract))
                step(dve.tensor_scalar(GENB[e], GENB[e], 1.0 / 16, None, ALU.mult))
                dve.tensor_tensor_scan(GB, GMASK, GENB[e], 0.0, ALU.mult, ALU.add).then_inc(S["b_ready"], 1)

            def decayed(hd):
                e = hd % 2
                dve.wait_ge(S["eb_ready"], 2 * hd + 2)
                q, k = GQ[:, hd, :], GK[:, hd, :]
                step(dve.tensor_tensor(q, q, GEB[e], ALU.mult))
                for n, dst in enumerate((GQE[e], GQO[e])):
                    part = (lambda v: v.rearrange("p (t a b) -> p t a b", a=2, b=64)[:, :, n, :])
                    dve.tensor_copy(part(dst), part(q))
                step(dve.tensor_tensor(GENB[e], k, GENB[e], ALU.mult))
                dve.tensor_tensor(k, k, GKT[e].rearrange("p a b -> p (a b)"), ALU.mult).then_inc(S["qkt_ready"], 1)

            def tile_mask(hd, t):
                bank = wait_aux(dve, ("gatt", hd, t))
                free_aux(dve.copy_predicated(GA[:, t % 2, :], block_mask.bitcast(mybir.dt.uint32), bank[:, 0:P]),
                         ("gatt", hd, t))

            def state(hd, t, half):
                n = 2 * t + half
                kv = wait_aux(dve, ("gkv", hd, t, half))
                if n == 0:
                    ins = dve.tensor_copy(GS[:, 1, :], kv[:, 0:GV])
                else:
                    aux_read(dve, "gkv", hd, (n - 1) // 2, (n - 1) % 2)
                    ins = dve.scalar_tensor_tensor(GS[:, (n + 1) % 4, :], GS[:, n % 4, :],
                                                   GEB[hd % 2][:, 64 * n + 63:64 * n + 64], kv[:, 0:GV], ALU.mult,
                                                   ALU.add)
                free_aux(ins, ("gkv", hd, t, half))

            def tile_rows(hd, t):
                bank = wait_aux(dve, ("go", hd, t))
                free_aux(dve.tensor_copy(GY[:, t, :], bank[:, 0:GV]), ("go", hd, t))

            def gated_head(hd):
                dve.wait_ge(S["gla_rstd"], hd + 1)
                chunk_read(dve, stage_chunk("gla_v") + 4 * hd + 3)
                step(dve.tensor_tensor(GY, GY, spread(sm[:, 9, TT * hd:TT * hd + TT], GV), ALU.mult))
                dve.tensor_tensor(GY, GY, GG[:, hd % 2], ALU.mult).then_inc(S["o_ready"], 1)

            def head_operand(hd):
                for j in range(2):
                    bank = wait_aux(dve, ("gt", hd, j))
                    k = 2 * hd + j
                    free_aux(operand_lo(y_hi[:, k, :], y_lo[:, k, :], bank[:, :], x_hi_done, "xh",
                                        par_col("odd_head_norm_g", j)), ("gt", hd, j))

            first = FIRST_PANEL["gla_v"]
            split_to(first + 1)
            gate_abs(0)
            gate_sums(0)
            chunk_read(dve, stage_end_chunk("gla_qk") - 1)
            decayed(0)
            split_to(first + 2)
            for hd in range(GH):
                for t in range(TT):
                    tile_mask(hd, t)
                    state(hd, t, 0)
                    if t:
                        tile_rows(hd, t - 1)
                    elif hd:
                        gated_head(hd - 1)
                    if t + 1 < TT:
                        state(hd, t, 1)
                    if t == 0 and hd + 1 < GH:
                        gate_abs(hd + 1)
                    if t == 0 and hd:
                        head_operand(hd - 1)
                    if t == 0:
                        split_to(first + 2 * hd + 3)
                    if hd + 1 < GH:
                        if t == 1:
                            gate_sums(hd + 1)
                        if t == 2:
                            split_to(first + 2 * hd + 4)
                            decayed(hd + 1)
                tile_rows(hd, TT - 1)
            gated_head(GH - 1)
            head_operand(GH - 1)
            residual("odd_out", scale=ALPHA, sums=True)
            normalise("m1", lambda k: h[:, k, :], to_x)
            cross_attention(1)
            mlp(1)

            dve.wait_ge(S["lam_loaded"], 16 * 6)
            lq = LAMB[:, 0:256].rearrange("p (a b c) -> p a b c", a=2, b=2)
            prod = LAMB[:, 256:384].rearrange("p (a b) -> p a b", a=2)
            step(dve.tensor_tensor(prod, lq[:, :, 0, :], lq[:, :, 1, :], ALU.mult))
            dve.tensor_reduce(lam[:, 0:2], prod, AX.X, ALU.add).then_inc(S["lam_sum"], 1)
            dve.wait_ge(S["lam_ready"], 1)
            step(dve.tensor_tensor(lam[:, 2:3], lam[:, 1:2], lam[:, 0:1], ALU.subtract))
            step(dve.tensor_scalar(lam[:, 2:3], lam[:, 2:3], -0.2, None, ALU.add))
            step(dve.tensor_scalar(lam[:, 3:4], par_col("subln_gain_2"), 0.8, None, ALU.mult))
            for k in range(KC):
                accumulate(k, None, False)

            def rms_lo(k):
                dve.scalar_tensor_tensor(x_lo[:, k, :], LN[:, 3 + k % 2, :], par_col("norm_gain_2", k),
                                         x_hi[:, k, :].bitcast(F32), ALU.mult, ALU.subtract).then_inc(x_ready, 1)
                dve.wait_ge(x_ready, KC * X_FILLS.index("rms") + k + 1)

            normalise(0, lambda k: h[:, k, :], rms_lo, center=False, lag=1)
            dve.wait_ge(consts_ready, 2)
            for n_, b in enumerate("abc"):
                B = b.upper()
                for stage in (f"qk_{b}", f"kv_{b}", f"v_{b}", f"g_{b}"):
                    if stage in FIRST_PANEL:
                        for n in range(FIRST_PANEL[stage], len(PLAN)):
                            if PLAN[n][0] == stage:
                                split_to(n + 1)
                if b == "c":
                    bank = wait_aux(dve, ("fc",))
                    z = sm[:, 0:4, 0:8]
                    zabs = sm[:, 12:14, :].rearrange("p a b -> p (a b)").rearrange("p (a b) -> p a b", b=8)
                    free_aux(dve.tensor_tensor(z, bank[:, 0:32].rearrange("p (a b) -> p a b", b=8),
                                               over(row16[:, 0, 0:8], 4), ALU.add), ("fc",))
                    aux_read(dve, "fc")
                    dve.scalar_tensor_tensor(zabs, z, -1.0, z, ALU.mult, ALU.max).then_inc(S["c_abs"], 1)
                    dve.wait_ge(S["c_soft"], 1)
                    dve.scalar_tensor_tensor(z, z, 0.0, zabs, ALU.min, ALU.subtract).then_inc(S["log_ready"], 1)
                    bank = wait_aux(dve, ("cc",))
                    free_aux(dve.tensor_copy(sm[:, 4:8, 0:8], bank[:, 0:32].rearrange("p (a b) -> p a b", b=8)),
                             ("cc",))
                    aux_read(dve, "cc")
                    step(dve.tensor_scalar(R[:, 0:P], R[:, 384:512], NEG / 10, NEG, ALU.is_le, ALU.mult))

                def maxima(u):
                    e = unit_slot(b, u)
                    hd, t = u
                    n = (t + 1) * P
                    if b == "a":
                        for m in range(2):
                            bank = wait_aux(dve, ("A", "S", u, m))
                            free_aux(dve.scalar_tensor_tensor(EX[:, e, m, 0:n], R[:, 512 - n:512], 0.25 ** (hd + 1),
                                                              bank[:, 0:n], ALU.mult, ALU.add), ("A", "S", u, m))
                        aux_read(dve, "A", "S", u, 1)
                        ins = dve.tensor_reduce(mxs[:, e, 0:2], EX[:, e, :, 0:n], AX.X, ALU.max, negate=True)
                    elif b == "b":
                        row = unit_row(b, u)
                        off = P if t == 0 else 0
                        for g in range(2):
                            bank = wait_aux(dve, ("B", "S", u, g))
                            s = slice(g * 256 + off, (g + 1) * 256)
                            free_aux(dve.scalar_tensor_tensor(row[:, s], RB[:, off:256],
                                                              0.5 ** (hd + 4 * g + 1), bank[:, off:256],
                                                              ALU.mult, ALU.add), ("B", "S", u, g))
                        aux_read(dve, "B", "S", u, 1)
                        m = mxs[:, e, 0:2]
                        step(dve.tensor_reduce(m, row.rearrange("p (a b) -> p a b", a=2)[:, :, off:], AX.X, ALU.max))
                        step(dve.tensor_tensor(m, m, row16[:, 1, hd:hd + 5:4], ALU.max))
                        ins = dve.tensor_scalar(m, m, -1.0, None, ALU.mult)
                    else:
                        row = unit_row(b, u)
                        bank = wait_aux(dve, ("C", "S", u, 0))
                        free_aux(dve.scalar_tensor_tensor(row[:, 0:n], EX[:, hd % 2, 1, 0:n],
                                                          sm[:, 4 + t, hd:hd + 1], bank[:, 0:n], ALU.add, ALU.add),
                                 ("C", "S", u, 0))
                        aux_read(dve, "C", "S", u, 0)
                        step(dve.tensor_tensor(row[:, n - P:n], row[:, n - P:n], R[:, 0:P], ALU.add))
                        ins = dve.tensor_reduce(mxs[:, e, 0:1], row[:, 0:n], AX.X, ALU.max, negate=True)
                    ins.then_inc(S["unit_max"], 1)

                def weights(u):
                    e = unit_slot(b, u)
                    n = (u[1] + 1) * P
                    dve.wait_ge(S["unit_exp"], UNIT[(B, u)] - 2 * TT + 1)
                    if b == "a":
                        step(dve.reciprocal(rs[:, e, 2:4], rs[:, e, 0:2]))
                        step(dve.scalar_tensor_tensor(rs[:, e, 1:2], rs[:, e, 0:1], rs[:, e, 3:4], lam[:, 2:3],
                                                      ALU.mult, ALU.mult))
                        dve.scalar_tensor_tensor(EX[:, e, 0, 0:n], EX[:, e, 1, 0:n], rs[:, e, 1:2], EX[:, e, 0, 0:n],
                                                 ALU.mult, ALU.add).then_inc(S["p_ready"], 1)
                    elif b == "b":
                        step(dve.tensor_tensor(rs[:, e, 0:2], rs[:, e, 0:2], rs[:, e, 2:4], ALU.add))
                        step(dve.reciprocal(rs[:, e, 2:4], rs[:, e, 0:2]))
                    else:
                        step(dve.reciprocal(rs[:, e, 2:3], rs[:, e, 0:1]))

                def values(u, last):
                    hd, t = u
                    e = unit_slot(b, u)
                    bank = wait_aux(dve, (B, "PV", u))
                    if b == "a":
                        ins = dve.tensor_scalar(YT[:, t, hd * P:(hd + 1) * P], bank[:, 0:P], rs[:, e, 2:3], None,
                                                ALU.mult)
                    elif b == "b":
                        for g in range(2):
                            s = slice(256 * g + 64 * hd, 256 * g + 64 * hd + 64)
                            ins = dve.scalar_tensor_tensor(YT[:, t, s], bank[:, 64 * g:64 * g + 64],
                                                           rs[:, e, 2 + g:3 + g], BG[:, t, s], ALU.mult, ALU.mult)
                    else:
                        s = slice(64 * hd, 64 * hd + 64)
                        ins = dve.scalar_tensor_tensor(YT[:, t, s], bank[:, 0:64], rs[:, e, 2:3], BG[:, t, s],
                                                       ALU.mult, ALU.mult)
                    free_aux(ins, (B, "PV", u))
                    if last and b != "a":
                        aux_read(dve, B, "PV", u)
                        dve.engine_nop().then_inc(S["y_tm_ready"], 1)

                def key_sums(hd):
                    bank = wait_aux(dve, ("cb_c", hd))
                    free_aux(dve.tensor_scalar(EX[:, hd % 2, 1, :], bank[:, :], -1.0, None, ALU.mult), ("cb_c", hd))
                    aux_read(dve, "cb_c", hd)

                us = [(hd, t) for hd in range(8 if b == "c" else 4) for t in range(TT)]
                per = len(us) // KC
                split_chunks(2 * FIRST_PANEL[f"gm_{b}"] + W_SLOTS)
                if b == "c":
                    key_sums(0)
                for u in us[:AHEAD[b]]:
                    maxima(u)
                for n, u in enumerate(us):
                    if n + AHEAD[b] < len(us):
                        maxima(us[n + AHEAD[b]])
                    weights(u)
                    if n % per == per - 1:
                        split_chunks(2 * FIRST_PANEL[f"gm_{b}"] + W_SLOTS + n // per)
                    values(u, u == us[-1])
                    if b == "c" and u[1] == 1 and u[0] + 1 < 8:
                        key_sums(u[0] + 1)
                split_chunks(2 * FIRST_PANEL[f"gm_{b}"] + W_SLOTS + KC)
                if b == "a":
                    dve.wait_ge(S["ya_rstd"], 1)
                    rows = YT.rearrange("p t (h d) -> p t h d", d=P)
                    for t in range(TT):
                        at["step"] += 1
                        dve.tensor_tensor(rows[:, t], rows[:, t], spread(sm[:, 9, 4 * t:4 * t + 4], P), ALU.mult)\
                           .then_inc(dve_step, 1)
                    dve.wait_ge(dve_step, at["step"])
                    for t in range(TT):
                        ins = dve.tensor_tensor(YT[:, t, :], YT[:, t, :], BG[:, t, :], ALU.mult)
                    ins.then_inc(S["y_tm_ready"], 1)
                for j in range(4):
                    bank = wait_aux(dve, (B + "t", j))
                    free_aux(operand_lo(y_hi[:, j, :], y_lo[:, j, :], bank[:, :], y_hi_done, "yh",
                                        lam[:, 3:4] if b == "a" else None), (B + "t", j))
                for i, f in enumerate(UP_ORDER):
                    n0 = FIRST_PANEL[f"up_{b}"]
                    split_to(n0 + i // 4)
                    dve.wait_ge(S["gate_ready"], KC * (n_ + 1))
                    c = CHUNK0[n0] + i
                    bank = wait_chunk(dve, c)
                    m = MG[:, f, :]
                    if n_ == 0:
                        free_chunk(dve.tensor_tensor(m, bank[:, :], GATE[:, f, :], ALU.mult), c)
                    else:
                        free_chunk(dve.tensor_tensor(GATE[:, f, :], bank[:, :], GATE[:, f, :], ALU.mult), c)
                        chunk_read(dve, c)
                        dve.tensor_tensor(m, m, GATE[:, f, :], ALU.add).then_inc(S["merged_ready"], 1)
            split_to(FIRST_PANEL["w_o"])
            for f in UP_ORDER:
                operand_lo(x_hi[:, f, :], x_lo[:, f, :], MG[:, f, :], x_hi_done, "xh").then_inc(x_ready, 1)
            dve.wait_ge(S["reloaded"], 32)
            residual("w_o", sums=False)
            normalise(1, lambda k: h[:, k, :], lambda k: None, center=False)


def build_program(nc, shapes):
    t = {n: nc.dram_tensor(f"in_{n}_dram", s, F32, kind="ExternalInput").ap() for n, s in shapes}
    out = nc.dram_tensor("out_0_dram", (1, T, D), F32, kind="ExternalOutput").ap()
    w = {}
    for n, a in t.items():
        if n.startswith(("xa_w", "mlp_w")):
            for i in range(2):
                w[f"{n}{i}"] = a[i]
        elif n in ("ln_g", "ln_b", "final_gain_2"):
            w[n] = a
        else:
            w[n] = a[0]
    build(nc, w, out[0])


def kernel(**inputs):
    import numpy as _np
    import concourse.bacc as _bacc
    from concourse.bass_utils import run_bass_kernel_spmd as _run

    nc = _bacc.Bacc("TRN2", target_bir_lowering=False, num_devices=1)
    arrays = {f"in_{n}_dram": _np.ascontiguousarray(a) for n, a in inputs.items()}
    build_program(nc, [(n, a.shape) for n, a in inputs.items()])
    r = _run(nc, [arrays], core_ids=[0])
    return r.results[0]["out_0_dram"]
```
